# Optimizing a Trainium2 kernel written in Bass

```python
import math
import jax, jax.numpy as jnp
from jax import lax
import numpy as np

D_MODEL = 1024
BATCH = 1
SEQ = 256
DEPTH = 2

N_EVEN = (DEPTH + 1) // 2
N_ODD = DEPTH // 2
HEAD_DIM = 64
ATT_HEADS = D_MODEL // (2 * HEAD_DIM)
ATT_WIDTH = ATT_HEADS * HEAD_DIM
ROPE_DIM = HEAD_DIM // 4
ROPE_THETA = 500000.0
DILATED_BRANCHES = ((128, 1), (512, 4), (2048, 16))
ATT_BLOCK = 128
NEG_INF = -1e30
SSM_WIDTH = D_MODEL - ATT_WIDTH
SSM_GROUP = 16
SSM_GROUPS = SSM_WIDTH // SSM_GROUP
SSM_STATE = 64
EVEN_IN = 3 * ATT_WIDTH + SSM_WIDTH
LRU_WIDTH = D_MODEL
LRU_BLOCKS = 4
LRU_BLOCK_DIM = LRU_WIDTH // LRU_BLOCKS
CONV_WIDTH = 4
RG_C = 8.0
FFN_HIDDEN = -(-8 * D_MODEL // (3 * 256)) * 256
NORM_EPS = 1e-6


def rms_norm(x, g):
    x32 = x.astype(jnp.float32)
    y = x32 * lax.rsqrt(jnp.mean(x32 * x32, axis=-1, keepdims=True) + NORM_EPS) * g.astype(jnp.float32)
    return y.astype(x.dtype)

def swiglu(x, w_gate, w_up, w_down):
    return (jax.nn.silu(x @ w_gate) * (x @ w_up)) @ w_down

def _linear_combine(e1, e2):
    a1, b1 = e1
    a2, b2 = e2
    return a1 * a2, a2 * b1 + b2

def partial_rope(t, positions):
    half = ROPE_DIM // 2
    inv_freq = ROPE_THETA ** (-(jnp.arange(half, dtype=jnp.float32) * 2.0 / ROPE_DIM))
    ang = positions.astype(jnp.float32)[..., None] * inv_freq
    cos = jnp.cos(ang)[:, :, None, :]
    sin = jnp.sin(ang)[:, :, None, :]
    t1 = t[..., :half]
    t2 = t[..., half:ROPE_DIM]
    return jnp.concatenate([t1 * cos - t2 * sin, t2 * cos + t1 * sin, t[..., ROPE_DIM:]], axis=-1)

def _dilated_branch(q, k, v, window, dilation):
    b, s, h, c = q.shape
    L = s // dilation
    nb = -(-L // ATT_BLOCK)
    Lp = nb * ATT_BLOCK
    span = window // dilation

    def strided(t):
        t = t.reshape(b, L, dilation, h, c).transpose(0, 2, 1, 3, 4)
        return jnp.pad(t, ((0, 0), (0, 0), (0, Lp - L), (0, 0), (0, 0)))

    def band(t):
        t = jnp.pad(strided(t), ((0, 0), (0, 0), (ATT_BLOCK, 0), (0, 0), (0, 0)))
        t = t.reshape(b, dilation, nb + 1, ATT_BLOCK, h, c)
        return jnp.concatenate([t[:, :, :-1], t[:, :, 1:]], axis=3)

    qb = strided(q).reshape(b, dilation, nb, ATT_BLOCK, h, c)
    kb = band(k)
    vb = band(v)
    scores = jnp.einsum('brnqhc,brnkhc->brnhqk', qb, kb)
    qi = jnp.arange(ATT_BLOCK)[:, None] + ATT_BLOCK
    ki = jnp.arange(2 * ATT_BLOCK)[None, :]
    dist = qi - ki
    kpos = jnp.arange(nb)[:, None, None] * ATT_BLOCK + ki[None] - ATT_BLOCK
    mask = ((dist >= 0) & (dist <= span))[None] & (kpos >= 0)
    scores = jnp.where(mask[None, None, :, None], scores, NEG_INF)
    m = jnp.max(scores, axis=-1)
    p = jnp.exp(scores - m[..., None])
    l = jnp.sum(p, axis=-1)
    acc = jnp.einsum('brnhqk,brnkhc->brnqhc', p, vb)

    def unstride(t):
        t = t.reshape((b, dilation, Lp) + t.shape[4:])[:, :, :L]
        t = jnp.moveaxis(t, 1, 2)
        return t.reshape((b, s) + t.shape[3:])

    m = jnp.moveaxis(m, -1, 3)
    l = jnp.moveaxis(l, -1, 3)
    return unstride(acc), unstride(m), unstride(l)

def dilated_attention(q, k, v):
    outs = [_dilated_branch(q, k, v, w, d) for (w, d) in DILATED_BRANCHES]
    acc_all = jnp.stack([o[0] for o in outs])
    m_all = jnp.stack([o[1] for o in outs])
    l_all = jnp.stack([o[2] for o in outs])
    wts = jnp.exp(m_all - jnp.max(m_all, axis=0, keepdims=True))
    num = jnp.einsum('ibsh,ibshc->bshc', wts, acc_all)
    den = jnp.sum(wts * l_all, axis=0)
    return num / den[..., None]

def s5_mixer(u, a_re, a_im, log_dt, b_re, b_im, c_re, c_im, d_skip, w_glu):
    b, s, _ = u.shape
    u = u.reshape(b, s, SSM_GROUPS, SSM_GROUP)
    f32 = jnp.float32
    A = lax.complex(a_re.astype(f32), a_im.astype(f32))
    dt = jnp.exp(log_dt.astype(f32))[:, None]
    a_bar = jnp.exp(A * dt)
    b_bar = ((a_bar - 1.0) / A)[..., None] * lax.complex(b_re.astype(f32), b_im.astype(f32))
    bu = jnp.einsum('gpc,bsgc->bsgp', b_bar, u.astype(jnp.complex64))
    a_seq = jnp.broadcast_to(a_bar, (s,) + a_bar.shape)
    h = jax.vmap(lambda bu_b: lax.associative_scan(_linear_combine, (a_seq, bu_b), axis=0)[1])(bu)
    c_mat = lax.complex(c_re.astype(f32), c_im.astype(f32))
    y = jnp.einsum('gcp,bsgp->bsgc', c_mat, h).real + d_skip.astype(f32) * u
    y = jax.nn.gelu(y.reshape(b, s, SSM_WIDTH))
    return y * jax.nn.sigmoid(y @ w_glu.astype(f32))

def rglru_mixer(xb, conv_w, conv_b, w_r, b_r, w_i, b_i, lam):
    b, s, r = xb.shape
    f32 = jnp.float32
    xc = lax.conv_general_dilated(xb, conv_w.astype(f32)[:, None, :], window_strides=(1,),
                                  padding=[(CONV_WIDTH - 1, 0)],
                                  dimension_numbers=('NWC', 'WIO', 'NWC'),
                                  feature_group_count=r) + conv_b.astype(f32)
    xh = xc.reshape(b, s, LRU_BLOCKS, LRU_BLOCK_DIM)
    gate_r = jax.nn.sigmoid(jnp.einsum('bshi,hij->bshj', xh, w_r.astype(f32)).reshape(b, s, r) + b_r.astype(f32))
    gate_i = jax.nn.sigmoid(jnp.einsum('bshi,hij->bshj', xh, w_i.astype(f32)).reshape(b, s, r) + b_i.astype(f32))
    log_a = -RG_C * gate_r * jax.nn.softplus(-lam.astype(f32))
    a = jnp.exp(log_a)
    mult = jnp.sqrt(-jnp.expm1(2.0 * log_a))
    _, h = lax.associative_scan(_linear_combine, (a, mult * (gate_i * xc)), axis=1)
    return h

def even_mixer(xn, positions, w_in, w_out, a_re, a_im, log_dt, b_re, b_im, c_re, c_im, d_skip, w_glu):
    b, s, _ = xn.shape
    z = (xn @ w_in).astype(jnp.float32)
    q = z[..., :ATT_WIDTH].reshape(b, s, ATT_HEADS, HEAD_DIM)
    k = z[..., ATT_WIDTH:2 * ATT_WIDTH].reshape(b, s, ATT_HEADS, HEAD_DIM)
    v = z[..., 2 * ATT_WIDTH:3 * ATT_WIDTH].reshape(b, s, ATT_HEADS, HEAD_DIM)
    u = z[..., 3 * ATT_WIDTH:]
    q = partial_rope(q, positions) * (HEAD_DIM ** -0.5)
    k = partial_rope(k, positions)
    att = dilated_attention(q, k, v).reshape(b, s, ATT_WIDTH)
    ssm = s5_mixer(u, a_re, a_im, log_dt, b_re, b_im, c_re, c_im, d_skip, w_glu)
    y = jnp.concatenate([att, ssm], axis=-1).astype(w_out.dtype)
    return (y @ w_out).astype(xn.dtype)

def odd_mixer(xn, w_in, w_out, conv_w, conv_b, w_r, b_r, w_i, b_i, lam):
    z = (xn @ w_in).astype(jnp.float32)
    h = rglru_mixer(z[..., :LRU_WIDTH], conv_w, conv_b, w_r, b_r, w_i, b_i, lam)
    y = (h * jax.nn.gelu(z[..., LRU_WIDTH:])).astype(w_out.dtype)
    return (y @ w_out).astype(xn.dtype)

def first_inputs(seed: int = 0) -> dict:
    key = jax.random.key(seed)
    ks = iter(jax.random.split(key, 32))
    f32 = jnp.float32

    def nrm(shape, scale):
        return jax.random.normal(next(ks), shape, f32) * scale

    G, P, NC, BD = SSM_GROUPS, SSM_STATE, SSM_GROUP, LRU_BLOCK_DIM
    x = nrm((BATCH, SEQ, D_MODEL), 1.0)
    offset = jax.random.randint(next(ks), (BATCH, 1), 0, SEQ, dtype=jnp.int32)
    positions = offset + jnp.arange(SEQ, dtype=jnp.int32)[None, :]
    norm_mix_pre = 1.0 + nrm((DEPTH, D_MODEL), 0.05)
    norm_mix_post = 1.0 + nrm((DEPTH, D_MODEL), 0.05)
    norm_ffn_pre = 1.0 + nrm((DEPTH, D_MODEL), 0.05)
    norm_ffn_post = 1.0 + nrm((DEPTH, D_MODEL), 0.05)
    ev_w_in = nrm((N_EVEN, D_MODEL, EVEN_IN), D_MODEL ** -0.5)
    ev_w_out = nrm((N_EVEN, D_MODEL, D_MODEL), D_MODEL ** -0.5)
    s5_a_re = -0.5 * jnp.exp(nrm((N_EVEN, G, P), 0.02))
    s5_a_im = jnp.pi * jnp.arange(P, dtype=f32) + nrm((N_EVEN, G, P), 0.02)
    s5_log_dt = jax.random.uniform(next(ks), (N_EVEN, G), f32, math.log(1e-3), math.log(1e-1))
    s5_b_re = nrm((N_EVEN, G, P, NC), (2 * NC) ** -0.5)
    s5_b_im = nrm((N_EVEN, G, P, NC), (2 * NC) ** -0.5)
    s5_c_re = nrm((N_EVEN, G, NC, P), (2 * P) ** -0.5)
    s5_c_im = nrm((N_EVEN, G, NC, P), (2 * P) ** -0.5)
    s5_d = nrm((N_EVEN, G, NC), 1.0)
    s5_w_glu = nrm((N_EVEN, SSM_WIDTH, SSM_WIDTH), SSM_WIDTH ** -0.5)
    od_w_in = nrm((N_ODD, D_MODEL, 2 * LRU_WIDTH), D_MODEL ** -0.5)
    od_w_out = nrm((N_ODD, LRU_WIDTH, D_MODEL), LRU_WIDTH ** -0.5)
    rg_conv_w = nrm((N_ODD, CONV_WIDTH, LRU_WIDTH), CONV_WIDTH ** -0.5)
    rg_conv_b = nrm((N_ODD, LRU_WIDTH), 0.01)
    rg_w_r = nrm((N_ODD, LRU_BLOCKS, BD, BD), BD ** -0.5)
    rg_b_r = nrm((N_ODD, LRU_WIDTH), 0.01)
    rg_w_i = nrm((N_ODD, LRU_BLOCKS, BD, BD), BD ** -0.5)
    rg_b_i = nrm((N_ODD, LRU_WIDTH), 0.01)
    a0 = jax.random.uniform(next(ks), (N_ODD, LRU_WIDTH), f32, 0.9, 0.999)
    sig = a0 ** (1.0 / RG_C)
    rg_lam = jnp.log(sig) - jnp.log1p(-sig)
    ffn_w_gate = nrm((DEPTH, D_MODEL, FFN_HIDDEN), D_MODEL ** -0.5)
    ffn_w_up = nrm((DEPTH, D_MODEL, FFN_HIDDEN), D_MODEL ** -0.5)
    ffn_w_down = nrm((DEPTH, FFN_HIDDEN, D_MODEL), FFN_HIDDEN ** -0.5)
    return {'x': x, 'positions': positions,
            'norm_mix_pre': norm_mix_pre, 'norm_mix_post': norm_mix_post,
            'norm_ffn_pre': norm_ffn_pre, 'norm_ffn_post': norm_ffn_post,
            'ev_w_in': ev_w_in, 'ev_w_out': ev_w_out,
            's5_a_re': s5_a_re, 's5_a_im': s5_a_im, 's5_log_dt': s5_log_dt,
            's5_b_re': s5_b_re, 's5_b_im': s5_b_im, 's5_c_re': s5_c_re, 's5_c_im': s5_c_im,
            's5_d': s5_d, 's5_w_glu': s5_w_glu,
            'od_w_in': od_w_in, 'od_w_out': od_w_out,
            'rg_conv_w': rg_conv_w, 'rg_conv_b': rg_conv_b,
            'rg_w_r': rg_w_r, 'rg_b_r': rg_b_r, 'rg_w_i': rg_w_i, 'rg_b_i': rg_b_i, 'rg_lam': rg_lam,
            'ffn_w_gate': ffn_w_gate, 'ffn_w_up': ffn_w_up, 'ffn_w_down': ffn_w_down}

def first_block(x, positions, norm_mix_pre, norm_mix_post, norm_ffn_pre, norm_ffn_post,
              ev_w_in, ev_w_out, s5_a_re, s5_a_im, s5_log_dt, s5_b_re, s5_b_im, s5_c_re, s5_c_im,
              s5_d, s5_w_glu, od_w_in, od_w_out, rg_conv_w, rg_conv_b, rg_w_r, rg_b_r, rg_w_i, rg_b_i,
              rg_lam, ffn_w_gate, ffn_w_up, ffn_w_down):
    for layer in range(DEPTH):
        hn = rms_norm(x, norm_mix_pre[layer])
        if layer % 2 == 0:
            e = layer // 2
            mix = even_mixer(hn, positions, ev_w_in[e], ev_w_out[e], s5_a_re[e], s5_a_im[e],
                             s5_log_dt[e], s5_b_re[e], s5_b_im[e], s5_c_re[e], s5_c_im[e],
                             s5_d[e], s5_w_glu[e])
        else:
            o = layer // 2
            mix = odd_mixer(hn, od_w_in[o], od_w_out[o], rg_conv_w[o], rg_conv_b[o],
                            rg_w_r[o], rg_b_r[o], rg_w_i[o], rg_b_i[o], rg_lam[o])
        x = x + rms_norm(mix, norm_mix_post[layer])
        hn = rms_norm(x, norm_ffn_pre[layer])
        ff = swiglu(hn, ffn_w_gate[layer], ffn_w_up[layer], ffn_w_down[layer])
        x = x + rms_norm(ff, norm_ffn_post[layer])
    return x


GRID_W = 64
ROPE_THETA_2 = 10000.0
Q_BLOCK = 128
EPS = 1e-6
N_MIXERS = 2

N_MEM = 256
MEM_HEADS = 4
MEM_HEAD_DIM = 128
MEM_W = MEM_HEADS * MEM_HEAD_DIM

MLA_HEADS = 8
MLA_Q_RANK = 384
MLA_KV_RANK = 256
MLA_NOPE = 128
MLA_ROPE = 64
MLA_V = 128
MLA_IN_W = MLA_Q_RANK + MLA_KV_RANK + MLA_ROPE

GQA_HEADS = 8
GQA_KV_HEADS = 2
GQA_HEAD_DIM = 128
GQA_Q_W = GQA_HEADS * GQA_HEAD_DIM
GQA_KV_W = GQA_KV_HEADS * GQA_HEAD_DIM
GQA_IN_W = GQA_Q_W + 2 * GQA_KV_W

MIX_W = MLA_HEADS * MLA_V + MEM_W

D_FF = -(-8 * D_MODEL // (3 * 256)) * 256


def _rmsnorm(x, g):
    x32 = x.astype(jnp.float32)
    y = x32 * lax.rsqrt(jnp.mean(x32 * x32, axis=-1, keepdims=True) + EPS)
    return (y * g.astype(jnp.float32)).astype(x.dtype)

def _axial_rope_tables(seq, dim, dtype):
    rows = seq // GRID_W
    row = jnp.repeat(jnp.arange(rows, dtype=jnp.float32), GRID_W)
    col = jnp.tile(jnp.arange(GRID_W, dtype=jnp.float32), rows)
    axis_dim = dim // 2
    inv = ROPE_THETA_2 ** (-jnp.arange(0, axis_dim, 2, dtype=jnp.float32) / axis_dim)
    ang_r = row[:, None] * inv
    ang_c = col[:, None] * inv
    tabs = (jnp.cos(ang_r), jnp.sin(ang_r), jnp.cos(ang_c), jnp.sin(ang_c))
    return tuple(t[:, None, :].astype(dtype) for t in tabs)

def _rope_1d(x, cos, sin):
    x1, x2 = jnp.split(x, 2, axis=-1)
    return jnp.concatenate([x1 * cos - x2 * sin, x2 * cos + x1 * sin], axis=-1)

def _apply_axial_rope(x, tabs):
    cos_r, sin_r, cos_c, sin_c = tabs
    xr, xc = jnp.split(x, 2, axis=-1)
    return jnp.concatenate([_rope_1d(xr, cos_r, sin_r), _rope_1d(xc, cos_c, sin_c)], axis=-1)

def _blocked_attention(q_parts, k_parts, v, scale):
    B, S, Hk, Dv = v.shape
    H = q_parts[0].shape[2]
    G = H // Hk
    nb = S // Q_BLOCK
    qb = tuple(q.reshape(B, nb, Q_BLOCK, Hk, G, q.shape[-1]).transpose(1, 0, 2, 3, 4, 5)
               for q in q_parts)

    def one_block(qs):
        s = None
        for qp, kp in zip(qs, k_parts):
            eq = 'bqkgd,bskd->bkgqs' if kp.ndim == 4 else 'bqkgd,bsd->bkgqs'
            t = jnp.einsum(eq, qp, kp, preferred_element_type=jnp.float32)
            s = t if s is None else s + t
        p = jax.nn.softmax(s * scale, axis=-1).astype(v.dtype)
        return jnp.einsum('bkgqs,bskd->bqkgd', p, v)

    out = lax.map(one_block, qb)
    return out.transpose(1, 0, 2, 3, 4, 5).reshape(B, S, H, Dv)

def _mla_mixer(p, q_a_norm, w_q_b, kv_a_norm, w_kv_b, q_norm, k_norm, rope):
    B, S, _ = p.shape
    c_q = p[..., :MLA_Q_RANK]
    c_kv = p[..., MLA_Q_RANK:MLA_Q_RANK + MLA_KV_RANK]
    k_pe = p[..., MLA_Q_RANK + MLA_KV_RANK:]
    q = (_rmsnorm(c_q, q_a_norm) @ w_q_b).reshape(B, S, MLA_HEADS, MLA_NOPE + MLA_ROPE)
    kv = (_rmsnorm(c_kv, kv_a_norm) @ w_kv_b).reshape(B, S, MLA_HEADS, MLA_NOPE + MLA_V)
    q_nope = _rmsnorm(q[..., :MLA_NOPE], q_norm[:MLA_NOPE])
    q_pe = _apply_axial_rope(_rmsnorm(q[..., MLA_NOPE:], q_norm[MLA_NOPE:]), rope)
    k_nope = _rmsnorm(kv[..., :MLA_NOPE], k_norm[:MLA_NOPE])
    v = kv[..., MLA_NOPE:]
    k_pe = _apply_axial_rope(_rmsnorm(k_pe, k_norm[MLA_NOPE:])[:, :, None, :], rope)[:, :, 0, :]
    out = _blocked_attention([q_nope, q_pe], [k_nope, k_pe], v,
                             (MLA_NOPE + MLA_ROPE) ** -0.5)
    return out.reshape(B, S, MLA_HEADS * MLA_V)

def _gqa_mixer(p, q_norm, k_norm, rope):
    B, S, _ = p.shape
    q = p[..., :GQA_Q_W].reshape(B, S, GQA_HEADS, GQA_HEAD_DIM)
    k = p[..., GQA_Q_W:GQA_Q_W + GQA_KV_W].reshape(B, S, GQA_KV_HEADS, GQA_HEAD_DIM)
    v = p[..., GQA_Q_W + GQA_KV_W:].reshape(B, S, GQA_KV_HEADS, GQA_HEAD_DIM)
    q = _apply_axial_rope(_rmsnorm(q, q_norm), rope)
    k = _apply_axial_rope(_rmsnorm(k, k_norm), rope)
    out = _blocked_attention([q], [k], v, GQA_HEAD_DIM ** -0.5)
    return out.reshape(B, S, GQA_Q_W)

def _memory_attention(q, mem_n, w_kv, q_norm, k_norm):
    B, S, _ = q.shape
    M = mem_n.shape[1]
    q = _rmsnorm(q.reshape(B, S, MEM_HEADS, MEM_HEAD_DIM), q_norm)
    kv = (mem_n @ w_kv).reshape(B, M, 2, MEM_HEADS, MEM_HEAD_DIM)
    k = _rmsnorm(kv[:, :, 0], k_norm)
    v = kv[:, :, 1]
    s = jnp.einsum('bqhd,bmhd->bhqm', q, k, preferred_element_type=jnp.float32)
    p = jax.nn.softmax(s * (MEM_HEAD_DIM ** -0.5), axis=-1).astype(v.dtype)
    return jnp.einsum('bhqm,bmhd->bqhd', p, v).reshape(B, S, MEM_W)

def _swiglu(h, w_gate_up, w_down):
    gu = h @ w_gate_up
    g, u = gu[..., :D_FF], gu[..., D_FF:]
    return (jax.nn.silu(g) * u) @ w_down

def second_inputs(seed: int = 0) -> dict:
    key = jax.random.key(seed)
    ks = iter(jax.random.split(key, 32))
    n_mla = (DEPTH + 1) // 2
    n_gqa = DEPTH // 2

    def w(shape, fan_in):
        return jax.random.normal(next(ks), shape, jnp.float32) * (fan_in ** -0.5)

    def gain(shape):
        return 1.0 + 0.05 * jax.random.normal(next(ks), shape, jnp.float32)

    return {
        "x": jax.random.normal(next(ks), (BATCH, SEQ, D_MODEL), jnp.float32),
        "mem": jax.random.normal(next(ks), (BATCH, N_MEM, D_MODEL), jnp.float32),
        "mem_norm": gain((D_MODEL,)),
        "norm_mix": gain((DEPTH, D_MODEL)),
        "norm_ffn": gain((DEPTH, D_MODEL)),
        "w_out": w((DEPTH, MIX_W, D_MODEL), MIX_W),
        "w_mem_kv": w((DEPTH, D_MODEL, 2 * MEM_W), D_MODEL),
        "memq_norm": gain((DEPTH, MEM_HEAD_DIM)),
        "memk_norm": gain((DEPTH, MEM_HEAD_DIM)),
        "w_gate_up": w((DEPTH, D_MODEL, 2 * D_FF), D_MODEL),
        "w_down": w((DEPTH, D_FF, D_MODEL), D_FF),
        "mla_w_in": w((n_mla, D_MODEL, MLA_IN_W + MEM_W), D_MODEL),
        "mla_q_a_norm": gain((n_mla, MLA_Q_RANK)),
        "mla_w_q_b": w((n_mla, MLA_Q_RANK, MLA_HEADS * (MLA_NOPE + MLA_ROPE)), MLA_Q_RANK),
        "mla_kv_a_norm": gain((n_mla, MLA_KV_RANK)),
        "mla_w_kv_b": w((n_mla, MLA_KV_RANK, MLA_HEADS * (MLA_NOPE + MLA_V)), MLA_KV_RANK),
        "mla_q_norm": gain((n_mla, MLA_NOPE + MLA_ROPE)),
        "mla_k_norm": gain((n_mla, MLA_NOPE + MLA_ROPE)),
        "gqa_w_in": w((n_gqa, D_MODEL, GQA_IN_W + MEM_W), D_MODEL),
        "gqa_q_norm": gain((n_gqa, GQA_HEAD_DIM)),
        "gqa_k_norm": gain((n_gqa, GQA_HEAD_DIM)),
    }

def second_block(x, mem, mem_norm, norm_mix, norm_ffn, w_out, w_mem_kv, memq_norm, memk_norm,
              w_gate_up, w_down, mla_w_in, mla_q_a_norm, mla_w_q_b, mla_kv_a_norm, mla_w_kv_b,
              mla_q_norm, mla_k_norm, gqa_w_in, gqa_q_norm, gqa_k_norm):
    S = x.shape[1]
    rope_mla = _axial_rope_tables(S, MLA_ROPE, x.dtype)
    rope_gqa = _axial_rope_tables(S, GQA_HEAD_DIM, x.dtype)
    mem_n = _rmsnorm(mem, mem_norm)
    for i in range(DEPTH):
        j = i // N_MIXERS
        h = _rmsnorm(x, norm_mix[i])
        if i % N_MIXERS == 0:
            proj = h @ mla_w_in[j]
            mix = _mla_mixer(proj[..., :MLA_IN_W], mla_q_a_norm[j], mla_w_q_b[j],
                             mla_kv_a_norm[j], mla_w_kv_b[j], mla_q_norm[j], mla_k_norm[j],
                             rope_mla)
            q_mem = proj[..., MLA_IN_W:]
        else:
            proj = h @ gqa_w_in[j]
            mix = _gqa_mixer(proj[..., :GQA_IN_W], gqa_q_norm[j], gqa_k_norm[j], rope_gqa)
            q_mem = proj[..., GQA_IN_W:]
        mem_out = _memory_attention(q_mem, mem_n, w_mem_kv[i], memq_norm[i], memk_norm[i])
        x = x + jnp.concatenate([mix, mem_out], axis=-1) @ w_out[i]
        x = x + _swiglu(_rmsnorm(x, norm_ffn[i]), w_gate_up[i], w_down[i])
    return x


def setup_inputs(seed=0):
    out = dict(first_inputs(seed))
    for name, value in second_inputs(seed + 1).items():
        if name != "x":
            out[name + "_2"] = value
    return out


def reference(
    x, positions, norm_mix_pre, norm_mix_post, norm_ffn_pre, norm_ffn_post, ev_w_in, ev_w_out,
    s5_a_re, s5_a_im, s5_log_dt, s5_b_re, s5_b_im, s5_c_re, s5_c_im, s5_d, s5_w_glu, od_w_in,
    od_w_out, rg_conv_w, rg_conv_b, rg_w_r, rg_b_r, rg_w_i, rg_b_i, rg_lam, ffn_w_gate,
    ffn_w_up, ffn_w_down, mem_2, mem_norm_2, norm_mix_2, norm_ffn_2, w_out_2, w_mem_kv_2,
    memq_norm_2, memk_norm_2, w_gate_up_2, w_down_2, mla_w_in_2, mla_q_a_norm_2, mla_w_q_b_2,
    mla_kv_a_norm_2, mla_w_kv_b_2, mla_q_norm_2, mla_k_norm_2, gqa_w_in_2, gqa_q_norm_2,
    gqa_k_norm_2,
):
    x = first_block(
        x, positions, norm_mix_pre, norm_mix_post, norm_ffn_pre, norm_ffn_post, ev_w_in,
        ev_w_out, s5_a_re, s5_a_im, s5_log_dt, s5_b_re, s5_b_im, s5_c_re, s5_c_im, s5_d,
        s5_w_glu, od_w_in, od_w_out, rg_conv_w, rg_conv_b, rg_w_r, rg_b_r, rg_w_i, rg_b_i,
        rg_lam, ffn_w_gate, ffn_w_up, ffn_w_down,
    )
    return second_block(
        x, mem_2, mem_norm_2, norm_mix_2, norm_ffn_2, w_out_2, w_mem_kv_2, memq_norm_2,
        memk_norm_2, w_gate_up_2, w_down_2, mla_w_in_2, mla_q_a_norm_2, mla_w_q_b_2,
        mla_kv_a_norm_2, mla_w_kv_b_2, mla_q_norm_2, mla_k_norm_2, gqa_w_in_2, gqa_q_norm_2,
        gqa_k_norm_2,
    )


_drawn_inputs = setup_inputs


def setup_inputs(seed=0):
    import zlib

    import numpy as np

    out = dict(_drawn_inputs(seed))
    spreads = {}
    factors = {'s5_a_re': 8.0,
     'rg_conv_b': 2.902,
     'rg_b_r': 8.0,
     'rg_b_i': 8.0,
     'mem_norm_2': 8.0,
     'norm_mix_2': 6.133,
     'memq_norm_2': 8.0,
     'memk_norm_2': 8.0,
     'mla_q_a_norm_2': 8.0,
     'mla_kv_a_norm_2': 8.0,
     'mla_q_norm_2': 8.0,
     'mla_k_norm_2': 8.0,
     'gqa_q_norm_2': 8.0,
     'gqa_k_norm_2': 8.0}
    for name, (base, spread) in spreads.items():
        noise = np.random.default_rng([zlib.crc32(name.encode()), seed]).standard_normal(out[name].shape)
        drawn = base * np.exp(spread * noise) if base else spread * noise
        out[name] = __import__('jax').numpy.asarray(drawn.astype(out[name].dtype))
    for name, factor in factors.items():
        out[name] = (out[name] * factor).astype(out[name].dtype)
    return out
```

```python
import numpy as np
import concourse.bass as bass
from concourse import mybir
from contextlib import ExitStack

F = 2816
CH = 2048
NR = 3
NW = 3



def cut(name, lead, k0, nk, cols):
    return ("mat", name, lead, k0, nk, tuple(cols))


def wide(name, lead, nkt):
    return [[cut(name, lead, k, 2, [(0, 1024)])] for k in range(0, nkt, 2)]


def nat(name, lead, cols, nkt=8, per=4):
    return [[cut(name, lead, k, per, cols)] for k in range(0, nkt, per)]


def ffn_chunks(gate, up, uo, down, lead):
    out = []
    for g in range(11):
        for k in (0, 4):
            out.append([("pair", gate, up, lead, k, 4, 256 * g, uo + 256 * g)])
    return out + wide(down, lead, 22)


def plan():
    p = {}
    order = []

    def add(key, chunks):
        p[key] = list(range(len(order), len(order) + len(chunks)))
        order.extend(chunks)

    for key, c in (("u", 1536), ("q", 0), ("k", 512), ("v", 1024)):
        add("ev_" + key, nat("ev_w_in", 0, [(c, 512)]))
    add("glu", nat("s5_w_glu", 0, [(0, 512)], 4))
    add("ev_out", wide("ev_w_out", 0, 8))
    add("ffn0", ffn_chunks("ffn_w_gate", "ffn_w_up", 0, "ffn_w_down", 0))
    for g in range(4):
        add(f"od{g}", nat("od_w_in", 0, [(512 * g, 512)]))
    add("rg", [[("rg", h) for h in (b, b + 1)] for b in (0, 2)])
    for i in range(2):
        add(f"mem0{i}", nat("w_mem_kv_2", 0, [(512 * i, 512)]))
    add("od_out", wide("od_w_out", 0, 8))
    add("ffn1", ffn_chunks("ffn_w_gate", "ffn_w_up", 0, "ffn_w_down", 1))
    add("mla_a", nat("mla_w_in_2", 0, [(0, 384), (640, 64)]))
    add("mla_b", nat("mla_w_in_2", 0, [(384, 256)], 8, 8))
    add("mla_c", nat("mla_w_in_2", 0, [(704, 512)]))
    for g in range(2):
        add(f"qb{g}", nat("mla_w_q_b_2", 0, [(192 * h, 128) for h in range(4 * g, 4 * g + 4)], 3, 3))
    add("qb2", nat("mla_w_q_b_2", 0, [(192 * h + 128, 64) for h in range(8)], 3, 3))
    for j in range(2):
        add(f"kvb{j}", [[cut("mla_w_kv_b_2", 0, 0, 2, [(256 * h + 128 * j, 128) for h in range(4 * g, 4 * g + 4)])
                         for g in range(2)]])
    for i in range(2):
        add(f"mem1{i}", nat("w_mem_kv_2", 1, [(512 * i, 512)]))
    add("out0", wide("w_out_2", 0, 12))
    add("ffn2", ffn_chunks("w_gate_up_2", "w_gate_up_2", F, "w_down_2", 0))
    for g in range(4):
        add(f"gqa{g}", nat("gqa_w_in_2", 0, [(512 * g, 512)]))
    add("out1", wide("w_out_2", 1, 12))
    add("ffn3", ffn_chunks("w_gate_up_2", "w_gate_up_2", F, "w_down_2", 1))
    return p, order


def kmat(a, k0, nk, c0, nc_):
    return a[128 * k0:128 * (k0 + nk), c0:c0 + nc_].reshape(nk, 128, nc_).transpose(1, 0, 2)


def pack(inputs, order):
    out = np.zeros((len(order), 128, CH), np.float32)
    for n, pieces in enumerate(order):
        at = 0
        for pc in pieces:
            if pc[0] == "mat":
                _, name, lead, k0, nk, cols = pc
                a = inputs[name][lead]
                w = np.concatenate([kmat(a, k0, nk, c, m) for c, m in cols], axis=2)
            elif pc[0] == "pair":
                _, gate, up, lead, k0, nk, cg, cu = pc
                w = np.concatenate([kmat(inputs[gate][lead], k0, nk, cg, 256),
                                    kmat(inputs[up][lead], k0, nk, cu, 256)], axis=2)
            else:
                w = np.concatenate([kmat(inputs[nm][0][pc[1]], 0, 2, 0, 256) for nm in ("rg_w_r", "rg_w_i")], axis=1)
            w = w.reshape(128, -1)
            out[n, :, at:at + w.shape[1]] = w
            at += w.shape[1]
    return out


COLS = [("norm_mix_pre", 16), ("norm_ffn_pre", 16), ("norm_mix_2", 16), ("norm_ffn_2", 16), ("mem_norm_2", 8),
        ("memq_norm_2", 2), ("memk_norm_2", 2), ("mla_q_a_norm_2", 3), ("mla_kv_a_norm_2", 2),
        ("mla_qn", 1), ("mla_kn", 1), ("rg_conv_w", 32), ("rg_conv_b", 8), ("rg_b_r", 8), ("rg_b_i", 8),
        ("rg_lam", 8), ("s5_d", 4), ("s5_a_re", 16), ("s5_a_im", 16), ("s5_log_dt", 16)]
COL = {}
_n = 0
for _name, _w in COLS:
    COL[_name] = _n
    _n += _w
NCOL = _n


def columns(inputs):
    parts = []
    for name, w in COLS:
        if name in ("mla_qn", "mla_kn"):
            a = inputs["mla_q_norm_2" if name == "mla_qn" else "mla_k_norm_2"][0, :128]
            parts.append(a.reshape(1, 128).T)
        elif name in ("s5_a_re", "s5_a_im"):
            parts.append(inputs[name][0].reshape(16, 128).T)
        elif name == "s5_log_dt":
            parts.append(np.repeat(inputs[name][0].reshape(16, 2), 64, axis=1).T)
        else:
            parts.append(np.ascontiguousarray(inputs[name]).reshape(w, 128).T)
    return np.ascontiguousarray(np.concatenate(parts, axis=1))


def s5_layout(inputs):
    out = []
    for name in ("s5_b_re", "s5_b_im"):
        b = inputs[name][0].reshape(4, 4, 2, 64, 16)
        w = np.zeros((4, 4, 2, 16, 2, 64), np.float32)
        for g in range(2):
            w[:, :, g, :, g, :] = b[:, :, g].transpose(0, 1, 3, 2)
        out.append(w.transpose(1, 2, 3, 0, 4, 5).reshape(128, 512))
    for name in ("s5_c_re", "s5_c_im"):
        c = inputs[name][0].reshape(16, 2, 16, 64)
        out.append(c.transpose(1, 3, 0, 2).reshape(128, 256))
    return np.ascontiguousarray(np.concatenate(out, axis=1))


def rope_tables(dim):
    row = np.repeat(np.arange(4, dtype=np.float32), 64)
    col = np.tile(np.arange(64, dtype=np.float32), 4)
    ax = dim // 2
    inv = (np.float32(10000.0) ** (-np.arange(0, ax, 2, dtype=np.float32) / np.float32(ax))).astype(np.float32)
    cs, sn = [], []
    for pos in (row, col):
        ang = (pos[:, None] * inv).astype(np.float32)
        cs += [np.cos(ang), np.cos(ang)]
        sn += [-np.sin(ang), np.sin(ang)]
    return [np.concatenate(t, axis=1).astype(np.float32).reshape(2, 128, dim).transpose(1, 0, 2).reshape(128, 2 * dim)
            for t in (cs, sn)]


def tables():
    q = np.arange(256)[:, None]
    k = np.arange(256)[None, :]
    d = q - k
    c = ((d >= 0) & (d <= 128)).astype(np.float32) + ((d >= 0) & (d % 4 == 0)) + ((d >= 0) & (d % 16 == 0))
    bias = np.where(c > 0, 0.0, -1e30)
    two = lambda a: a.reshape(2, 128, 256).transpose(1, 0, 2).reshape(128, 512)
    inv = (np.float32(500000.0) ** (-(np.arange(8, dtype=np.float32) * np.float32(2.0) / np.float32(16)))).astype(np.float32)
    ident = np.eye(128, dtype=np.float32)
    t0 = [ident, two(c), two(bias), np.tile(np.arange(256, dtype=np.float32), (128, 1)), np.tile(inv, (128, 1))]
    a = np.ascontiguousarray(np.concatenate([x.astype(np.float32) for x in t0], axis=1))
    b = np.ascontiguousarray(np.concatenate(rope_tables(64) + rope_tables(128), axis=1))
    return a, b


class Tok:

    def __init__(self, sem, inc):
        self.sem, self.inc, self.value, self.used = sem, inc, None, False


class Later:

    def matmul(self, *a, **k):
        return lambda e: e.matmul(*a, **k)

    def transpose(self, *a, **k):
        return lambda e: e.transpose(*a, **k)

    def activation(self, *a, **k):
        return lambda e: e.activation(*a, **k)

    def tensor_tensor(self, *a, **k):
        return lambda e: e.tensor_tensor(*a, **k)

    def tensor_scalar(self, *a, **k):
        return lambda e: e.tensor_scalar(*a, **k)

    def scalar_tensor_tensor(self, *a, **k):
        return lambda e: e.scalar_tensor_tensor(*a, **k)

    def tensor_copy(self, *a, **k):
        return lambda e: e.tensor_copy(*a, **k)

    def tensor_reduce(self, *a, **k):
        return lambda e: e.tensor_reduce(*a, **k)

    def tensor_tensor_scan(self, *a, **k):
        return lambda e: e.tensor_tensor_scan(*a, **k)

    def tensor_tensor_reduce(self, *a, **k):
        return lambda e: e.tensor_tensor_reduce(*a, **k)

    def tensor_single_scalar(self, *a, **k):
        return lambda e: e.tensor_single_scalar(*a, **k)

    def reciprocal(self, *a, **k):
        return lambda e: e.reciprocal(*a, **k)

    def memset(self, *a, **k):
        return lambda e: e.memset(*a, **k)

    def dma_start(self, *a, **k):
        return lambda e: e.dma_start(*a, **k)


LATER = Later()


def flat(deps):
    out = []
    for d in deps:
        out += flat(d) if isinstance(d, (list, tuple)) else [] if d is None else [d]
    return out


class Queues:

    def __init__(self):
        self.q = {}

    def op(self, eng, fn, *deps):
        t = Tok(eng, 1)
        self.put(eng, fn, t, deps)
        return t

    def dma(self, eng, out, in_, sem, *deps):
        t = Tok(sem, 16)
        t.used = True
        self.put(eng, lambda e: e.dma_start(out, in_), t, deps)
        return t

    def put(self, eng, fn, t, deps):
        deps = flat(deps)
        for d in deps:
            d.used = True
        self.q.setdefault(eng, []).append((fn(LATER), t, deps))

    def count(self):
        total = {}
        for eng in self.q:
            for _, t, _ in self.q[eng]:
                if t.used:
                    total[t.sem] = total.get(t.sem, 0) + t.inc
                    t.value = total[t.sem]

    def emit(self, eng, e, sems):
        seen = {}
        for fn, t, deps in self.q.get(eng, []):
            need = {}
            for d in deps:
                need[d.sem] = max(need.get(d.sem, 0), d.value)
            for s in sorted(need, key=str):
                if seen.get(s, 0) < need[s]:
                    e.wait_ge(sems[s], need[s])
                    seen[s] = need[s]
            ins = fn(e)
            if t.used:
                ins.then_inc(sems[t.sem], t.inc)


def program(nc, A, PLAN, NCH):
    f32, f32r, i32 = mybir.dt.float32, mybir.dt.float32r, mybir.dt.int32
    ALU, ACT, AX = mybir.AluOpType, mybir.ActivationFunctionType, mybir.AxisListType
    MUL, ADD, SUB = ALU.mult, ALU.add, ALU.subtract
    Q = Queues()
    PE = lambda fn, *d: Q.op("pe", fn, *d)
    V = lambda fn, *d: Q.op("dve", fn, *d)
    S = lambda fn, *d: Q.op("act", fn, *d)
    G = lambda fn, *d: Q.op("pool", fn, *d)
    TWO_PI = 6.283185307179586

    top = ExitStack()
    with top:
        scope = [top]

        def sb(name, shape, dt=f32):
            return scope[-1].enter_context(nc.sbuf_tensor(name, shape, dt))

        def sem(name):
            return top.enter_context(nc.semaphore(name))

        sems = {k: sem("s_" + k) for k in ("pe", "dve", "act", "pool")}
        for r in range(NR):
            sems[f"w{r}"] = sem(f"s_w{r}")

        def load(eng, out, in_, name, *deps):
            if name not in sems:
                sems[name] = sem("s_" + name)
            return Q.dma(eng, out, in_, name, *deps)

        X = sb("X", [128, 2, 1024])
        HTh, HTl = sb("HTh", [128, 8, 256], f32r), sb("HTl", [128, 8, 256], f32r)
        YAh, YAl = sb("YAh", [128, 12, 256], f32r), sb("YAl", [128, 12, 256], f32r)
        RAW = sb("RAW", [128, NR, CH])
        WH, WL = sb("WH", [128, NW, CH], f32r), sb("WL", [128, NW, CH], f32r)
        BC = sb("BC", [128, 1024])
        ident = sb("ident", [128, 128])
        cst = sb("cst", [128, NCOL])
        st = sb("st", [128, 64])
        mh = sb("mh", [128, 16])
        YG = sb("YG", [128, 2, 1024])
        PS = top.enter_context(nc.psum_tensor("PS", [128, 8, 512], f32))
        bank = [[] for _ in range(8)]

        def col(name, i=0, n=1):
            return cst[:, COL[name] + i:COL[name] + i + n]

        split_tok, used_tok, raw_free, dma_tok = {}, {}, {}, {}
        nxt = {"dma": 0, "split": 0}

        def stream_load():
            c = nxt["dma"]
            if c >= NCH:
                return
            nxt["dma"] = c + 1
            dma_tok[c] = Q.dma("sp", RAW[:, c % NR, :], A["w"][c], f"w{c % NR}", raw_free.get(c - NR))

        def stream_split():
            c = nxt["split"]
            nxt["split"] = c + 1
            s, r = c % NW, c % NR
            hi = S(lambda e: e.activation(WH[:, s, :], RAW[:, r, :], ACT.Copy), dma_tok[c], used_tok.get(c - NW))
            lo = V(lambda e: e.tensor_tensor(WL[:, s, :], RAW[:, r, :], WH[:, s, :].bitcast(f32), SUB),
                   hi, dma_tok[c], used_tok.get(c - NW))
            split_tok[c] = lo
            raw_free[c] = [hi, lo]
            stream_load()

        def pump():
            while nxt["split"] < NCH and (nxt["split"] < NW or (nxt["split"] - NW) in used_tok):
                stream_split()

        def chunk(c):
            while nxt["split"] <= c:
                stream_split()
            return c % NW

        def mm(out, a, b, start, stop, *deps):
            return PE(lambda e: e.matmul(out, a, b, start=start, stop=stop), *deps)

        def mm3(out, ah, al, bh, bl, start, stop, *deps):
            mm(out, ah, bh, start, False, *deps)
            mm(out, ah, bl, False, False)
            return mm(out, al, bh, False, stop)

        def nat_mm(cs, per, nkt, N, src, srcdeps, banks, off=0, keep=False):
            hi, lo = src
            k = 0
            for ci, c in enumerate(cs):
                s = chunk(c)
                for kk in range(per):
                    if k == nkt:
                        break
                    for t in range(2):
                        w = slice(off + kk * N, off + (kk + 1) * N)
                        tk = mm3(PS[:, banks[t], 0:N], hi[:, k, 128 * t:128 * t + 128], lo[:, k, 128 * t:128 * t + 128],
                                 WH[:, s, w], WL[:, s, w], k == 0, k == nkt - 1,
                                 split_tok[c], srcdeps[k], bank[banks[t]] if k == 0 else None)
                    k += 1
                if not keep:
                    used_tok[c] = tk
                    pump()
            return tk

        def wide_mm(cs, src_of, dep_of):
            ends = [None, None]
            n = len(cs)
            for ci, c in enumerate(cs):
                s = chunk(c)
                for t in range(2):
                    for kk in range(2):
                        k = 2 * ci + kk
                        hi, lo, j = src_of(k)
                        for half in range(2):
                            w = slice(kk * 1024 + half * 512, kk * 1024 + half * 512 + 512)
                            ends[t] = mm3(PS[:, 2 * t + half, :], hi[:, j, 128 * t:128 * t + 128],
                                          lo[:, j, 128 * t:128 * t + 128], WH[:, s, w], WL[:, s, w],
                                          k == 0, k == 2 * n - 1, split_tok[c], dep_of(k),
                                          bank[2 * t + half] if k == 0 else None)
                used_tok[c] = ends[1]
                if ci < n - 1:
                    pump()
            return ends

        def transp(out, in_, *deps):
            p = in_.shape[0]
            return PE(lambda e: e.transpose(out, in_, ident[0:p, 0:p]), *deps)

        def to_features(src, srctok, gain, gi, banks, free):
            T = [None] * 8
            for t in range(2):
                for k in range(8):
                    b, o = banks[k // 2], (k % 2) * 256 + t * 128
                    T[k] = transp(PS[:, b, o:o + 128], src[:, t, 128 * k:128 * k + 128], srctok[t], bank[b] if t == 0 else None)
            return [d for j in range(4) for d in parts((2 * j, 2 * j + 1), HTh, HTl, banks[j], T[2 * j + 1],
                                                       lambda k: col(gain, gi + k), free)]

        def parts(ks, dh, dl, b, tk, gain, free):
            for i, k in enumerate(ks):
                hi = S(lambda e: e.activation(dh[:, k, :], PS[:, b, 256 * i:256 * i + 256], ACT.Copy, scale=gain(k)), tk, free)
            out = []
            for i, k in enumerate(ks):
                out.append(V(lambda e: e.scalar_tensor_tensor(dl[:, k, :], PS[:, b, 256 * i:256 * i + 256], gain(k),
                                                              dh[:, k, :].bitcast(f32), MUL, SUB), hi, free))
            bank[b] = out[-1:]
            return out

        def rstd(out, ss, n, eps_toks, free=None):
            w = out.shape[1]
            a = V(lambda e: e.tensor_scalar(out, ss, 1.0 / n, 1e-6, MUL, ADD), eps_toks, free)
            return G(lambda e: e.tensor_tensor(out, out, mh[:, 0:w], ALU.pow), a, k_mh)

        def row_norm(src, srctok, out):
            a = [square(lambda e: e.activation(JK[:, :], src[:, t, :], ACT.Square, accum_out=out[:, t:t + 1]), srctok[t])
                 for t in range(2)]
            return rstd(out, out, 1024, a)

        JK = sb("JK", [128, 1024])
        jk = [None]

        def square(fn, *deps):
            jk[0] = S(fn, jk[0], *deps)
            return jk[0]

        def residual(ends, scale, gain_tok):
            toks = []
            for t in range(2):
                sq, yg = [], []
                for hf in range(2):
                    y = PS[:, 2 * t + hf, :]
                    cs = slice(512 * hf, 512 * hf + 512)
                    sq.append(square(lambda e: e.activation(JK[:, cs], y, ACT.Square, scale=scale,
                                                       accum_out=st[:, 60 + 2 * t + hf:61 + 2 * t + hf]), ends[t]))
                    yg.append(V(lambda e: e.tensor_tensor(YG[:, t, cs], y, BC[:, cs], MUL), sq[-1], gain_tok))
                    bank[2 * t + hf] = yg[-1:]
                s0 = V(lambda e: e.tensor_tensor(st[:, t:t + 1], st[:, 60 + 2 * t:61 + 2 * t], st[:, 61 + 2 * t:62 + 2 * t], ADD), sq)
                r = rstd(st[:, t:t + 1], st[:, t:t + 1], 1024, s0)
                if scale != 1.0:
                    r = V(lambda e: e.tensor_scalar(st[:, t:t + 1], st[:, t:t + 1], scale, None, MUL), r)
                toks.append((r, yg))
            out = []
            for t in range(2):
                out.append(V(lambda e, t=t: e.scalar_tensor_tensor(X[:, t, :], YG[:, t, :], st[:, t:t + 1], X[:, t, :], MUL, ADD),
                             toks[t][0], toks[t][1]))
            return out

        def add_residual(ends):
            out = []
            for t in range(2):
                y = PS[:, 2 * t:2 * t + 2, :].rearrange("p a b -> p (a b)")
                a = V(lambda e, t=t, y=y: e.tensor_tensor(X[:, t, :], y, X[:, t, :], ADD), ends[t])
                bank[2 * t] = bank[2 * t + 1] = [a]
                out.append(a)
            return out

        def last(*names):
            return [Q.q[n][-1][1] for n in (names or ("pe", "dve", "act", "pool")) if Q.q.get(n)]

        def ffn(key, xtok, gain, gi, first_free):
            cs = PLAN[key]
            with ExitStack() as sc:
                scope.append(sc)
                fence = last()
                YBh, YBl = sb(key + "YBh", [128, 10, 256], f32r), sb(key + "YBl", [128, 10, 256], f32r)
                TH, SG, AN = (sb(key + n, [128, 2, 2, 256]) for n in ("TH", "SG", "AN"))
                scope.pop()
                ydst = lambda j: (YAh, YAl, j) if j < 12 else (YBh, YBl, j - 12)
                h = to_features(X, xtok, gain, gi, (4, 5, 6, 7), first_free)
                rs = row_norm(X, xtok, st[:, 2:4])
                rs2 = V(lambda e: e.tensor_tensor(st[:, 6:8], st[:, 2:4], st[:, 2:4], MUL), rs)
                rsh = V(lambda e: e.tensor_scalar(st[:, 4:6], st[:, 2:4], 0.5, None, MUL), rs)
                pump()
                pairs = [(0, 1), (2, 3), (6, 7)]
                done = {}
                free = {"TH": {}, "AN": {}}

                def act(g, tk):
                    p = pairs[(g + 1) % 3]
                    for t in range(2):
                        gg, uu = PS[:, p[t], 0:256], PS[:, p[t], 256:512]
                        b = g % 2
                        th = S(lambda e, t=t, b=b, gg=gg: e.activation(TH[:, b, t, :], gg, ACT.Tanh, scale=st[:, 4 + t:5 + t]),
                               tk, rsh, free["TH"].get((g - 2, t)), fence)
                        sg = V(lambda e, t=t, b=b, gg=gg: e.scalar_tensor_tensor(SG[:, b, t, :], TH[:, b, t, :], 1.0, gg, ADD, MUL),
                               th, fence)
                        free["TH"][(g, t)] = sg
                        an = V(lambda e, t=t, b=b, uu=uu: e.scalar_tensor_tensor(AN[:, b, t, :], uu, st[:, 6 + t:7 + t],
                                                                                 SG[:, b, t, :], MUL, MUL),
                               sg, rs2, free["AN"].get(g - 2))
                        bank[p[t]] = [an]
                        done[(g, t)] = an

                ydep = {}

                def fold(g):
                    b = 4 + g % 2
                    for t in range(2):
                        for j in range(2):
                            tk = transp(PS[:, b, j * 256 + t * 128:j * 256 + t * 128 + 128],
                                        AN[:, g % 2, t, 128 * j:128 * j + 128], done[(g, t)], bank[b] if t == 0 and j == 0 else None)
                    free["AN"][g] = tk
                    hi, lo, j = ydst(2 * g)
                    src = PS[:, b, :].rearrange("p (a c) -> p a c", a=2)
                    a = S(lambda e: e.activation(hi[:, j:j + 2, :], src, ACT.Copy, scale=0.5), tk, fence)
                    l = V(lambda e: e.scalar_tensor_tensor(lo[:, j:j + 2, :], src, 0.5, hi[:, j:j + 2, :].bitcast(f32), MUL, SUB), a, fence)
                    bank[b] = [a, l]
                    ydep[2 * g] = ydep[2 * g + 1] = l

                for g in range(11):
                    p = pairs[(g + 1) % 3]
                    tk = nat_mm(cs[2 * g:2 * g + 2], 4, 8, 512, (HTh, HTl), h, p)
                    if g >= 1:
                        fold(g - 1)
                    act(g, tk)
                box = {}

                def dep_of(k):
                    return ydep[k]

                ends = [None, None]
                dcs = cs[22:]
                n = len(dcs)
                for ci, c in enumerate(dcs):
                    s = chunk(c)
                    for t in range(2):
                        for kk in range(2):
                            k = 2 * ci + kk
                            hi, lo, j = ydst(k)
                            for half in range(2):
                                w = slice(kk * 1024 + half * 512, kk * 1024 + half * 512 + 512)
                                ends[t] = mm3(PS[:, 2 * t + half, :], hi[:, j, 128 * t:128 * t + 128],
                                              lo[:, j, 128 * t:128 * t + 128], WH[:, s, w], WL[:, s, w],
                                              k == 0, k == 2 * n - 1, split_tok[c], dep_of(k),
                                              bank[2 * t + half] if k == 0 else None)
                    used_tok[c] = ends[1]
                    if ci == 0:
                        fold(10)
                    if ci < n - 1:
                        pump()
                return ends

        def attention(nm, heads, scope_tok, mask=None):
            P = sb(nm + "P", [128, 2, 2, 256])
            PT = sb(nm + "PT", [128, 2, 2, 256])
            nH = len(heads)
            M = sb(nm + "M", [128, nH, 2])
            den = sb(nm + "den", [128, 2, nH])
            SM = sb(nm + "SM", [128, 2, 2, 256]) if mask else None
            ex, ptf, pvt, pt_ready, tT = {}, {}, {}, {}, {}

            def scores(h):
                parts, _, _, _, _, deps = heads[h]
                b = h % 2
                for t in range(2):
                    for i, (q, k) in enumerate(parts):
                        tk = mm(PS[:, b, 256 * t:256 * t + 256], q[:, 128 * t:128 * t + 128], k,
                                i == 0, i == len(parts) - 1, deps, bank[b] if t == 0 and i == 0 else None)
                src = PS[:, b, :].rearrange("p (t k) -> p t k", t=2)
                if mask:
                    m0 = V(lambda e: e.tensor_tensor(SM[:, b, :, :], src, mask[1], ADD), tk, ex.get(h - 2), mask[2], scope_tok)
                    m = V(lambda e: e.tensor_reduce(M[:, h, :], SM[:, b, :, :], AX.X, ALU.max, negate=True), m0)
                    src = SM[:, b, :, :]
                    bank[b] = [m0]
                else:
                    m = V(lambda e: e.tensor_reduce(M[:, h, :], src, AX.X, ALU.max, negate=True), tk)
                es = []
                for t in range(2):
                    es.append(S(lambda e, t=t: e.activation(P[:, b, t, :], src[:, t, :], ACT.Exp, bias=M[:, h, t:t + 1],
                                                            accum_out=None if mask else den[:, t, h:h + 1]),
                                m, tT.get(h - 2), scope_tok))
                if mask:
                    ex[h] = es
                    es = [V(lambda e, t=t: e.tensor_tensor_reduce(out=P[:, b, t, :], in0=P[:, b, t, :], in1=mask[0][:, t, :],
                                                                  scale=1.0, scalar=0.0, op0=MUL, op1=ADD,
                                                                  accum_out=den[:, t, h:h + 1]), es[t])
                          for t in range(2)]
                else:
                    bank[b] = es + [m]
                ex[("p", h)] = es

            def turn(h):
                b = 2 + h % 2
                for t in range(2):
                    for kt in range(2):
                        tk = transp(PS[:, b, kt * 256 + t * 128:kt * 256 + t * 128 + 128],
                                    P[:, h % 2, t, 128 * kt:128 * kt + 128], ex[("p", h)][t],
                                    bank[b] if t == 0 and kt == 0 else None)
                tT[h] = tk
                dst, src = PT[:, h % 2, :, :], PS[:, b, :].rearrange("p (t k) -> p t k", t=2)
                if h % 2:
                    c = S(lambda e: e.activation(dst, src, ACT.Copy), tk, pvt.get(h - 2), scope_tok)
                else:
                    c = V(lambda e: e.tensor_copy(dst, src), tk, pvt.get(h - 2), scope_tok)
                bank[b] = [c]
                pt_ready[h] = c

            def pv(h):
                _, v, dv, ob, oc, deps = heads[h]
                for t in range(2):
                    for kt in range(2):
                        tk = mm(PS[:, ob + t, oc:oc + dv], PT[:, h % 2, kt, 128 * t:128 * t + 128], v[kt],
                                kt == 0, kt == 1, pt_ready[h], deps, bank[ob + t] if kt == 0 and oc == 0 else None)
                pvt[h] = tk

            return scores, turn, pv, pvt, den, ex

        def run_attention(nm, heads, scope_tok, yout, per_out, mask=None, fill=None):
            scores, turn, pv, pvt, den, ex = attention(nm, heads, scope_tok, mask)
            dv = heads[0][2]
            Y = sb(nm + "Y", [128, 2, 512])
            ydeps = {}
            ytr = [None]

            def finish(h0):
                ob = heads[h0][3]
                hs = slice(h0, h0 + per_out)
                r = V(lambda e: e.reciprocal(den[:, :, hs], den[:, :, hs]), [x for h in range(h0, h0 + per_out) for x in ex[("p", h)]])
                ys = []
                for t in range(2):
                    y = V(lambda e, t=t: e.tensor_tensor(Y[:, t, :].rearrange("p (h d) -> p h d", d=dv),
                                                         PS[:, ob + t, :].rearrange("p (h d) -> p h d", d=dv),
                                                         den[:, t, hs].unsqueeze(2).to_broadcast([128, per_out, dv]), MUL),
                          r, pvt[h0 + per_out - 1], ytr[0], scope_tok)
                    bank[ob + t] = [y]
                    ys.append(y)
                for jp in range(2):
                    b = 2 + jp
                    for j in range(2):
                        for t in range(2):
                            tk = transp(PS[:, b, j * 256 + t * 128:j * 256 + t * 128 + 128],
                                        Y[:, t, 128 * (2 * jp + j):128 * (2 * jp + j) + 128], ys[t],
                                        bank[b] if j == 0 and t == 0 else None)
                    ytr[0] = tk
                    i0 = yout(h0) + 2 * jp
                    src = PS[:, b, :].rearrange("p (a c) -> p a c", a=2)
                    hi = S(lambda e, i0=i0, src=src: e.activation(YAh[:, i0:i0 + 2, :], src, ACT.Copy), tk)
                    lo = V(lambda e, i0=i0, src=src: e.tensor_tensor(YAl[:, i0:i0 + 2, :], src, YAh[:, i0:i0 + 2, :].bitcast(f32), SUB), hi)
                    bank[b] = [hi, lo]
                    ydeps[i0] = ydeps[i0 + 1] = lo

            n = len(heads)
            for h in range(n + 2):
                if h < n:
                    scores(h)
                if 0 <= h - 1 < n:
                    turn(h - 1)
                if 0 <= h - 2 < n:
                    pv(h - 2)
                    if (h - 2) % per_out == per_out - 1:
                        finish(h - 2 - per_out + 1)
                if fill:
                    fill(h)
            return ydeps

        def head_rstd(z, nh, d, out, ztok):
            j = JK[:, 0:nh * d]
            a = square(lambda e: e.activation(j, z, ACT.Square), ztok)
            b = V(lambda e: e.tensor_reduce(out, j.rearrange("p (h d) -> p h d", d=d), AX.X, ADD), a)
            jk[0] = b
            return rstd(out, out, d, b)

        def scaled(z, nh, d, r, *toks):
            zv = z.rearrange("p (h d) -> p h d", d=d)
            return V(lambda e: e.tensor_tensor(zv, zv, r.unsqueeze(2).to_broadcast([128, nh, d]), MUL), *toks)

        k_id = load("sp", ident[:, :], A["tab"][:, 0:128], "c_id")
        k_x = [load("sp", X[:, t, :], A["x"][128 * t:128 * t + 128, :], f"c_x{t}") for t in range(2)]
        k_c = load("sp", cst[:, :], A["cols"][:, :], "c_c")
        for _ in range(NR):
            stream_load()
        k_mh = G(lambda e: e.memset(mh[:, :], -0.5))

        def gain_row(i, *deps):
            return load("pool", BC[:, :], A["rows"][:, 1024 * i:1024 * i + 1024], "c_bc", *deps)

        k_bc = gain_row(0)

        with ExitStack() as sc:
            scope.append(sc)
            cmask, cbias = sb("cmask", [128, 2, 256]), sb("cbias", [128, 2, 256])
            tt = sb("tt", [128, 256])
            inv = sb("inv", [128, 8])
            uT = sb("uT", [128, 4, 256])
            Qn, Kn, Vn = sb("Qn", [128, 2, 512]), sb("Kn", [128, 2, 512]), sb("Vn", [128, 2, 512])
            QT, KT = sb("QT", [128, 4, 256]), sb("KT", [128, 4, 256])
            yq = sb("yq", [128, 4, 256])
            s5scope = sc.enter_context(ExitStack())
            scope.append(s5scope)
            BB = sb("BB", [128, 2, 4, 128])
            CC = sb("CC", [128, 2, 16, 16])
            pos = sb("pos", [128, 2], i32)
            k_m = load("sp", cmask[:, :, :], A["tab"][:, 128:640].rearrange("p (t k) -> p t k", t=2), "c_m")
            k_m2 = load("sp", cbias[:, :, :], A["tab"][:, 640:1152].rearrange("p (t k) -> p t k", t=2), "c_m2")
            k_t = load("sp", tt[:, :], A["tab"][:, 1152:1408], "c_t")
            k_i = load("sp", inv[:, :], A["tab"][:, 1408:1416], "c_i")
            k_B = load("sp", BB[:, :, :, :], A["s5"][:, 0:1024].rearrange("p (r q s) -> p r q s", r=2, q=4), "c_B")
            k_C = load("sp", CC[:, :, :, :], A["s5"][:, 1024:1536].rearrange("p (r j c) -> p r j c", r=2, j=16), "c_C")
            k_p = load("sp", pos[:, :], A["pos"][:, :], "c_p")

            h = to_features(X, [[k, k_id] for k in k_x], "norm_mix_pre", 0, (4, 5, 6, 7), k_c)
            rs = row_norm(X, k_x, st[:, 2:4])
            pump()

            def evac(banks, dst, tk):
                out = []
                for t in range(2):
                    a = S(lambda e, t=t: e.activation(dst[:, t, :], PS[:, banks[t], :], ACT.Copy, scale=st[:, 2 + t:3 + t]), tk, rs)
                    bank[banks[t]] = [a]
                    out.append(a)
                return out

            def turn_pairs(src, toks, dst, bks):
                out = []
                for jp in range(2):
                    b = bks[jp]
                    for j in range(2):
                        for t in range(2):
                            tk = transp(PS[:, b, j * 256 + t * 128:j * 256 + t * 128 + 128],
                                        src[:, t, 128 * (2 * jp + j):128 * (2 * jp + j) + 128], toks[t],
                                        bank[b] if j == 0 and t == 0 else None)
                    a = S(lambda e, b=b, jp=jp: e.activation(dst[:, 2 * jp:2 * jp + 2, :],
                                                             PS[:, b, :].rearrange("p (a c) -> p a c", a=2), ACT.Copy), tk)
                    bank[b] = [a]
                    out.append(a)
                return out

            tk = nat_mm(PLAN["ev_u"], 4, 8, 512, (HTh, HTl), h, (0, 1))
            ue = evac((0, 1), Qn, tk)
            tk = nat_mm(PLAN["ev_q"], 4, 8, 512, (HTh, HTl), h, (2, 3))
            uT_t = turn_pairs(Qn, ue, uT, (4, 5))

            s5 = sb("s5", [128, 16, 16])
            p = lambda i: s5[:, i, :]
            DT, R, TH_, PH, SN, CS, N1, N2, DEN, FR, FI = (p(i) for i in range(11))
            d1 = S(lambda e: e.activation(DT, col("s5_log_dt", 0, 16), ACT.Exp), k_c)
            d2 = V(lambda e: e.tensor_tensor(R, col("s5_a_re", 0, 16), DT, MUL), d1)
            d3 = S(lambda e: e.activation(R, R, ACT.Exp), d2)
            d4 = V(lambda e: e.tensor_tensor(TH_, col("s5_a_im", 0, 16), DT, MUL), d1)
            MAGIC = 12582912.0
            C1, C2 = 6.28125, float(np.float32(0.0019350051879882812))
            C3 = TWO_PI - C1 - C2

            def reduce_2pi(x, n, *deps):
                a = V(lambda e: e.tensor_scalar(n, x, 1.0 / TWO_PI, MAGIC, MUL, ADD), *deps)
                a = V(lambda e: e.tensor_scalar(n, n, MAGIC, None, SUB), a)
                for cc in (C1, C2, C3):
                    a = V(lambda e, cc=cc: e.scalar_tensor_tensor(x, n, -cc, x, MUL, ADD), a)
                return V(lambda e: e.tensor_scalar(x, x, 3.1415925, -3.1415925, ALU.min, ALU.max), a)

            d5 = reduce_2pi(TH_, N1, d4)
            d6 = V(lambda e: e.tensor_scalar(PH, TH_, 1.0 / TWO_PI, None, MUL), d5)
            ang = sb("ang", [128, 2, 8])
            angn = sb("angn", [128, 2, 8])
            rc, rsn = sb("rc", [128, 2, 2, 8]), sb("rsn", [128, 2, 2, 8])
            posf = sb("posf", [128, 2])
            a1 = V(lambda e: e.tensor_copy(posf[:, :], pos[:, :]), k_p)
            for t in range(2):
                a2 = V(lambda e, t=t: e.tensor_scalar(ang[:, t, :], inv[:, :], posf[:, t:t + 1], None, MUL), a1, k_i)
            a3 = reduce_2pi(ang[:, :, :], angn[:, :, :], a2)
            a4 = S(lambda e: e.activation(angn[:, :, :], ang[:, :, :], ACT.Abs), a3)
            d7 = S(lambda e: e.activation(N1, TH_, ACT.Abs), d5)
            a7 = V(lambda e: e.tensor_scalar(angn[:, :, :], angn[:, :, :], -1.0, TWO_PI / 4, MUL, ADD), a4)
            d8 = V(lambda e: e.tensor_scalar(N1, N1, -1.0, TWO_PI / 4, MUL, ADD), d7)
            for hh in range(2):
                a5 = S(lambda e, hh=hh: e.activation(rsn[:, :, hh, :], ang[:, :, :], ACT.Sin), a3)
                a6 = S(lambda e, hh=hh: e.activation(rc[:, :, hh, :], angn[:, :, :], ACT.Sin), a7)
            k_rope = [a5, a6]
            d9 = S(lambda e: e.activation(SN, TH_, ACT.Sin), d5)
            d10 = S(lambda e: e.activation(CS, N1, ACT.Sin), d8)
            AR, AI = col("s5_a_re", 0, 16), col("s5_a_im", 0, 16)
            e1 = V(lambda e: e.tensor_tensor(SN, SN, R, MUL), d9, d3)
            e2 = V(lambda e: e.tensor_tensor(CS, CS, R, MUL), d10, d3)
            e3 = V(lambda e: e.tensor_scalar(CS, CS, -1.0, None, ADD), e2)
            e4 = V(lambda e: e.tensor_tensor(N1, AR, AR, MUL), e3)
            e5 = V(lambda e: e.tensor_tensor(N2, AI, AI, MUL))
            e6 = V(lambda e: e.tensor_tensor(DEN, N1, N2, ADD), e4, e5)
            e7 = V(lambda e: e.reciprocal(DEN, DEN), e6)
            e8 = V(lambda e: e.tensor_tensor(N1, CS, AR, MUL), e6, e3)
            e9 = V(lambda e: e.tensor_tensor(N2, SN, AI, MUL), e6, e1)
            e10 = V(lambda e: e.tensor_tensor(FR, N1, N2, ADD), e8, e9)
            e11 = V(lambda e: e.tensor_tensor(FR, FR, DEN, MUL), e10, e7)
            e12 = V(lambda e: e.tensor_tensor(N1, SN, AR, MUL), e10)
            e13 = V(lambda e: e.tensor_tensor(N2, CS, AI, MUL), e10)
            e14 = V(lambda e: e.tensor_tensor(FI, N1, N2, SUB), e12, e13)
            k_f = V(lambda e: e.tensor_tensor(FI, FI, DEN, MUL), e14, e11)
            CF = sb("CF", [128, 2, 16, 16])
            CT = sb("CT", [128, 16, 16])
            fr = FR.unsqueeze(2).to_broadcast([128, 16, 16])
            fi = FI.unsqueeze(2).to_broadcast([128, 16, 16])
            c1 = V(lambda e: e.tensor_tensor(CF[:, 0, :, :], CC[:, 0, :, :], fr, MUL), k_f, k_C)
            c2 = V(lambda e: e.tensor_tensor(CT[:, :, :], CC[:, 1, :, :], fi, MUL), k_f)
            c3 = V(lambda e: e.tensor_tensor(CF[:, 0, :, :], CF[:, 0, :, :], CT[:, :, :], SUB), c1, c2)
            c4 = V(lambda e: e.tensor_tensor(CF[:, 1, :, :], CC[:, 0, :, :], fi, MUL), c3)
            c5 = V(lambda e: e.tensor_tensor(CT[:, :, :], CC[:, 1, :, :], fr, MUL), c3)
            c6 = V(lambda e: e.tensor_tensor(CF[:, 1, :, :], CF[:, 1, :, :], CT[:, :, :], ADD), c4, c5)
            k_cf = V(lambda e: e.tensor_scalar(CF[:, 1, :, :], CF[:, 1, :, :], -1.0, None, MUL), c6)
            CP = sb("CP", [128, 2, 4, 128])
            k_cp0 = G(lambda e: e.memset(CP[:, :, :, :], 0.0))
            cosT, sinT = sb("cosT", [128, 4, 256]), sb("sinT", [128, 4, 256])
            T2, T3 = sb("T2", [128, 4, 256]), sb("T3", [128, 4, 256])
            T0, T1 = (YG[:, i, :].rearrange("p (a b) -> p a b", a=4) for i in range(2))
            RB = sb("RB", [128, 4, 256])
            ssm = {}
            fr_s5 = {"cp": None, "tab": None, "T": []}

            def s5_quarter(qn):
                js = range(4 * qn, 4 * qn + 4)
                u = [V(lambda e, i=i, j=j: e.tensor_scalar(T0[:, i, :], tt[:, :], PH[:, j:j + 1], None, MUL), d6, k_t, fr_s5["T"])
                     for i, j in enumerate(js)]
                n = V(lambda e: e.tensor_scalar(T1[:, :, :], T0[:, :, :], MAGIC, None, ADD), u)
                nr = V(lambda e: e.scalar_tensor_tensor(T1[:, :, :], T1[:, :, :], MAGIC, T0[:, :, :], SUB, SUB), n)
                ab = V(lambda e: e.scalar_tensor_tensor(T0[:, :, :], T1[:, :, :], -1.0, T1[:, :, :], MUL, ALU.max), nr)
                ab = V(lambda e: e.tensor_scalar(T0[:, :, :], T0[:, :, :], -6.283185, TWO_PI / 4, MUL, ADD), ab)
                sn = S(lambda e: e.activation(sinT[:, :, :], T1[:, :, :], ACT.Sin, scale=-6.283185), nr, fr_s5["tab"])
                cs = S(lambda e: e.activation(cosT[:, :, :], T0[:, :, :], ACT.Sin), ab, fr_s5["tab"])
                rb = []
                for i, j in enumerate(js):
                    rb.append(G(lambda e, i=i, j=j: e.tensor_scalar(RB[:, i, :], tt[:, :], 0.0, R[:, j:j + 1], MUL, ADD),
                                d3, k_t, fr_s5["tab"]))
                rb.append(G(lambda e: e.memset(RB[:, :, 0:1], 0.0), rb))
                cp = []
                for jj in range(4):
                    for hf in range(2):
                        cp.append(V(lambda e, jj=jj, hf=hf: e.tensor_copy(
                            CP[64 * hf:64 * hf + 64, :, jj, 32 * jj + 16 * hf:32 * jj + 16 * hf + 16],
                            CF[64 * hf:64 * hf + 64, :, 4 * qn + jj, :]), k_cf, k_cp0, fr_s5["cp"]))
                for ri in range(2):
                    for jj in range(4):
                        bu = mm(PS[:, 4 + jj, 256 * ri:256 * ri + 256], BB[32 * jj:32 * jj + 32, ri, qn, :],
                                uT[32 * jj:32 * jj + 32, qn, :], True, True, k_B, uT_t, bank[4 + jj] if ri == 0 else None)
                br, bi = PS[:, 4:8, 0:256], PS[:, 4:8, 256:512]
                v1 = V(lambda e: e.tensor_tensor(T0[:, :, :], br, cosT[:, :, :], MUL), bu, sn, cs)
                v2 = V(lambda e: e.tensor_tensor(T1[:, :, :], bi, sinT[:, :, :], MUL))
                v3 = V(lambda e: e.tensor_tensor(T2[:, :, :], bi, cosT[:, :, :], MUL), fr_s5["T"])
                v4 = V(lambda e: e.tensor_tensor(T3[:, :, :], br, sinT[:, :, :], MUL))
                for b in range(4, 8):
                    bank[b] = [v4]
                v5 = G(lambda e: e.tensor_tensor(T0[:, :, :], T0[:, :, :], T1[:, :, :], ADD), v1, v2)
                v6 = G(lambda e: e.tensor_tensor(T2[:, :, :], T2[:, :, :], T3[:, :, :], SUB), v3, v4)
                fl = lambda a: a[:, :, :].rearrange("p a b -> p (a b)")
                g1 = V(lambda e: e.tensor_tensor_scan(fl(T0), fl(RB), fl(T0), 0.0, MUL, ADD), v5, rb)
                g2 = V(lambda e: e.tensor_tensor_scan(fl(T2), fl(RB), fl(T2), 0.0, MUL, ADD), v6, rb)
                w1 = V(lambda e: e.tensor_tensor(T1[:, :, :], T0[:, :, :], cosT[:, :, :], MUL), g1)
                w2 = V(lambda e: e.tensor_tensor(T3[:, :, :], T2[:, :, :], sinT[:, :, :], MUL), g2)
                w3 = V(lambda e: e.tensor_tensor(T0[:, :, :], T0[:, :, :], sinT[:, :, :], MUL), w1)
                w4 = V(lambda e: e.tensor_tensor(T2[:, :, :], T2[:, :, :], cosT[:, :, :], MUL), w2)
                fr_s5["tab"] = [w3, w4, g2]
                w5 = G(lambda e: e.tensor_tensor(T1[:, :, :], T1[:, :, :], T3[:, :, :], SUB), w1, w2)
                w6 = G(lambda e: e.tensor_tensor(T0[:, :, :], T0[:, :, :], T2[:, :, :], ADD), w3, w4)

                def tail():
                    b = 4 + qn
                    for jj in range(4):
                        mm(PS[:, b, 0:256], CP[:, 0, jj, :], T1[:, jj, :], jj == 0, False, w5, cp, bank[b] if jj == 0 else None)
                        y = mm(PS[:, b, 0:256], CP[:, 1, jj, :], T0[:, jj, :], False, jj == 3, w6)
                    fr_s5["cp"] = y
                    fr_s5["T"] = [y]
                    yy = V(lambda e: e.scalar_tensor_tensor(yq[:, qn, :], uT[:, qn, :], col("s5_d", qn), PS[:, b, 0:256], MUL, ADD), y)
                    bank[b] = [yy]
                    ssm[qn] = yy
                return tail

            tail = s5_quarter(0)
            qe = evac((2, 3), Qn, tk)
            tk = nat_mm(PLAN["ev_k"], 4, 8, 512, (HTh, HTl), h, (0, 1))
            ke = evac((0, 1), Kn, tk)
            tail()
            tail = s5_quarter(1)
            tk = nat_mm(PLAN["ev_v"], 4, 8, 512, (HTh, HTl), h, (2, 3))
            ve = evac((2, 3), Vn, tk)
            tail()
            tail = s5_quarter(2)

            RA, RBb = sb("RA", [128, 8, 16]), sb("RBb", [128, 8, 16])

            def rope16(z, toks, prev):
                for t in range(2):
                    zv = z[:, t, :].rearrange("p (h d) -> p h d", d=64)[:, :, 0:16]
                    cb = rc[:, t, :, :].rearrange("p a b -> p (a b)").unsqueeze(1).to_broadcast([128, 8, 16])
                    sbb = rsn[:, t, :, :].rearrange("p a b -> p (a b)").unsqueeze(1).to_broadcast([128, 8, 16])
                    x1 = G(lambda e, zv=zv, cb=cb: e.tensor_tensor(RA[:, :, :], zv, cb, MUL), toks[t], k_rope, prev)
                    x2 = G(lambda e, zv=zv, sbb=sbb: e.tensor_tensor(RBb[:, :, :], zv, sbb, MUL), prev)
                    x3 = G(lambda e, zv=zv: e.tensor_tensor(zv[:, :, 0:8], RA[:, :, 0:8], RBb[:, :, 8:16], SUB), x1, x2)
                    prev = G(lambda e, zv=zv: e.tensor_tensor(zv[:, :, 8:16], RA[:, :, 8:16], RBb[:, :, 0:8], ADD), x3)
                return prev

            rq = rope16(Qn, qe, None)
            rk = rope16(Kn, ke, rq)
            for t in range(2):
                qs = V(lambda e, t=t: e.tensor_scalar(Qn[:, t, :], Qn[:, t, :], 0.125, None, MUL), rq)
            qT_t = turn_pairs(Qn, [qs, qs], QT, (0, 1))
            kT_t = turn_pairs(Kn, [rk, rk], KT, (0, 1))
            tail()
            tail = s5_quarter(3)
            heads = []
            for hh in range(8):
                pr = slice(64 * (hh % 2), 64 * (hh % 2) + 64)
                heads.append(([(QT[pr, hh // 2, :], KT[pr, hh // 2, :])], [Vn[:, kt, 64 * hh:64 * hh + 64] for kt in range(2)],
                              64, 6, 64 * hh, [qT_t, kT_t, ve]))
            tail()
            scope.pop()
            s5scope.close()
            fence = last()
            ydeps = run_attention("A0", heads, fence, lambda h0: 0, 8, mask=(cmask, cbias[:, :, :], [k_m, k_m2]))

            gy = S(lambda e: e.activation(yq[:, :, :], yq[:, :, :], ACT.Gelu_apprx_tanh), [ssm[i] for i in range(4)])
            gh = S(lambda e: e.activation(YAh[:, 8:12, :], yq[:, :, :], ACT.Copy), gy)
            gl = V(lambda e: e.tensor_tensor(YAl[:, 8:12, :], yq[:, :, :], YAh[:, 8:12, :].bitcast(f32), SUB), gh)
            c = PLAN["glu"][0]
            s = chunk(c)
            gt = {}
            for m in range(4):
                b = 4 + m // 2
                o = 256 * (m % 2)
                for k in range(4):
                    w = slice(512 * k + 128 * m, 512 * k + 128 * m + 128)
                    tk = mm3(PS[:, b, o:o + 256], WH[:, s, w], WL[:, s, w], YAh[:, 8 + k, :], YAl[:, 8 + k, :],
                             k == 0, k == 3, split_tok[c], gl, bank[b] if k == 0 and m % 2 == 0 else None)
                gt[m] = tk
            used_tok[c] = tk
            pump()
            ty = S(lambda e: e.activation(T0[:, :, :], PS[:, 4:6, :].rearrange("p a (b c) -> p (a b) c", b=2), ACT.Tanh, scale=0.5), tk)
            bank[4] = bank[5] = [ty]
            t2 = V(lambda e: e.tensor_scalar(T0[:, :, :], T0[:, :, :], 0.5, 0.5, MUL, ADD), ty)
            t3 = V(lambda e: e.tensor_tensor(T0[:, :, :], T0[:, :, :], yq[:, :, :], MUL), t2)
            t4 = S(lambda e: e.activation(YAh[:, 4:8, :], T0[:, :, :], ACT.Copy), t3)
            t5 = V(lambda e: e.tensor_tensor(YAl[:, 4:8, :], T0[:, :, :], YAh[:, 4:8, :].bitcast(f32), SUB), t4)
            for i in range(4, 8):
                ydeps[i] = t5
            ends = wide_mm(PLAN["ev_out"], lambda k: (YAh, YAl, k), lambda k: ydeps[k])
            scope.pop()
        xt = residual(ends, 1.0, k_bc)
        k_bc = gain_row(2, xt)
        ends = ffn("ffn0", xt, "norm_ffn_pre", 0, ends)
        xt = residual(ends, 1.0, k_bc)
        k_bc = gain_row(1, xt)

        KM, VM = sb("KM", [128, 2, 4, 256]), sb("VM", [128, 2, 2, 512])
        kmt, vmt = {}, {}
        k_mem = {}

        def mem_project(i, MN, fence):
            k_mem = [load("pool", MN[:, t, :], A["mem"][128 * t:128 * t + 128, :], f"c_mem{i}{t}", fence) for t in range(2)]
            return k_mem

        def mem_kv(i, MN, k_mem, mr, free, kz, kz_free):
            h = to_features(MN, k_mem, "mem_norm_2", 0, (4, 5, 6, 7), free)
            rs = row_norm(MN, k_mem, mr)
            tk = nat_mm(PLAN[f"mem{i}0"], 4, 8, 512, (HTh, HTl), h, (0, 1))
            z = []
            for t in range(2):
                a = S(lambda e, t=t: e.activation(kz[:, t, :], PS[:, t, :], ACT.Copy, scale=mr[:, t:t + 1]), tk, rs, kz_free)
                bank[t] = [a]
                z.append(a)
            tk = nat_mm(PLAN[f"mem{i}1"], 4, 8, 512, (HTh, HTl), h, (2, 3))
            done = tk
            for t in range(2):
                a = S(lambda e, t=t: e.activation(VM[:, i, t, :], PS[:, 2 + t, :], ACT.Copy, scale=mr[:, t:t + 1]), tk, rs)
                bank[2 + t] = [a]
                vmt.setdefault(i, []).append(a)
            zz = []
            for t in range(2):
                r = head_rstd(kz[:, t, :], 4, 128, st[:, 8 + 4 * t:12 + 4 * t], z[t])
                zz.append(scaled(kz[:, t, :], 4, 128, st[:, 8 + 4 * t:12 + 4 * t], r))
            kmt[i] = gain_turn(kz, zz, lambda j: KM[:, i, j:j + 2, :], col("memk_norm_2", i), (4, 5))
            return done

        def gain_turn(src, toks, dst, gain, bks, ntile=4):
            out = []
            for jp in range(ntile // 2):
                b = bks[jp % 2]
                for j in range(2):
                    for t in range(2):
                        tk = transp(PS[:, b, j * 256 + t * 128:j * 256 + t * 128 + 128],
                                    src[:, t, 128 * (2 * jp + j):128 * (2 * jp + j) + 128], toks[t],
                                    bank[b] if j == 0 and t == 0 else None)
                a = S(lambda e, b=b, jp=jp: e.activation(dst(2 * jp), PS[:, b, :].rearrange("p (a c) -> p a c", a=2),
                                                         ACT.Copy, scale=gain), tk)
                bank[b] = [a]
                out.append(a)
            return out

        with ExitStack() as sc:
            scope.append(sc)
            fence = last()
            XB = sb("XB", [128, 8, 259])
            GT = sb("GT", [128, 8, 256])
            XC = sb("XC", [128, 8, 256])
            TR, TI = sb("TR", [128, 8, 256]), sb("TI", [128, 8, 256])
            ZN = sb("ZN", [128, 2, 2, 512])
            MN = YG
            KZ = sb("KZ", [128, 2, 512])
            k_mem = mem_project(0, MN, fence)
            h = to_features(X, xt, "norm_mix_pre", 8, (4, 5, 6, 7), ends)
            rs = row_norm(X, xt, st[:, 2:4])
            pump()
            z0 = V(lambda e: e.memset(XB[:, :, 0:3], 0.0), fence)
            lm = sb("lm", [128, 8, 8])
            L = lambda i: lm[:, i, :]
            l1 = S(lambda e: e.activation(L(0), col("rg_lam", 0, 8), ACT.Abs), fence)
            l2 = S(lambda e: e.activation(L(0), L(0), ACT.Exp, scale=-1.0), l1)
            l3 = V(lambda e: e.tensor_scalar(L(1), L(0), 2.0, None, ADD), l2)
            l4 = V(lambda e: e.reciprocal(L(1), L(1)), l3)
            l5 = V(lambda e: e.tensor_tensor(L(1), L(1), L(0), MUL), l4)
            l6 = V(lambda e: e.tensor_tensor(L(2), L(1), L(1), MUL), l5)
            a = V(lambda e: e.tensor_scalar(L(3), L(2), 1.0 / 19, 1.0 / 17, MUL, ADD), l6)
            for m in (15, 13, 11, 9, 7, 5, 3, 1):
                a = V(lambda e: e.tensor_tensor(L(3), L(3), L(2), MUL), a)
                a = V(lambda e, m=m: e.tensor_scalar(L(3), L(3), 1.0 / m, None, ADD), a)
            l7 = V(lambda e: e.tensor_tensor(L(3), L(3), L(1), MUL), a)
            l8 = V(lambda e: e.tensor_scalar(L(4), col("rg_lam", 0, 8), -1.0, 0.0, MUL, ALU.max), l7)
            l9 = V(lambda e: e.scalar_tensor_tensor(L(3), L(3), 2.0, L(4), MUL, ADD), l8)
            l10 = V(lambda e: e.tensor_scalar(L(5), L(3), 4.0, None, MUL), l9)
            l11 = V(lambda e: e.tensor_scalar(L(6), L(3), -4.0, None, MUL), l9)
            l12 = V(lambda e: e.tensor_scalar(L(0), col("rg_b_r", 0, 8), 0.5, None, MUL), l5)
            l13 = V(lambda e: e.tensor_scalar(L(1), col("rg_b_i", 0, 8), 0.5, None, MUL), l7)
            k_l = [l10, l11, l12, l13]

            zt = {}
            xb, xc, tt_ = {}, {}, {}
            for g in range(4):
                pr = ((0, 1), (2, 3))[g % 2]
                tk = nat_mm(PLAN[f"od{g}"], 4, 8, 512, (HTh, HTl), h, pr)
                zz = []
                for t in range(2):
                    a = S(lambda e, t=t, g=g, pr=pr: e.activation(ZN[:, g % 2, t, :], PS[:, pr[t], :], ACT.Copy, scale=st[:, 2 + t:3 + t]),
                          tk, rs, zt.get(g - 2), fence)
                    bank[pr[t]] = [a]
                    zz.append(a)
                for jp in range(2):
                    b = 4 + jp
                    for j in range(2):
                        for t in range(2):
                            tk = transp(PS[:, b, j * 256 + t * 128:j * 256 + t * 128 + 128],
                                        ZN[:, g % 2, t, 128 * (2 * jp + j):128 * (2 * jp + j) + 128], zz[t],
                                        bank[b] if j == 0 and t == 0 else None)
                    zt[g] = tk
                    src = PS[:, b, :].rearrange("p (a c) -> p a c", a=2)
                    i0 = (4 * g + 2 * jp) % 8
                    if g < 2:
                        a = S(lambda e, i0=i0, src=src: e.activation(XB[:, i0:i0 + 2, 3:259], src, ACT.Copy), tk, fence)
                        xb[i0] = xb[i0 + 1] = a
                    else:
                        a = S(lambda e, i0=i0, src=src: e.activation(GT[:, i0:i0 + 2, :], src, ACT.Gelu_apprx_tanh), tk, fence)
                        gtok = a
                    bank[b] = [a]
                if g < 2:
                    for j in range(4 * g, 4 * g + 4):
                        a = V(lambda e, j=j: e.tensor_scalar(XC[:, j, :], XB[:, j, 3:259], col("rg_conv_w", 24 + j), col("rg_conv_b", j), MUL, ADD),
                              xb[j], z0, fence)
                        for w in range(3):
                            a = V(lambda e, j=j, w=w: e.scalar_tensor_tensor(XC[:, j, :], XB[:, j, w:w + 256], col("rg_conv_w", 8 * w + j),
                                                                             XC[:, j, :], MUL, ADD), a)
                        if j % 4 == 3:
                            hi = S(lambda e, j=j: e.activation(YAh[:, j - 3:j + 1, :], XC[:, j - 3:j + 1, :], ACT.Copy), a, fence)
                            lo = V(lambda e, j=j: e.tensor_tensor(YAl[:, j - 3:j + 1, :], XC[:, j - 3:j + 1, :],
                                                                  YAh[:, j - 3:j + 1, :].bitcast(f32), SUB), hi, fence)
                            for m in range(j - 3, j + 1):
                                xc[m] = lo
            odlast = tk
            for hb in range(4):
                c = PLAN["rg"][hb // 2]
                s = chunk(c)
                for gi in range(2):
                    b = 6 + gi
                    for j in range(2):
                        for k in range(2):
                            o = 1024 * (hb % 2) + 512 * gi + 256 * k + 128 * j
                            tk = mm3(PS[:, b, 256 * j:256 * j + 256], WH[:, s, o:o + 128], WL[:, s, o:o + 128],
                                     YAh[:, 2 * hb + k, :], YAl[:, 2 * hb + k, :], k == 0, k == 1,
                                     split_tok[c], xc[2 * hb + k], bank[b] if j == 0 and k == 0 else None)
                    es = []
                    for j in range(2):
                        es.append(S(lambda e, gi=gi, hb=hb, j=j, b=b: e.activation(
                            (TR, TI)[gi][:, 2 * hb + j, :], PS[:, b, 256 * j:256 * j + 256], ACT.Tanh,
                            bias=L(gi)[:, 2 * hb + j:2 * hb + j + 1], scale=0.5), tk, k_l, fence))
                    bank[b] = es
                    tt_[(gi, hb)] = es
                if hb % 2:
                    used_tok[c] = tk
                    pump()
            rg_pe = tk
            th = [S(lambda e, j=j: e.activation(XB[:, j, 0:256], TR[:, j, :], ACT.Tanh, bias=L(5)[:, j:j + 1], scale=L(5)[:, j:j + 1]),
                    tt_[(0, j // 2)], [xc[m] for m in range(8)]) for j in range(8)]
            aa = [S(lambda e, j=j: e.activation(TR[:, j, :], TR[:, j, :], ACT.Exp, bias=L(6)[:, j:j + 1], scale=L(6)[:, j:j + 1]), th[j])
                  for j in range(8)]
            memdone = mem_kv(0, MN, k_mem, st[:, 16:18], odlast, KZ, None)
            HS = XC
            b4 = V(lambda e: e.scalar_tensor_tensor(TI[:, :, :], TI[:, :, :], 1.0, XC[:, :, :], ADD, MUL), [x for hb in range(4) for x in tt_[(1, hb)]])
            b1 = V(lambda e: e.tensor_tensor(HS[:, :, :], TR[:, :, :], TR[:, :, :], MUL), aa, b4)
            b2 = V(lambda e: e.scalar_tensor_tensor(HS[:, :, :], HS[:, :, :], 1.0, XB[:, :, 0:256], ADD, MUL), b1, th)
            b3 = S(lambda e: e.activation(HS[:, :, :], HS[:, :, :], ACT.Sqrt, scale=0.25), b2)
            b5 = V(lambda e: e.tensor_tensor(TI[:, :, :], TI[:, :, :], HS[:, :, :], MUL), b3, b4)
            b6 = V(lambda e: e.memset(TR[:, :, 0:1], 0.0), b1)
            fl = lambda a: a[:, :, :].rearrange("p a b -> p (a b)")
            for hf in range(2):
                hs = slice(4 * hf, 4 * hf + 4)
                fl4 = lambda a: a[:, hs, :].rearrange("p a b -> p (a b)")
                b7 = V(lambda e, fl4=fl4: e.tensor_tensor_scan(fl4(HS), fl4(TR), fl4(TI), 0.0, MUL, ADD), b5, b6)
                b8 = V(lambda e, hs=hs: e.tensor_tensor(HS[:, hs, :], HS[:, hs, :], GT[:, hs, :], MUL), b7, gtok)
                b9 = S(lambda e, hs=hs: e.activation(YAh[:, hs, :], HS[:, hs, :], ACT.Copy), b8, rg_pe)
                b10 = V(lambda e, hs=hs: e.tensor_tensor(YAl[:, hs, :], HS[:, hs, :], YAh[:, hs, :].bitcast(f32), SUB), b9, rg_pe)
                for m in range(4 * hf, 4 * hf + 4):
                    ydeps[m] = b10
            ends = wide_mm(PLAN["od_out"], lambda k: (YAh, YAl, k), lambda k: ydeps[k])
            scope.pop()
        xt = residual(ends, 1.0, k_bc)
        k_bc = gain_row(3, xt)
        ends = ffn("ffn1", xt, "norm_ffn_pre", 8, ends)
        xt = residual(ends, 1.0, k_bc)

        with ExitStack() as sc:
            scope.append(sc)
            fence = last()
            QMT = sb("QMT", [128, 4, 256])
            QTn, KTn = sb("QTn", [128, 8, 256]), sb("KTn", [128, 8, 256])
            QTp = sb("QTp", [64, 8, 256])
            KPT = sb("KPT", [64, 256])
            VV = YG
            inner = sc.enter_context(ExitStack())
            scope.append(inner)
            tb = sb("tb", [128, 2, 2, 64])
            GR = sb("GR", [128, 2, 64])
            k_tb = load("pool", tb[:, :, :, :], A["tab2"][:, 0:256].rearrange("p (c t d) -> p c t d", c=2, t=2), "c_tb", fence)
            k_gr = load("pool", GR[:, :, :], A["rows"][:, 4096:4224].rearrange("p (a d) -> p a d", a=2), "c_gr", fence)
            ZA = sb("ZA", [128, 2, 448])
            ZB = sb("ZB", [128, 2, 512])
            CTh, CTl = YAh, YAl
            gq = sb("gq", [128, 4])
            sc_mla = 192.0 ** -0.5
            sc_mem = 128.0 ** -0.5
            g1 = V(lambda e: e.tensor_scalar(gq[:, 0:1], col("mla_qn"), sc_mla, None, MUL), fence)
            g2 = V(lambda e: e.tensor_scalar(gq[:, 1:2], col("memq_norm_2", 0), sc_mem, None, MUL))
            g3 = V(lambda e: e.tensor_scalar(gq[:, 2:3], col("memq_norm_2", 1), sc_mem, None, MUL))

            h = to_features(X, xt, "norm_mix_2", 0, (4, 5, 6, 7), ends)
            rs = row_norm(X, xt, st[:, 2:4])
            pump()

            def z_evac(pr, dst, n, tk, *deps):
                out = []
                for t in range(2):
                    a = S(lambda e, t=t: e.activation(dst[:, t, 0:n], PS[:, pr[t], 0:n], ACT.Copy, scale=st[:, 2 + t:3 + t]), tk, rs, *deps)
                    bank[pr[t]] = [a]
                    out.append(a)
                return out

            ta = nat_mm(PLAN["mla_a"], 4, 8, 448, (HTh, HTl), h, (0, 1))
            za = z_evac((0, 1), ZA, 448, ta, fence)
            tb_ = nat_mm(PLAN["mla_b"], 8, 8, 256, (HTh, HTl), h, (2, 3))
            zb = z_evac((2, 3), ZB, 256, tb_, fence)
            tc_ = nat_mm(PLAN["mla_c"], 4, 8, 512, (HTh, HTl), h, (0, 1))

            zq, zk = [], []
            for t in range(2):
                r = head_rstd(ZA[:, t, 0:384], 1, 384, st[:, 20 + t:21 + t], za[t])
                zq.append(V(lambda e, t=t: e.tensor_scalar(ZA[:, t, 0:384], ZA[:, t, 0:384], st[:, 20 + t:21 + t], None, MUL), r))
                r = head_rstd(ZB[:, t, 0:256], 1, 256, st[:, 22 + t:23 + t], zb[t])
                zk.append(V(lambda e, t=t: e.tensor_scalar(ZB[:, t, 0:256], ZB[:, t, 0:256], st[:, 22 + t:23 + t], None, MUL), r))
            ctk = {}
            for k in range(5):
                b, o = 4 + k // 2, 256 * (k % 2)
                for t in range(2):
                    src = ZA[:, t, 128 * k:128 * k + 128] if k < 3 else ZB[:, t, 128 * (k - 3):128 * (k - 3) + 128]
                    tk = transp(PS[:, b, o + 128 * t:o + 128 * t + 128], src, (zq if k < 3 else zk)[t],
                                bank[b] if t == 0 and k % 2 == 0 else None)
                ctk[b] = tk
            gn = lambda k: col("mla_q_a_norm_2", k) if k < 3 else col("mla_kv_a_norm_2", k - 3)
            ctt = [d for b in range(4, 7) for d in parts(range(2 * (b - 4), min(2 * (b - 4) + 2, 5)), CTh, CTl, b, ctk[b], gn, fence)]
            ckt = ctt[3:5]
            RP, RQ = sb("RP", [128, 8, 64]), sb("RQ", [128, 8, 64])

            def rope64(z, nh, t, gi, tok):
                gb = GR[:, gi, :].unsqueeze(1).to_broadcast([128, nh, 64])
                x0 = V(lambda e: e.tensor_tensor(z, z, gb, MUL), tok, k_gr)
                cb = tb[:, 0, t, :].unsqueeze(1).to_broadcast([128, nh, 64])
                x1 = V(lambda e: e.tensor_tensor(RP[:, 0:nh, :], z, cb, MUL), x0, k_tb, fence)
                xs = []
                for ax in range(2):
                    for hf in range(2):
                        a, b = 32 * ax + 16 * hf, 32 * ax + 16 * (1 - hf)
                        s_ = tb[:, 1, t, a:a + 16].unsqueeze(1).to_broadcast([128, nh, 16])
                        xs.append(V(lambda e, a=a, b=b, s_=s_: e.tensor_tensor(RQ[:, 0:nh, a:a + 16], z[:, :, b:b + 16], s_, MUL), x0))
                return V(lambda e: e.tensor_tensor(z, RP[:, 0:nh, :], RQ[:, 0:nh, :], ADD), x1, xs)

            kp = []
            for t in range(2):
                r = head_rstd(ZA[:, t, 384:448], 1, 64, st[:, 24 + t:25 + t], za[t])
                a = V(lambda e, t=t: e.tensor_scalar(ZA[:, t, 384:448], ZA[:, t, 384:448], st[:, 24 + t:25 + t], None, MUL), r)
                kp.append(rope64(ZA[:, t, 384:448].rearrange("p (h d) -> p h d", h=1), 1, t, 1, a))
            for t in range(2):
                tk = transp(PS[0:64, 7, 128 * t:128 * t + 128], ZA[:, t, 384:448], kp[t], bank[7] if t == 0 else None)
            kpt = S(lambda e: e.activation(KPT[:, :], PS[0:64, 7, 0:256], ACT.Copy), tk, fence)
            bank[7] = [kpt]

            zc = z_evac((0, 1), ZB, 512, tc_, ctt)
            zm = []
            for t in range(2):
                r = head_rstd(ZB[:, t, :], 4, 128, st[:, 26 + 4 * t:30 + 4 * t], zc[t])
                zm.append(scaled(ZB[:, t, :], 4, 128, st[:, 26 + 4 * t:30 + 4 * t], r))
            ZQ = sb("ZQ", [128, 2, 2, 512])
            zqf = {}

            def put_group(n, pr, cs, per, nkt, k0, off, deps, keep=False):
                tk = nat_mm(cs, per, nkt, 512, (CTh[:, k0:k0 + nkt, :], CTl[:, k0:k0 + nkt, :]), deps, pr, off=off, keep=keep)
                out = []
                for t in range(2):
                    a = S(lambda e, t=t: e.activation(ZQ[:, n % 2, t, :], PS[:, pr[t], :], ACT.Copy), tk, zqf.get(n - 2), fence)
                    bank[pr[t]] = [a]
                    out.append(a)
                return out

            def norm_group(n, nh, d, toks, so):
                out = []
                for t in range(2):
                    r = head_rstd(ZQ[:, n % 2, t, :], nh, d, st[:, so:so + nh], toks[t])
                    out.append(scaled(ZQ[:, n % 2, t, :], nh, d, st[:, so:so + nh], r))
                    so += nh
                return out

            g0 = put_group(0, (2, 3), PLAN["qb0"], 3, 3, 0, 0, ctt[0:3])
            qmt = gain_turn(ZB, zm, lambda j: QMT[:, j:j + 2, :], gq[:, 1:2], (4, 5))
            g1_ = put_group(1, (0, 1), PLAN["qb1"], 3, 3, 0, 0, ctt[0:3])
            n0 = norm_group(0, 4, 128, g0, 34)
            qt0 = gain_turn(ZQ[:, 0, :, :], n0, lambda j: QTn[:, j:j + 2, :], gq[:, 0:1], (6, 7))
            zqf[0] = last("pe")
            n1 = norm_group(1, 4, 128, g1_, 34)
            g2_ = put_group(2, (2, 3), PLAN["qb2"], 3, 3, 0, 0, ctt[0:3])
            qt1 = gain_turn(ZQ[:, 1, :, :], n1, lambda j: QTn[:, 4 + j:6 + j, :], gq[:, 0:1], (4, 5))
            zqf[1] = last("pe")
            n2 = norm_group(2, 8, 64, g2_, 42)
            qp = []
            for t in range(2):
                a = V(lambda e, t=t: e.tensor_scalar(ZQ[:, 0, t, :], ZQ[:, 0, t, :], sc_mla, None, MUL), n2[t])
                qp.append(rope64(ZQ[:, 0, t, :].rearrange("p (h d) -> p h d", h=8), 8, t, 0, a))
            c = PLAN["kvb0"][0]
            g3_ = put_group(3, (0, 1), [c], 2, 2, 3, 0, ckt, keep=True)
            qpt = []
            for h2 in range(4):
                b = 4 + h2
                for j in range(2):
                    for t in range(2):
                        hh = 2 * h2 + j
                        tk = transp(PS[0:64, b, 256 * j + 128 * t:256 * j + 128 * t + 128], ZQ[:, 0, t, 64 * hh:64 * hh + 64], qp[t],
                                    bank[b] if j == 0 and t == 0 else None)
                a = S(lambda e, b=b, h2=h2: e.activation(QTp[:, 2 * h2:2 * h2 + 2, :], PS[0:64, b, :].rearrange("p (a c) -> p a c", a=2), ACT.Copy),
                      tk, fence)
                bank[b] = [a]
                qpt.append(a)
            zqf[2] = last("pe")
            n3 = norm_group(3, 4, 128, g3_, 34)
            g4_ = put_group(4, (2, 3), [c], 2, 2, 3, 1024, ckt)
            kt0 = gain_turn(ZQ[:, 1, :, :], n3, lambda j: KTn[:, j:j + 2, :], col("mla_kn"), (6, 7))
            n4 = norm_group(4, 4, 128, g4_, 34)
            c = PLAN["kvb1"][0]
            vt = []
            for g in range(2):
                pr = ((0, 1), (2, 3))[g]
                tk = nat_mm([c], 2, 2, 512, (CTh[:, 3:5, :], CTl[:, 3:5, :]), ckt, pr, off=1024 * g, keep=g == 0)
                for t in range(2):
                    a = S(lambda e, t=t, g=g, pr=pr: e.activation(VV[:, t, 512 * g:512 * g + 512], PS[:, pr[t], :], ACT.Copy), tk, fence)
                    bank[pr[t]] = [a]
                    vt.append(a)
            kt1 = gain_turn(ZQ[:, 0, :, :], n4, lambda j: KTn[:, 4 + j:6 + j, :], col("mla_kn"), (4, 5))
            heads = []
            for hh in range(8):
                heads.append(([(QTn[:, hh, :], KTn[:, hh, :]), (QTp[:, hh, :], KPT[:, :])],
                              [VV[:, kt, 128 * hh:128 * hh + 128] for kt in range(2)], 128, 4 + 2 * (hh // 4 % 2), 128 * (hh % 4),
                              [qt0, qt1, qpt, kt0, kt1, kpt, vt]))
            for hh in range(4):
                heads.append(([(QMT[:, hh, :], KM[:, 0, hh, :])], [VM[:, 0, kt, 128 * hh:128 * hh + 128] for kt in range(2)],
                              128, 4, 128 * hh, [qmt, kmt[0], vmt[0]]))
            scope.pop()
            inner.close()
            ydeps = run_attention("A2", heads, last(), lambda h0: h0, 4)
            scope.pop()
            mla_last = last()
        with ExitStack() as sc:
            scope.append(sc)
            MN = YG
            KZ = sb("KZ1", [128, 2, 512])
            k_mem = mem_project(1, MN, mla_last)
            mem_kv(1, MN, k_mem, st[:, 16:18], mla_last, KZ, mla_last)
            scope.pop()
        ends = wide_mm(PLAN["out0"], lambda k: (YAh, YAl, k), lambda k: ydeps[k])
        xt = add_residual(ends)
        ends = ffn("ffn2", xt, "norm_ffn_2", 0, ends)
        xt = add_residual(ends)

        with ExitStack() as sc:
            scope.append(sc)
            fence = last()
            tb = sb("tbg", [128, 2, 2, 128])
            GR = sb("GRg", [128, 2, 128])
            k_tb = load("pool", tb[:, :, :, :], A["tab2"][:, 256:768].rearrange("p (c t d) -> p c t d", c=2, t=2), "c_tb", fence)
            k_gr = load("pool", GR[:, :, :], A["rows"][:, 4224:4480].rearrange("p (a d) -> p a d", a=2), "c_gr", fence)
            Z = [sb(f"Zg{i}", [128, 2, 512]) for i in range(4)]
            QT, KT2, QMT = sb("QTg", [128, 8, 256]), sb("KTg", [128, 2, 256]), sb("QMg", [128, 4, 256])
            RP, RQ = sb("RPg", [128, 4, 128]), sb("RQg", [128, 4, 128])
            gq2 = sb("gqg", [128, 2])
            k1 = V(lambda e: e.tensor_scalar(gq2[:, 0:1], col("memq_norm_2", 1), sc_mem, None, MUL), fence)
            k2 = V(lambda e: e.memset(gq2[:, 1:2], sc_mem), fence)
            h = to_features(X, xt, "norm_mix_2", 8, (4, 5, 6, 7), ends)
            rs = row_norm(X, xt, st[:, 2:4])
            pump()

            def rope128(z, nh, t, gi, tok):
                gb = GR[:, gi, :].unsqueeze(1).to_broadcast([128, nh, 128])
                x0 = V(lambda e: e.tensor_tensor(z, z, gb, MUL), tok, k_gr)
                cb = tb[:, 0, t, :].unsqueeze(1).to_broadcast([128, nh, 128])
                x1 = V(lambda e: e.tensor_tensor(RP[:, 0:nh, :], z, cb, MUL), x0, k_tb, fence)
                xs = []
                for ax in range(2):
                    for hf in range(2):
                        a, b = 64 * ax + 32 * hf, 64 * ax + 32 * (1 - hf)
                        s_ = tb[:, 1, t, a:a + 32].unsqueeze(1).to_broadcast([128, nh, 32])
                        xs.append(V(lambda e, a=a, b=b, s_=s_: e.tensor_tensor(RQ[:, 0:nh, a:a + 32], z[:, :, b:b + 32], s_, MUL), x0))
                return V(lambda e: e.tensor_tensor(z, RP[:, 0:nh, :], RQ[:, 0:nh, :], ADD), x1, xs)

            zt = {}
            post = {}
            order = [0, 1, 2, 3]

            def finish_group(g):
                if g < 2:
                    n = []
                    for t in range(2):
                        r = head_rstd(Z[g][:, t, :], 4, 128, st[:, 8 + 4 * t:12 + 4 * t], zt[g][t])
                        a = scaled(Z[g][:, t, :], 4, 128, st[:, 8 + 4 * t:12 + 4 * t], r)
                        n.append(rope128(Z[g][:, t, :].rearrange("p (h d) -> p h d", h=4), 4, t, 0, a))
                    post[g] = gain_turn(Z[g], n, lambda j: QT[:, 4 * g + j:4 * g + j + 2, :], gq2[:, 1:2], (4, 5))
                elif g == 2:
                    n = []
                    for t in range(2):
                        r = head_rstd(Z[2][:, t, 0:256], 2, 128, st[:, 20 + 2 * t:22 + 2 * t], zt[2][t])
                        a = scaled(Z[2][:, t, 0:256], 2, 128, st[:, 20 + 2 * t:22 + 2 * t], r)
                        n.append(rope128(Z[2][:, t, 0:256].rearrange("p (h d) -> p h d", h=2), 2, t, 1, a))
                    post[2] = gain_turn(Z[2], n, lambda j: KT2[:, :, :], 1.0, (6, 7), 2)
                else:
                    n = []
                    for t in range(2):
                        r = head_rstd(Z[3][:, t, :], 4, 128, st[:, 26 + 4 * t:30 + 4 * t], zt[3][t])
                        n.append(scaled(Z[3][:, t, :], 4, 128, st[:, 26 + 4 * t:30 + 4 * t], r))
                    post[3] = gain_turn(Z[3], n, lambda j: QMT[:, j:j + 2, :], gq2[:, 0:1], (4, 5))

            for g in range(4):
                pr = ((0, 1), (2, 3))[g % 2]
                tk = nat_mm(PLAN[f"gqa{g}"], 4, 8, 512, (HTh, HTl), h, pr)
                zt[g] = []
                for t in range(2):
                    a = S(lambda e, t=t, g=g, pr=pr: e.activation(Z[g][:, t, :], PS[:, pr[t], :], ACT.Copy, scale=st[:, 2 + t:3 + t]), tk, rs, fence)
                    bank[pr[t]] = [a]
                    zt[g].append(a)
                if g:
                    finish_group(g - 1)
            finish_group(3)
            heads = []
            for hh in range(4):
                heads.append(([(QMT[:, hh, :], KM[:, 1, hh, :])], [VM[:, 1, kt, 128 * hh:128 * hh + 128] for kt in range(2)],
                              128, 4, 128 * hh, [post[3], kmt[1], vmt[1]]))
            for hh in range(8):
                kv = hh // 4
                heads.append(([(QT[:, hh, :], KT2[:, kv, :])], [Z[2][:, kt, 256 + 128 * kv:384 + 128 * kv] for kt in range(2)],
                              128, 6 - 2 * (hh // 4 % 2), 128 * (hh % 4), [post[0], post[1], post[2], zt[2]]))
            ydeps = run_attention("A3", heads, fence, lambda h0: 8 if h0 == 0 else h0 - 4, 4)
            ends = wide_mm(PLAN["out1"], lambda k: (YAh, YAl, k), lambda k: ydeps[k])
            scope.pop()
        xt = add_residual(ends)
        ends = ffn("ffn3", xt, "norm_ffn_2", 8, ends)
        xt = add_residual(ends)
        outs = [load("sp", A["out"][128 * t:128 * t + 128, :], X[:, t, :], f"c_o{t}", xt[t]) for t in range(2)]
        end = lambda e: None

        Q.count()
        block = top.enter_context(nc.Block())

        @block.sync
        def _(e):
            Q.emit("sp", e, sems)
            for t in range(2):
                e.wait_ge(sems[f"c_o{t}"], outs[t].value)

        @block.gpsimd
        def _(e):
            Q.emit("pool", e, sems)

        @block.scalar
        def _(e):
            Q.emit("act", e, sems)

        @block.vector
        def _(e):
            Q.emit("dve", e, sems)

        @block.tensor
        def _(e):
            Q.emit("pe", e, sems)


def kernel(**inputs):
    import concourse.bacc as bacc
    from concourse.bass_utils import run_bass_kernel_spmd

    a = {k: np.asarray(v) for k, v in inputs.items()}
    PLAN, order = plan()
    tab, tab2 = tables()
    rows = np.concatenate([a["norm_mix_post"][0], a["norm_mix_post"][1], a["norm_ffn_post"][0], a["norm_ffn_post"][1],
                           a["mla_q_norm_2"][0, 128:], a["mla_k_norm_2"][0, 128:], a["gqa_q_norm_2"][0], a["gqa_k_norm_2"][0]])
    arrays = {
        "w": pack(a, order),
        "cols": columns(a),
        "rows": np.ascontiguousarray(np.broadcast_to(rows[None, :], (128, rows.shape[0]))),
        "s5": s5_layout(a),
        "tab": tab,
        "tab2": tab2,
        "x": np.ascontiguousarray(a["x"][0]),
        "mem": np.ascontiguousarray(a["mem_2"][0]),
        "pos": np.ascontiguousarray(a["positions"].reshape(2, 128).T),
    }
    nc = bacc.Bacc("TRN2", target_bir_lowering=False, num_devices=1)
    A = {n: nc.dram_tensor("in_" + n, v.shape, mybir.dt.from_np(v.dtype), kind="ExternalInput").ap() for n, v in arrays.items()}
    A["out"] = nc.dram_tensor("out_x", (256, 1024), mybir.dt.float32, kind="ExternalOutput").ap()
    program(nc, A, PLAN, len(order))
    r = run_bass_kernel_spmd(nc, [{"in_" + n: v for n, v in arrays.items()}], core_ids=[0])
    return np.asarray(r.results[0]["out_x"]).reshape(1, 256, 1024)
```

```python
import numpy as np
import concourse.bass as bass
from concourse import mybir
from contextlib import ExitStack

F = 2816
CH = 2048
NR = 3
NW = 3



def cut(name, lead, k0, nk, cols):
    return ("mat", name, lead, k0, nk, tuple(cols))


def wide(name, lead, nkt):
    return [[cut(name, lead, k, 2, [(0, 1024)])] for k in range(0, nkt, 2)]


def nat(name, lead, cols, nkt=8, per=4):
    return [[cut(name, lead, k, per, cols)] for k in range(0, nkt, per)]


def ffn_chunks(gate, up, uo, down, lead):
    out = []
    for g in range(11):
        for k in (0, 4):
            out.append([("pair", gate, up, lead, k, 4, 256 * g, uo + 256 * g)])
    return out + wide(down, lead, 22)


def plan():
    p = {}
    order = []

    def add(key, chunks):
        p[key] = list(range(len(order), len(order) + len(chunks)))
        order.extend(chunks)

    for key, c in (("u", 1536), ("q", 0), ("k", 512), ("v", 1024)):
        add("ev_" + key, nat("ev_w_in", 0, [(c, 512)]))
    add("glu", nat("s5_w_glu", 0, [(0, 512)], 4))
    add("ev_out", wide("ev_w_out", 0, 8))
    add("ffn0", ffn_chunks("ffn_w_gate", "ffn_w_up", 0, "ffn_w_down", 0))
    for g in range(4):
        add(f"od{g}", nat("od_w_in", 0, [(512 * g, 512)]))
        if g > 1:
            add(f"rg{g - 2}", [[("rg", 2 * g - 4), ("rg", 2 * g - 3)]])
    for i in range(2):
        add(f"mem0{i}", nat("w_mem_kv_2", 0, [(512 * i, 512)]))
    add("od_out", wide("od_w_out", 0, 8))
    add("ffn1", ffn_chunks("ffn_w_gate", "ffn_w_up", 0, "ffn_w_down", 1))
    add("mla_a", nat("mla_w_in_2", 0, [(0, 384), (640, 64)]))
    add("mla_b", nat("mla_w_in_2", 0, [(384, 256)], 8, 8))
    add("mla_c", nat("mla_w_in_2", 0, [(704, 512)]))
    add("mem10", nat("w_mem_kv_2", 1, [(0, 512)]))
    add("qb2", nat("mla_w_q_b_2", 0, [(192 * h + 128, 64) for h in range(8)], 3, 3))
    add("mem11", nat("w_mem_kv_2", 1, [(512, 512)]))
    for g in range(2):
        hs = range(4 * g, 4 * g + 4)
        add(f"qb{g}", nat("mla_w_q_b_2", 0, [(192 * h, 128) for h in hs], 3, 3))
        add(f"kvb{g}", [[cut("mla_w_kv_b_2", 0, 0, 2, [(256 * h + 128 * j, 128) for h in hs]) for j in range(2)]])
    add("out0", wide("w_out_2", 0, 12))
    add("ffn2", ffn_chunks("w_gate_up_2", "w_gate_up_2", F, "w_down_2", 0))
    for g in (3, 2, 0, 1):
        add(f"gqa{g}", nat("gqa_w_in_2", 0, [(512 * g, 512)]))
    add("out1", wide("w_out_2", 1, 12))
    add("ffn3", ffn_chunks("w_gate_up_2", "w_gate_up_2", F, "w_down_2", 1))
    return p, order


def kmat(a, k0, nk, c0, nc_):
    return a[128 * k0:128 * (k0 + nk), c0:c0 + nc_].reshape(nk, 128, nc_).transpose(1, 0, 2)


def pack(inputs, order):
    out = np.zeros((len(order), 128, CH), np.float32)
    for n, pieces in enumerate(order):
        at = 0
        for pc in pieces:
            if pc[0] == "mat":
                _, name, lead, k0, nk, cols = pc
                a = inputs[name][lead]
                w = np.concatenate([kmat(a, k0, nk, c, m) for c, m in cols], axis=2)
            elif pc[0] == "pair":
                _, gate, up, lead, k0, nk, cg, cu = pc
                w = np.concatenate([kmat(inputs[gate][lead], k0, nk, cg, 256),
                                    kmat(inputs[up][lead], k0, nk, cu, 256)], axis=2)
            else:
                w = np.concatenate([kmat(inputs[nm][0][pc[1]], 0, 2, 0, 256) for nm in ("rg_w_r", "rg_w_i")], axis=1)
            w = w.reshape(128, -1)
            out[n, :, at:at + w.shape[1]] = w
            at += w.shape[1]
    return out


COLS = [("norm_mix_pre", 16), ("norm_ffn_pre", 16), ("norm_mix_2", 16), ("norm_ffn_2", 16), ("mem_norm_2", 8),
        ("memq_norm_2", 2), ("memk_norm_2", 2), ("mla_q_a_norm_2", 3), ("mla_kv_a_norm_2", 2),
        ("mla_qn", 1), ("mla_kn", 1), ("rg_conv_w", 32), ("rg_conv_b", 8), ("rg_b_r", 8), ("rg_b_i", 8),
        ("rg_lam", 8), ("s5_d", 4), ("s5_a_re", 16), ("s5_a_im", 16), ("s5_log_dt", 16)]
COL = {}
_n = 0
for _name, _w in COLS:
    COL[_name] = _n
    _n += _w
NCOL = _n


def columns(inputs):
    parts = []
    for name, w in COLS:
        if name in ("mla_qn", "mla_kn"):
            a = inputs["mla_q_norm_2" if name == "mla_qn" else "mla_k_norm_2"][0, :128]
            parts.append(a.reshape(1, 128).T)
        elif name in ("s5_a_re", "s5_a_im"):
            parts.append(inputs[name][0].reshape(16, 128).T)
        elif name == "s5_log_dt":
            parts.append(np.repeat(inputs[name][0].reshape(16, 2), 64, axis=1).T)
        else:
            parts.append(np.ascontiguousarray(inputs[name]).reshape(w, 128).T)
    return np.ascontiguousarray(np.concatenate(parts, axis=1))


def s5_layout(inputs):
    out = []
    for name in ("s5_b_re", "s5_b_im"):
        b = inputs[name][0].reshape(4, 4, 2, 64, 16)
        w = np.zeros((4, 4, 2, 16, 2, 64), np.float32)
        for g in range(2):
            w[:, :, g, :, g, :] = b[:, :, g].transpose(0, 1, 3, 2)
        out.append(w.transpose(1, 2, 3, 0, 4, 5).reshape(128, 512))
    for name in ("s5_c_re", "s5_c_im"):
        c = inputs[name][0].reshape(16, 2, 16, 64)
        out.append(c.transpose(1, 3, 0, 2).reshape(128, 256))
    return np.ascontiguousarray(np.concatenate(out, axis=1))


def rope_tables(dim):
    row = np.repeat(np.arange(4, dtype=np.float32), 64)
    col = np.tile(np.arange(64, dtype=np.float32), 4)
    ax = dim // 2
    inv = (np.float32(10000.0) ** (-np.arange(0, ax, 2, dtype=np.float32) / np.float32(ax))).astype(np.float32)
    cs, sn = [], []
    for pos in (row, col):
        ang = (pos[:, None] * inv).astype(np.float32)
        cs += [np.cos(ang), np.cos(ang)]
        sn += [-np.sin(ang), np.sin(ang)]
    return [np.concatenate(t, axis=1).astype(np.float32).reshape(2, 128, dim).transpose(1, 0, 2).reshape(128, 2 * dim)
            for t in (cs, sn)]


def tables():
    q = np.arange(256)[:, None]
    k = np.arange(256)[None, :]
    d = q - k
    c = ((d >= 0) & (d <= 128)).astype(np.float32) + ((d >= 0) & (d % 4 == 0)) + ((d >= 0) & (d % 16 == 0))
    bias = np.where(c > 0, np.log(np.maximum(c, 1)), -1e30)
    two = lambda a: a.reshape(2, 128, 256).transpose(1, 0, 2).reshape(128, 512)
    inv = (np.float32(500000.0) ** (-(np.arange(8, dtype=np.float32) * np.float32(2.0) / np.float32(16)))).astype(np.float32)
    ident = np.eye(128, dtype=np.float32)
    t0 = [ident, two(bias), np.tile(np.arange(256, dtype=np.float32), (128, 1)), np.tile(inv, (128, 1))]
    a = np.ascontiguousarray(np.concatenate([x.astype(np.float32) for x in t0], axis=1))
    b = np.ascontiguousarray(np.concatenate(rope_tables(64) + rope_tables(128), axis=1))
    return a, b


class Tok:

    def __init__(self, sem, inc):
        self.sem, self.inc, self.value, self.used = sem, inc, None, False


class Later:

    def matmul(self, *a, **k):
        return lambda e: e.matmul(*a, **k)

    def transpose(self, *a, **k):
        return lambda e: e.transpose(*a, **k)

    def activation(self, *a, **k):
        return lambda e: e.activation(*a, **k)

    def tensor_tensor(self, *a, **k):
        return lambda e: e.tensor_tensor(*a, **k)

    def tensor_scalar(self, *a, **k):
        return lambda e: e.tensor_scalar(*a, **k)

    def scalar_tensor_tensor(self, *a, **k):
        return lambda e: e.scalar_tensor_tensor(*a, **k)

    def tensor_copy(self, *a, **k):
        return lambda e: e.tensor_copy(*a, **k)

    def tensor_reduce(self, *a, **k):
        return lambda e: e.tensor_reduce(*a, **k)

    def tensor_tensor_scan(self, *a, **k):
        return lambda e: e.tensor_tensor_scan(*a, **k)

    def tensor_tensor_reduce(self, *a, **k):
        return lambda e: e.tensor_tensor_reduce(*a, **k)

    def tensor_single_scalar(self, *a, **k):
        return lambda e: e.tensor_single_scalar(*a, **k)

    def reciprocal(self, *a, **k):
        return lambda e: e.reciprocal(*a, **k)

    def memset(self, *a, **k):
        return lambda e: e.memset(*a, **k)

    def dma_start(self, *a, **k):
        return lambda e: e.dma_start(*a, **k)


LATER = Later()


def flat(deps):
    out = []
    for d in deps:
        out += flat(d) if isinstance(d, (list, tuple)) else [] if d is None else [d]
    return out


class Queues:

    def __init__(self):
        self.q = {}

    def op(self, eng, fn, *deps):
        t = Tok(eng, 1)
        self.put(eng, fn, t, deps)
        return t

    def dma(self, eng, out, in_, sem, *deps):
        t = Tok(sem, 16)
        t.used = True
        self.put(eng, lambda e: e.dma_start(out, in_), t, deps)
        return t

    def put(self, eng, fn, t, deps):
        deps = flat(deps)
        for d in deps:
            d.used = True
        self.q.setdefault(eng, []).append((fn(LATER), t, deps))

    def count(self):
        total = {}
        for eng in self.q:
            for _, t, _ in self.q[eng]:
                if t.used:
                    total[t.sem] = total.get(t.sem, 0) + t.inc
                    t.value = total[t.sem]

    def emit(self, eng, e, sems):
        seen = {}
        for fn, t, deps in self.q.get(eng, []):
            need = {}
            for d in deps:
                need[d.sem] = max(need.get(d.sem, 0), d.value)
            for s in sorted(need, key=str):
                if seen.get(s, 0) < need[s]:
                    e.wait_ge(sems[s], need[s])
                    seen[s] = need[s]
            ins = fn(e)
            if t.used:
                ins.then_inc(sems[t.sem], t.inc)


def program(nc, A, PLAN, NCH):
    f32, f32r, i32 = mybir.dt.float32, mybir.dt.float32r, mybir.dt.int32
    ALU, ACT, AX = mybir.AluOpType, mybir.ActivationFunctionType, mybir.AxisListType
    MUL, ADD, SUB = ALU.mult, ALU.add, ALU.subtract
    Q = Queues()
    PE = lambda fn, *d: Q.op("pe", fn, *d)
    V = lambda fn, *d: Q.op("dve", fn, *d)
    S = lambda fn, *d: Q.op("act", fn, *d)
    G = lambda fn, *d: Q.op("pool", fn, *d)
    TWO_PI = 6.283185307179586

    top = ExitStack()
    with top:
        scope = [top]

        def sb(name, shape, dt=f32):
            return scope[-1].enter_context(nc.sbuf_tensor(name, shape, dt))

        def sem(name):
            return top.enter_context(nc.semaphore(name))

        sems = {k: sem("s_" + k) for k in ("pe", "dve", "act", "pool")}
        for r in range(NR):
            sems[f"w{r}"] = sem(f"s_w{r}")

        def load(eng, out, in_, name, *deps):
            if name not in sems:
                sems[name] = sem("s_" + name)
            return Q.dma(eng, out, in_, name, *deps)

        X = sb("X", [128, 2, 1024])
        HTh, HTl = sb("HTh", [128, 8, 256], f32r), sb("HTl", [128, 8, 256], f32r)
        YAh, YAl = sb("YAh", [128, 12, 256], f32r), sb("YAl", [128, 12, 256], f32r)
        RAW = sb("RAW", [128, NR, CH])
        WH, WL = sb("WH", [128, NW, CH], f32r), sb("WL", [128, NW, CH], f32r)
        BC = sb("BC", [128, 1024])
        ident = sb("ident", [128, 128])
        cst = sb("cst", [128, NCOL])
        st = sb("st", [128, 64])
        mh = sb("mh", [128, 16])
        YG = sb("YG", [128, 2, 1024])
        PS = top.enter_context(nc.psum_tensor("PS", [128, 8, 512], f32))
        bank = [[] for _ in range(8)]

        def col(name, i=0, n=1):
            return cst[:, COL[name] + i:COL[name] + i + n]

        split_tok, used_tok, raw_free, dma_tok = {}, {}, {}, {}
        nxt = {"dma": 0, "split": 0}

        def stream_load():
            c = nxt["dma"]
            if c >= NCH:
                return
            nxt["dma"] = c + 1
            dma_tok[c] = Q.dma("sp", RAW[:, c % NR, :], A["w"][c], f"w{c % NR}", raw_free.get(c - NR))

        def stream_split():
            c = nxt["split"]
            nxt["split"] = c + 1
            s, r = c % NW, c % NR
            hi = S(lambda e: e.activation(WH[:, s, :], RAW[:, r, :], ACT.Copy), dma_tok[c], used_tok.get(c - NW))
            lo = V(lambda e: e.tensor_tensor(WL[:, s, :], RAW[:, r, :], WH[:, s, :].bitcast(f32), SUB),
                   hi, dma_tok[c], used_tok.get(c - NW))
            split_tok[c] = lo
            raw_free[c] = [hi, lo]
            stream_load()

        def pump():
            while nxt["split"] < NCH and (nxt["split"] < NW or (nxt["split"] - NW) in used_tok):
                stream_split()

        def chunk(c):
            while nxt["split"] <= c:
                stream_split()
            return c % NW

        def mm(out, a, b, start, stop, *deps):
            return PE(lambda e: e.matmul(out, a, b, start=start, stop=stop), *deps)

        def mm3(out, ah, al, bh, bl, start, stop, *deps):
            mm(out, ah, bh, start, False, *deps)
            mm(out, ah, bl, False, False)
            return mm(out, al, bh, False, stop)

        def nat_mm(cs, per, nkt, N, src, srcdeps, banks, off=0, keep=False, hook=None):
            hi, lo = src
            k = 0
            for ci, c in enumerate(cs):
                s = chunk(c)
                for kk in range(per):
                    if k == nkt:
                        break
                    for t in range(2):
                        w = slice(off + kk * N, off + (kk + 1) * N)
                        tk = mm3(PS[:, banks[t], 0:N], hi[:, k, 128 * t:128 * t + 128], lo[:, k, 128 * t:128 * t + 128],
                                 WH[:, s, w], WL[:, s, w], k == 0, k == nkt - 1,
                                 split_tok[c], srcdeps[k], bank[banks[t]] if k == 0 else None)
                    k += 1
                if not keep:
                    used_tok[c] = tk
                    pump()
                if hook:
                    hook()
            return tk

        def wide_mm(cs, src_of, dep_of):
            ends = [None, None]
            n = len(cs)
            for ci, c in enumerate(cs):
                s = chunk(c)
                for t in range(2):
                    for kk in range(2):
                        k = 2 * ci + kk
                        hi, lo, j = src_of(k)
                        for half in range(2):
                            w = slice(kk * 1024 + half * 512, kk * 1024 + half * 512 + 512)
                            ends[t] = mm3(PS[:, 2 * t + half, :], hi[:, j, 128 * t:128 * t + 128],
                                          lo[:, j, 128 * t:128 * t + 128], WH[:, s, w], WL[:, s, w],
                                          k == 0, k == 2 * n - 1, split_tok[c], dep_of(k),
                                          bank[2 * t + half] if k == 0 else None)
                used_tok[c] = ends[1]
                if ci < n - 1:
                    pump()
            return ends

        def transp(out, in_, *deps):
            p = in_.shape[0]
            return PE(lambda e: e.transpose(out, in_, ident[0:p, 0:p]), *deps)

        def turn_rows(src, srctok, banks, free=None):
            T = [None] * 8
            for t in range(2):
                for k in range(8):
                    b, o = banks[k // 2], (k % 2) * 256 + t * 128
                    T[k] = transp(PS[:, b, o:o + 128], src[:, t, 128 * k:128 * k + 128], srctok[t], bank[b] if t == 0 else None)
            return T

        def split_rows(T, gain, gi, banks, free):
            return [d for j in range(4) for d in parts((2 * j, 2 * j + 1), HTh, HTl, banks[j], T[2 * j + 1],
                                                       lambda k: col(gain, gi + k), free)]

        def to_features(src, srctok, gain, gi, banks, free):
            return split_rows(turn_rows(src, srctok, banks), gain, gi, banks, free)

        def parts(ks, dh, dl, b, tk, gain, free):
            for i, k in enumerate(ks):
                hi = S(lambda e: e.activation(dh[:, k, :], PS[:, b, 256 * i:256 * i + 256], ACT.Copy, scale=gain(k)), tk, free)
            out = []
            for i, k in enumerate(ks):
                out.append(V(lambda e: e.scalar_tensor_tensor(dl[:, k, :], PS[:, b, 256 * i:256 * i + 256], gain(k),
                                                              dh[:, k, :].bitcast(f32), MUL, SUB), hi, free))
            bank[b] = out[-1:]
            return out

        def rstd(out, ss, n, eps_toks, free=None):
            w = out.shape[1]
            a = V(lambda e: e.tensor_scalar(out, ss, 1.0 / n, 1e-6, MUL, ADD), eps_toks, free)
            return G(lambda e: e.tensor_tensor(out, out, mh[:, 0:w], ALU.pow), a, k_mh)

        def row_norm(src, srctok, out):
            a = [square(lambda e: e.activation(JK[:, :], src[:, t, :], ACT.Square, accum_out=out[:, t:t + 1]), srctok[t])
                 for t in range(2)]
            return rstd(out, out, 1024, a)

        JK = sb("JK", [128, 1024])
        jk = [None]

        def square(fn, *deps):
            jk[0] = S(fn, jk[0], *deps)
            return jk[0]

        def residual(ends, scale, gain_tok):
            toks = []
            for t in range(2):
                sq, yg = [], []
                for hf in range(2):
                    y = PS[:, 2 * t + hf, :]
                    cs = slice(512 * hf, 512 * hf + 512)
                    sq.append(square(lambda e: e.activation(JK[:, cs], y, ACT.Square, scale=scale,
                                                       accum_out=st[:, 60 + 2 * t + hf:61 + 2 * t + hf]), ends[t]))
                    yg.append(V(lambda e: e.tensor_tensor(YG[:, t, cs], y, BC[:, cs], MUL), sq[-1], gain_tok))
                    bank[2 * t + hf] = yg[-1:]
                s0 = V(lambda e: e.tensor_tensor(st[:, t:t + 1], st[:, 60 + 2 * t:61 + 2 * t], st[:, 61 + 2 * t:62 + 2 * t], ADD), sq)
                r = rstd(st[:, t:t + 1], st[:, t:t + 1], 1024, s0)
                if scale != 1.0:
                    r = V(lambda e: e.tensor_scalar(st[:, t:t + 1], st[:, t:t + 1], scale, None, MUL), r)
                toks.append((r, yg))
            out = []
            for t in range(2):
                out.append(V(lambda e, t=t: e.scalar_tensor_tensor(X[:, t, :], YG[:, t, :], st[:, t:t + 1], X[:, t, :], MUL, ADD),
                             toks[t][0], toks[t][1]))
            return out

        def add_residual(ends):
            out = []
            for t in range(2):
                y = PS[:, 2 * t:2 * t + 2, :].rearrange("p a b -> p (a b)")
                a = V(lambda e, t=t, y=y: e.tensor_tensor(X[:, t, :], y, X[:, t, :], ADD), ends[t])
                bank[2 * t] = bank[2 * t + 1] = [a]
                out.append(a)
            return out

        def last(*names):
            return [Q.q[n][-1][1] for n in (names or ("pe", "dve", "act", "pool")) if Q.q.get(n)]

        def ffn(key, xtok, gain, gi, first_free):
            cs = PLAN[key]
            with ExitStack() as sc:
                scope.append(sc)
                fence = last()
                YBh, YBl = sb(key + "YBh", [128, 10, 256], f32r), sb(key + "YBl", [128, 10, 256], f32r)
                TH, SG, AN = (sb(key + n, [128, 2, 2, 256]) for n in ("TH", "SG", "AN"))
                scope.pop()
                ydst = lambda j: (YAh, YAl, j) if j < 12 else (YBh, YBl, j - 12)
                h = to_features(X, xtok, gain, gi, (4, 5, 6, 7), first_free)
                rs = row_norm(X, xtok, st[:, 2:4])
                rs2 = V(lambda e: e.tensor_tensor(st[:, 6:8], st[:, 2:4], st[:, 2:4], MUL), rs)
                rsh = V(lambda e: e.tensor_scalar(st[:, 4:6], st[:, 2:4], 0.5, None, MUL), rs)
                pump()
                pairs = [(0, 1), (2, 3), (6, 7)]
                done = {}
                free = {"TH": {}, "AN": {}}

                def act(g, tk):
                    p = pairs[(g + 1) % 3]
                    for t in range(2):
                        gg, uu = PS[:, p[t], 0:256], PS[:, p[t], 256:512]
                        b = g % 2
                        th = S(lambda e, t=t, b=b, gg=gg: e.activation(TH[:, b, t, :], gg, ACT.Tanh, scale=st[:, 4 + t:5 + t]),
                               tk, rsh, free["TH"].get((g - 2, t)), fence)
                        sg = V(lambda e, t=t, b=b, gg=gg: e.scalar_tensor_tensor(SG[:, b, t, :], TH[:, b, t, :], 1.0, gg, ADD, MUL),
                               th, fence)
                        free["TH"][(g, t)] = sg
                        an = V(lambda e, t=t, b=b, uu=uu: e.scalar_tensor_tensor(AN[:, b, t, :], uu, st[:, 6 + t:7 + t],
                                                                                 SG[:, b, t, :], MUL, MUL),
                               sg, rs2, free["AN"].get(g - 2))
                        bank[p[t]] = [an]
                        done[(g, t)] = an

                ydep = {}

                def fold(g):
                    b = 4 + g % 2
                    for t in range(2):
                        for j in range(2):
                            tk = transp(PS[:, b, j * 256 + t * 128:j * 256 + t * 128 + 128],
                                        AN[:, g % 2, t, 128 * j:128 * j + 128], done[(g, t)], bank[b] if t == 0 and j == 0 else None)
                    free["AN"][g] = tk
                    hi, lo, j = ydst(2 * g)
                    src = PS[:, b, :].rearrange("p (a c) -> p a c", a=2)
                    a = S(lambda e: e.activation(hi[:, j:j + 2, :], src, ACT.Copy, scale=0.5), tk, fence)
                    l = V(lambda e: e.scalar_tensor_tensor(lo[:, j:j + 2, :], src, 0.5, hi[:, j:j + 2, :].bitcast(f32), MUL, SUB), a, fence)
                    bank[b] = [a, l]
                    ydep[2 * g] = ydep[2 * g + 1] = l

                for g in range(11):
                    p = pairs[(g + 1) % 3]
                    tk = nat_mm(cs[2 * g:2 * g + 2], 4, 8, 512, (HTh, HTl), h, p)
                    if g >= 1:
                        fold(g - 1)
                    act(g, tk)
                box = {}

                def dep_of(k):
                    return ydep[k]

                ends = [None, None]
                dcs = cs[22:]
                n = len(dcs)
                for ci, c in enumerate(dcs):
                    s = chunk(c)
                    for t in range(2):
                        for kk in range(2):
                            k = 2 * ci + kk
                            hi, lo, j = ydst(k)
                            for half in range(2):
                                w = slice(kk * 1024 + half * 512, kk * 1024 + half * 512 + 512)
                                ends[t] = mm3(PS[:, 2 * t + half, :], hi[:, j, 128 * t:128 * t + 128],
                                              lo[:, j, 128 * t:128 * t + 128], WH[:, s, w], WL[:, s, w],
                                              k == 0, k == 2 * n - 1, split_tok[c], dep_of(k),
                                              bank[2 * t + half] if k == 0 else None)
                    used_tok[c] = ends[1]
                    if ci == 0:
                        fold(10)
                    if ci < n - 1:
                        pump()
                return ends

        def run_attention(nm, heads, free, yout, per_out, mask=None, fill=None, sbanks=(0, 1), tbanks=(2, 3), bufs=None, yfree=None):
            nH = len(heads)
            P, SM, Y, PT = bufs or (None,) * 4
            P = sb(nm + "P", [128, 2, 2, 256]) if P is None else P
            PT = sb(nm + "PT", [128, 2, 2, 256]) if PT is None else PT
            M, den = sb(nm + "M", [128, nH, 2]), sb(nm + "den", [128, 2, nH])
            dv = heads[0][2]
            wd = per_out * dv
            Y = sb(nm + "Y", [128, 2, wd]) if Y is None else Y
            ex, pvt, pt_ready, turned, ydeps, ytr = {}, {}, {}, {}, {}, [None]
            nk = lambda t: t + 1 if mask else 2
            sdone = {}

            def products(h):
                parts_, _, _, _, deps = heads[h]
                b = sbanks[h % 2]
                for t in range(2):
                    for i, (q, k) in enumerate(parts_):
                        tk = mm(PS[:, b, 256 * t:256 * t + 128 * nk(t)], q[:, 128 * t:128 * t + 128], k[:, 0:128 * nk(t)],
                                i == 0, i == len(parts_) - 1, deps, bank[b] if t == 0 and i == 0 else None)
                sdone[h] = tk

            def scores(h):
                b = sbanks[h % 2]
                tk = sdone[h]
                src = PS[:, b, :].rearrange("p (t k) -> p t k", t=2)
                ex[h] = []
                if mask:
                    for t in range(2):
                        n = 128 * nk(t)
                        m = V(lambda e: e.tensor_tensor_reduce(out=SM[:, h % 2, t, 0:n], in0=src[:, t, 0:n], in1=mask[0][:, t, 0:n],
                                                               scale=-1.0, scalar=3e38, op0=ADD, op1=ALU.min,
                                                               accum_out=M[:, h, t:t + 1]),
                              tk, ex.get(h - 2), mask[1], free)
                        ex[h].append(S(lambda e: e.activation(P[:, h % 2, t, 0:n], SM[:, h % 2, t, 0:n], ACT.Exp,
                                                              bias=M[:, h, t:t + 1], scale=-1.0, accum_out=den[:, t, h:h + 1]),
                                       m, turned.get(h - 2), free))
                    bank[b] = [m]
                else:
                    m = V(lambda e: e.tensor_reduce(M[:, h, :], src, AX.X, ALU.max, negate=True), tk)
                    for t in range(2):
                        ex[h].append(S(lambda e: e.activation(P[:, h % 2, t, :], src[:, t, :], ACT.Exp, bias=M[:, h, t:t + 1],
                                                              accum_out=den[:, t, h:h + 1]), m, turned.get(h - 2), free))
                    bank[b] = ex[h][-1:]

            def turn(h):
                b = tbanks[h % 2]
                for t in range(2):
                    for kt in range(nk(t)):
                        tk = transp(PS[:, b, kt * 256 + t * 128:kt * 256 + t * 128 + 128],
                                    P[:, h % 2, t, 128 * kt:128 * kt + 128], ex[h][t],
                                    bank[b] if t == 0 and kt == 0 else None)
                turned[h] = tk
                if mask:
                    dst, src = PT[:, h % 2, :, :].rearrange("p t k -> p (t k)"), PS[:, b, :]
                    cs = [(dst[:, 0:256], src[:, 0:256]), (dst[:, 384:512], src[:, 384:512])]
                else:
                    cs = [(PT[:, h % 2, :, :], PS[:, b, :].rearrange("p (t k) -> p t k", t=2))]
                for dst, src in cs:
                    if h % 2 or mask:
                        c = S(lambda e: e.activation(dst, src, ACT.Copy), tk, pvt.get(h - 2), free)
                    else:
                        c = V(lambda e: e.tensor_copy(dst, src), tk, pvt.get(h - 2), free)
                bank[b] = [c]
                pt_ready[h] = c

            def pv(h):
                _, v, dv, out, deps = heads[h]
                for t in range(2):
                    b, o = out[t]
                    for kt in range(nk(t)):
                        tk = mm(PS[:, b, o:o + dv], PT[:, h % 2, kt, 128 * t:128 * t + 128], v[kt],
                                kt == 0, kt == nk(t) - 1, pt_ready[h], deps, bank[b] if kt == 0 and h % per_out == 0 else None)
                pvt[h] = tk

            def finish(h0):
                hs = slice(h0, h0 + per_out)
                r = V(lambda e: e.reciprocal(den[:, :, hs], den[:, :, hs]), [ex[h] for h in range(h0, h0 + per_out)])
                ys = []
                for t in range(2):
                    b, o = heads[h0][3][t]
                    ys.append(V(lambda e: e.tensor_tensor(Y[:, t, :].rearrange("p (h d) -> p h d", d=dv),
                                                          PS[:, b, o:o + wd].rearrange("p (h d) -> p h d", d=dv),
                                                          den[:, t, hs].unsqueeze(2).to_broadcast([128, per_out, dv]), MUL),
                                r, pvt[h0 + per_out - 1], ytr[0], free))
                    bank[b] = [ys[-1]]
                for jp in range(wd // 256):
                    b = tbanks[jp]
                    for j in range(2):
                        for t in range(2):
                            tk = transp(PS[:, b, j * 256 + t * 128:j * 256 + t * 128 + 128],
                                        Y[:, t, 128 * (2 * jp + j):128 * (2 * jp + j) + 128], ys[t],
                                        bank[b] if j == 0 and t == 0 else None)
                    ytr[0] = tk
                    i0 = yout(h0) + 2 * jp
                    src = PS[:, b, :].rearrange("p (a c) -> p a c", a=2)
                    hi = S(lambda e: e.activation(YAh[:, i0:i0 + 2, :], src, ACT.Copy), tk, yfree)
                    lo = V(lambda e: e.tensor_tensor(YAl[:, i0:i0 + 2, :], src, YAh[:, i0:i0 + 2, :].bitcast(f32), SUB), hi)
                    bank[b] = [hi, lo]
                    ydeps[i0] = ydeps[i0 + 1] = lo

            for h in range(nH + 2):
                if h < nH:
                    products(h)
                    if not mask:
                        scores(h)
                if fill and mask:
                    fill(h)
                    if h < nH:
                        scores(h)
                if 0 <= h - 1 < nH:
                    turn(h - 1)
                if fill and not mask:
                    fill(h)
                if 0 <= h - 2 < nH:
                    pv(h - 2)
                    if (h - 2) % per_out == per_out - 1:
                        finish(h - 2 - per_out + 1)
            return ydeps

        def head_rstd(z, nh, d, out, ztok):
            if nh <= 4:
                b = [square(lambda e: e.activation(JK[:, d * i:d * i + d], z[:, d * i:d * i + d], ACT.Square, accum_out=out[:, i:i + 1]), ztok)
                     for i in range(nh)]
                return rstd(out, out, d, b)
            j = JK[:, 0:nh * d]
            a = square(lambda e: e.activation(j, z, ACT.Square), ztok)
            b = V(lambda e: e.tensor_reduce(out, j.rearrange("p (h d) -> p h d", d=d), AX.X, ADD), a)
            jk[0] = b
            return rstd(out, out, d, b)

        def scaled(z, nh, d, r, *toks):
            zv = z.rearrange("p (h d) -> p h d", d=d)
            return V(lambda e: e.tensor_tensor(zv, zv, r.unsqueeze(2).to_broadcast([128, nh, d]), MUL), *toks)

        k_c = load("sp", cst[:, :], A["cols"][:, :], "c_c")
        k_id = load("sp", ident[:, :], A["tab"][:, 0:128], "c_id")
        k_x = [load("sp", X[:, t, :], A["x"][128 * t:128 * t + 128, :], f"c_x{t}") for t in range(2)]
        k_mh = G(lambda e: e.memset(mh[:, :], -0.5))

        def rope_table(dst, tb, gr, d, *deps):
            q = d // 4
            out = []
            for t in range(2):
                out.append(V(lambda e: e.tensor_tensor(dst[:, 0, t, :], tb[:, 0, t, :], gr, MUL), *deps))
                v = lambda a: a.rearrange("p (a f c) -> p a f c", a=2, f=2)
                for f in range(2):
                    out.append(V(lambda e: e.tensor_tensor(v(dst[:, 1, t, :])[:, :, f, :], v(tb[:, 1, t, :])[:, :, f, :],
                                                           v(gr)[:, :, 1 - f, :], MUL), *deps))
            return out

        def rope(z, nh, d, t, tg, RP, RQ, r, tok, *deps):
            zv = z.rearrange("p (h d) -> p h d", d=d)
            cb = tg[:, 0, t, :].unsqueeze(1).to_broadcast([128, nh, d])
            x = [V(lambda e: e.tensor_tensor(RP[:, 0:nh, :], zv, cb, MUL), tok, *deps)]
            q = d // 4
            for ax in range(2):
                for f in range(2):
                    a, b = 2 * q * ax + q * f, 2 * q * ax + q * (1 - f)
                    s_ = tg[:, 1, t, a:a + q].unsqueeze(1).to_broadcast([128, nh, q])
                    x.append(V(lambda e: e.tensor_tensor(RQ[:, 0:nh, a:a + q], zv[:, :, b:b + q], s_, MUL), *deps))
            y = V(lambda e: e.tensor_tensor(zv, RP[:, 0:nh, :], RQ[:, 0:nh, :], ADD), x)
            return V(lambda e: e.tensor_tensor(zv, zv, r[0].unsqueeze(2).to_broadcast([128, nh, d]), MUL), y, r[1])

        def gain_row(i, *deps):
            return load("sp" if i == 0 else "pool", BC[:, :], A["rows"][:, 1024 * i:1024 * i + 1024], "c_bc" if i else "c_b0", *deps)

        with ExitStack() as sc:
            scope.append(sc)
            cbias = sb("cbias", [128, 2, 256])
            tt = sb("tt", [128, 256])
            inv = sb("inv", [128, 8])
            uT = sb("uT", [128, 4, 256])
            Qn, Kn, Vn = sb("Qn", [128, 2, 512]), sb("Kn", [128, 2, 512]), sb("Vn", [128, 2, 512])
            QT, KT = sb("QT", [128, 4, 256]), sb("KT", [128, 4, 256])
            yq = sb("yq", [128, 4, 256])
            s5scope = sc.enter_context(ExitStack())
            scope.append(s5scope)
            BB = sb("BB", [128, 2, 4, 128])
            CC = sb("CC", [128, 2, 16, 16])
            pos = sb("pos", [128, 2], i32)
            k_p = load("sp", pos[:, :], A["pos"][:, :], "c_p")
            k_i = load("sp", inv[:, :], A["tab"][:, 896:904], "c_i")
            for _ in range(NR):
                stream_load()
            k_t = load("sp", tt[:, :], A["tab"][:, 640:896], "c_t")
            k_B = load("sp", BB[:, :, :, :], A["s5"][:, 0:1024].rearrange("p (r q s) -> p r q s", r=2, q=4), "c_B")
            k_C = load("sp", CC[:, :, :, :], A["s5"][:, 1024:1536].rearrange("p (r j c) -> p r j c", r=2, j=16), "c_C")
            k_m = load("sp", cbias[:, :, :], A["tab"][:, 128:640].rearrange("p (t k) -> p t k", t=2), "c_m")
            k_bc = gain_row(0)

            S(lambda e: e.activation(st[:, 62:64], mh[:, 0:2], ACT.Copy), k_mh)
            T = turn_rows(X, [[k, k_id] for k in k_x], (4, 5, 6, 7))
            gain = lambda k: col("norm_mix_pre", k)
            h = parts((0, 1), HTh, HTl, 4, T[1], gain, k_c)
            stream_split()
            for j in range(1, 4):
                h += parts((2 * j, 2 * j + 1), HTh, HTl, 4 + j, T[2 * j + 1], gain, k_c)
            pump()
            rs = row_norm(X, k_x, st[:, 2:4])
            s5 = sb("s5", [128, 16, 16])
            p = lambda i: s5[:, i, :]
            DT, R, TH_, PH, SN, CS, N1, N2, DEN, FR, FI = (p(i) for i in range(11))
            d1 = S(lambda e: e.activation(DT, col("s5_log_dt", 0, 16), ACT.Exp), k_c)
            d2 = V(lambda e: e.tensor_tensor(R, col("s5_a_re", 0, 16), DT, MUL), d1)
            d3 = S(lambda e: e.activation(R, R, ACT.Exp), d2)
            d4 = V(lambda e: e.tensor_tensor(TH_, col("s5_a_im", 0, 16), DT, MUL), d1)
            MAGIC = 12582912.0
            C1, C2 = 6.28125, float(np.float32(0.0019350051879882812))
            C3 = TWO_PI - C1 - C2

            def reduce_2pi(x, n, *deps):
                a = V(lambda e: e.tensor_scalar(n, x, 1.0 / TWO_PI, MAGIC, MUL, ADD), *deps)
                a = V(lambda e: e.tensor_scalar(n, n, MAGIC, None, SUB), a)
                for cc in (C1, C2, C3):
                    a = V(lambda e, cc=cc: e.scalar_tensor_tensor(x, n, -cc, x, MUL, ADD), a)
                return V(lambda e: e.tensor_scalar(x, x, 3.1415925, -3.1415925, ALU.min, ALU.max), a)

            d5 = reduce_2pi(TH_, N1, d4)
            d6 = V(lambda e: e.tensor_scalar(PH, TH_, 1.0 / TWO_PI, None, MUL), d5)
            ang = sb("ang", [128, 2, 8])
            angn = sb("angn", [128, 2, 8])
            rc, rsn = sb("rc", [128, 2, 2, 8]), sb("rsn", [128, 2, 2, 8])
            posf = sb("posf", [128, 2])
            a1 = V(lambda e: e.tensor_copy(posf[:, :], pos[:, :]), k_p)
            for t in range(2):
                a2 = V(lambda e, t=t: e.tensor_scalar(ang[:, t, :], inv[:, :], posf[:, t:t + 1], None, MUL), a1, k_i)
            a3 = reduce_2pi(ang[:, :, :], angn[:, :, :], a2)
            a4 = S(lambda e: e.activation(angn[:, :, :], ang[:, :, :], ACT.Abs), a3)
            d7 = S(lambda e: e.activation(N1, TH_, ACT.Abs), d5)
            a7 = V(lambda e: e.tensor_scalar(angn[:, :, :], angn[:, :, :], -1.0, TWO_PI / 4, MUL, ADD), a4)
            d8 = V(lambda e: e.tensor_scalar(N1, N1, -1.0, TWO_PI / 4, MUL, ADD), d7)
            for hh in range(2):
                a5 = S(lambda e, hh=hh: e.activation(rsn[:, :, hh, :], ang[:, :, :], ACT.Sin), a3)
                a6 = S(lambda e, hh=hh: e.activation(rc[:, :, hh, :], angn[:, :, :], ACT.Sin), a7)
            k_rope = [a5, a6]
            d9 = S(lambda e: e.activation(SN, TH_, ACT.Sin), d5)
            d10 = S(lambda e: e.activation(CS, N1, ACT.Sin), d8)
            AR, AI = col("s5_a_re", 0, 16), col("s5_a_im", 0, 16)
            e1 = V(lambda e: e.tensor_tensor(SN, SN, R, MUL), d9, d3)
            e2 = V(lambda e: e.tensor_tensor(CS, CS, R, MUL), d10, d3)
            e3 = V(lambda e: e.tensor_scalar(CS, CS, -1.0, None, ADD), e2)
            e4 = V(lambda e: e.tensor_tensor(N1, AR, AR, MUL), e3)
            e5 = V(lambda e: e.tensor_tensor(N2, AI, AI, MUL))
            e6 = V(lambda e: e.tensor_tensor(DEN, N1, N2, ADD), e4, e5)
            e7 = V(lambda e: e.reciprocal(DEN, DEN), e6)
            e8 = V(lambda e: e.tensor_tensor(N1, CS, AR, MUL), e6, e3)
            e9 = V(lambda e: e.tensor_tensor(N2, SN, AI, MUL), e6, e1)
            e10 = V(lambda e: e.tensor_tensor(FR, N1, N2, ADD), e8, e9)
            e11 = V(lambda e: e.tensor_tensor(FR, FR, DEN, MUL), e10, e7)
            e12 = V(lambda e: e.tensor_tensor(N1, SN, AR, MUL), e10)
            e13 = V(lambda e: e.tensor_tensor(N2, CS, AI, MUL), e10)
            e14 = V(lambda e: e.tensor_tensor(FI, N1, N2, SUB), e12, e13)
            k_f = V(lambda e: e.tensor_tensor(FI, FI, DEN, MUL), e14, e11)
            CF = sb("CF", [128, 3, 16, 16])
            CT = sb("CT", [128, 16, 16])
            fr = FR.unsqueeze(2).to_broadcast([128, 16, 16])
            fi = FI.unsqueeze(2).to_broadcast([128, 16, 16])
            c1 = V(lambda e: e.tensor_tensor(CF[:, 0, :, :], CC[:, 0, :, :], fr, MUL), k_f, k_C)
            c2 = V(lambda e: e.tensor_tensor(CT[:, :, :], CC[:, 1, :, :], fi, MUL), k_f)
            c3 = V(lambda e: e.tensor_tensor(CF[:, 0, :, :], CF[:, 0, :, :], CT[:, :, :], SUB), c1, c2)
            c3b = V(lambda e: e.tensor_scalar(CF[:, 1, :, :], CF[:, 0, :, :], -1.0, None, MUL), c3)
            c4 = V(lambda e: e.tensor_tensor(CF[:, 2, :, :], CC[:, 0, :, :], fi, MUL), c3)
            c5 = V(lambda e: e.tensor_tensor(CT[:, :, :], CC[:, 1, :, :], fr, MUL), c3)
            c6 = V(lambda e: e.tensor_tensor(CF[:, 2, :, :], CF[:, 2, :, :], CT[:, :, :], ADD), c4, c5)
            k_cf = V(lambda e: e.tensor_scalar(CF[:, 2, :, :], CF[:, 2, :, :], -1.0, None, MUL), c6)
            CP = sb("CP", [128, 3, 4, 128])

            def evac(banks, dst, tk):
                out = []
                for t in range(2):
                    a = S(lambda e, t=t: e.activation(dst[:, t, :], PS[:, banks[t], :], ACT.Copy, scale=st[:, 2 + t:3 + t]), tk, rs)
                    bank[banks[t]] = [a]
                    out.append(a)
                return out

            def turn_pairs(src, toks, dst, bks, scale=1.0):
                out = []
                for jp in range(2):
                    b = bks[jp]
                    for j in range(2):
                        for t in range(2):
                            tk = transp(PS[:, b, j * 256 + t * 128:j * 256 + t * 128 + 128],
                                        src[:, t, 128 * (2 * jp + j):128 * (2 * jp + j) + 128], toks[t],
                                        bank[b] if j == 0 and t == 0 else None)
                    a = S(lambda e, b=b, jp=jp: e.activation(dst[:, 2 * jp:2 * jp + 2, :],
                                                             PS[:, b, :].rearrange("p (a c) -> p a c", a=2), ACT.Copy, scale=scale), tk)
                    bank[b] = [a]
                    out.append(a)
                return out

            tk = nat_mm(PLAN["ev_u"], 4, 8, 512, (HTh, HTl), h, (0, 1))
            ue = evac((0, 1), Qn, tk)
            k_cp0 = G(lambda e: e.memset(CP[:, :, :, :], 0.0))
            cosT, sinT = sb("cosT", [128, 4, 256]), sb("sinT", [128, 4, 256])
            T2, TN = (JK[:, 512 * i:512 * i + 512].rearrange("p (a b) -> p a b", a=2) for i in range(2))
            W = [sb(f"W{i}", [128, 2, 256]) for i in range(4)]
            hp = sb("hp", [128, 2])
            k_hp = G(lambda e: e.memset(hp[:, 0:1], TWO_PI / 4))
            k_hp = [k_hp, G(lambda e: e.memset(hp[:, 1:2], MAGIC))]
            T0, T1 = (YG[:, i, :].rearrange("p (a b) -> p a b", a=4) for i in range(2))
            ssm, gl = {}, {}

            def gelu(q0, q1):
                qs, hs = slice(q0, q1), slice(8 + q0, 8 + q1)
                gy = S(lambda e: e.activation(yq[:, qs, :], yq[:, qs, :], ACT.Gelu_apprx_tanh), [ssm[i] for i in range(q0, q1)])
                gh = S(lambda e: e.activation(YAh[:, hs, :], yq[:, qs, :], ACT.Copy), gy)
                lo = V(lambda e: e.tensor_tensor(YAl[:, hs, :], yq[:, qs, :], YAh[:, hs, :].bitcast(f32), SUB), gh)
                for q in range(q0, q1):
                    gl[q] = lo

            def s5_steps():
                tab, used, w_read, v_free, cp, cp_read = {}, {}, None, {}, None, None
                y = None

                def table(k):
                    C, Sn = cosT[:, 2 * (k % 2):2 * (k % 2) + 2, :], sinT[:, 2 * (k % 2):2 * (k % 2) + 2, :]
                    fr, ns = used.get(k - 2), []
                    for i in range(2):
                        u = S(lambda e: e.activation(C[:, i, :], tt[:, :], ACT.Copy, scale=PH[:, 2 * k + i:2 * k + i + 1]), fr, d6, k_t)
                        ns.append(V(lambda e: e.tensor_scalar(Sn[:, i, :], C[:, i, :], MAGIC, None, ADD), u, fr))
                    nr = V(lambda e: e.scalar_tensor_tensor(TN[:, :, :], Sn, MAGIC, C, SUB, SUB), ns, jk if k == 0 else tab[k - 1])
                    ab = S(lambda e: e.activation(C, TN[:, :, :], ACT.Abs), nr)
                    sn = S(lambda e: e.activation(Sn, TN[:, :, :], ACT.Sin, scale=-6.283185), nr)
                    cs = S(lambda e: e.activation(C, C, ACT.Sin, bias=hp[:, 0:1], scale=-6.283185), ab, k_hp)
                    tab[k] = [sn, cs]
                    return C, Sn

                def b_u(k):
                    for jj in (2 * (k % 2), 2 * (k % 2) + 1):
                        b = 4 + jj % 2
                        for ri in range(2):
                            bu = mm(PS[:, b, 256 * ri:256 * ri + 256], BB[32 * jj:32 * jj + 32, ri, k // 2, :],
                                    uT[32 * jj:32 * jj + 32, k // 2, :], True, True, k_B, uT_t, bank[b] if ri == 0 else None)
                    return bu

                def c_h(k, w, cp):
                    for jj in (2 * (k % 2), 2 * (k % 2) + 1):
                        for i in range(4):
                            y = mm(PS[:, 7, 0:256], CP[:, (0, 1, 2, 2)[i], jj, :], W[i][:, jj % 2, :], jj == 0 and i == 0, jj == 3 and i == 3,
                                   w[i], cp, bank[7] if jj == 0 and i == 0 else None)
                    if k % 2:
                        q = k // 2
                        ssm[q] = V(lambda e: e.scalar_tensor_tensor(yq[:, q, :], uT[:, q, :], col("s5_d", q), PS[:, 7, 0:256], MUL, ADD), y)
                        bank[7] = [ssm[q]]
                        if q > 1:
                            gelu(0 if q == 2 else 3, q + 1)
                    return y

                CS_ = {0: table(0)}
                yield
                bu = b_u(0)
                before = None
                for k in range(8):
                    C, Sn = CS_[k]
                    a = slice(2 * (k % 2), 2 * (k % 2) + 2)
                    br, bi = PS[:, 4:6, 0:256], PS[:, 4:6, 256:512]
                    A0, A1 = T0[:, a, :], T1[:, a, :]
                    fr = v_free.get(k - 2)
                    v1 = V(lambda e: e.tensor_tensor(A0, br, C, MUL), bu, tab[k], fr)
                    v3 = V(lambda e: e.tensor_tensor(A1, bi, C, MUL), fr)
                    v2 = V(lambda e: e.tensor_tensor(T2[:, :, :], bi, Sn, MUL), jk if k == 0 else v_free[k - 1])
                    v5 = V(lambda e: e.tensor_tensor(A0, A0, T2[:, :, :], ADD), v1, v2)
                    v4 = V(lambda e: e.tensor_tensor(T2[:, :, :], br, Sn, MUL), v5)
                    bank[4] = bank[5] = [v4]
                    v6 = V(lambda e: e.tensor_tensor(A1, A1, T2[:, :, :], SUB), v3, v4)
                    if before:
                        w_read = c_h(*before)
                        if k % 2 == 0:
                            cp_read = w_read
                    yield
                    if k < 7:
                        bu = b_u(k + 1)
                        CS_[k + 1] = table(k + 1)
                    if k % 2 == 0:
                        cp = []
                        for jj in range(4):
                            for half in range(2):
                                ps = slice(64 * half, 64 * half + 64)
                                cp.append(S(lambda e: e.activation(CP[ps, :, jj, 32 * jj + 16 * half:32 * jj + 16 * half + 16],
                                                                   CF[ps, :, 2 * k + jj, :], ACT.Copy), k_cf, k_cp0, cp_read))
                    g1, g2 = [], []
                    for i in range(2):
                        rj = R[:, 2 * k + i:2 * k + i + 1].to_broadcast([128, 256])
                        g1.append(V(lambda e: e.tensor_tensor_scan(A0[:, i, :], rj, A0[:, i, :], 0.0, MUL, ADD), v5, d3))
                        g2.append(V(lambda e: e.tensor_tensor_scan(A1[:, i, :], rj, A1[:, i, :], 0.0, MUL, ADD), v6))
                    w = [V(lambda e: e.tensor_tensor(W[i][:, :, :], (A0, A1)[i % 2], (C, Sn)[i in (1, 2)], MUL),
                           (g1, g2)[i % 2], w_read) for i in range(4)]
                    used[k] = v_free[k] = w
                    before = (k, w, cp)
                    yield
                c_h(*before)
                jk[0] = w[-1]

            steps = s5_steps()

            def s5_more(n=1):
                for _ in range(n):
                    next(steps, None)

            def each(*fns):
                left = list(fns)
                return lambda: left.pop(0)()

            uT_t = []
            tk = nat_mm(PLAN["ev_q"], 4, 8, 512, (HTh, HTl), h, (2, 3),
                        hook=each(lambda: (uT_t.extend(turn_pairs(Qn, ue, uT, (4, 5))), s5_more()), s5_more))
            qe = evac((2, 3), Qn, tk)
            tk = nat_mm(PLAN["ev_k"], 4, 8, 512, (HTh, HTl), h, (0, 1), hook=s5_more)
            ke = evac((0, 1), Kn, tk)

            RA, RBb = sb("RA", [128, 8, 16]), sb("RBb", [128, 8, 16])

            def rope16(z, toks, prev):
                for t in range(2):
                    zv = z[:, t, :].rearrange("p (h d) -> p h d", d=64)[:, :, 0:16]
                    cb = rc[:, t, :, :].rearrange("p a b -> p (a b)").unsqueeze(1).to_broadcast([128, 8, 16])
                    sbb = rsn[:, t, :, :].rearrange("p a b -> p (a b)").unsqueeze(1).to_broadcast([128, 8, 16])
                    x1 = G(lambda e: e.tensor_tensor(RA[:, :, :], zv, cb, MUL), toks[t], k_rope, prev)
                    x2 = G(lambda e: e.tensor_tensor(RBb[:, :, :], zv, sbb, MUL), prev)
                    x3 = G(lambda e: e.tensor_tensor(zv[:, :, 0:8], RA[:, :, 0:8], RBb[:, :, 8:16], SUB), x1, x2)
                    prev = G(lambda e: e.tensor_tensor(zv[:, :, 8:16], RA[:, :, 8:16], RBb[:, :, 0:8], ADD), x3)
                return prev

            rq = rope16(Qn, qe, None)
            rk = rope16(Kn, ke, rq)
            qT_t, kT_t = [], []
            tk = nat_mm(PLAN["ev_v"], 4, 8, 512, (HTh, HTl), h, (2, 3),
                        hook=each(lambda: (qT_t.extend(turn_pairs(Qn, [rq, rq], QT, (0, 1), 0.125)), s5_more()),
                                  lambda: (kT_t.extend(turn_pairs(Kn, [rk, rk], KT, (0, 1))), s5_more())))
            kT_pe = last("pe")
            ve = evac((2, 3), Vn, tk)
            heads = []
            for hh in range(8):
                pr = slice(64 * (hh % 2), 64 * (hh % 2) + 64)
                heads.append(([(QT[pr, hh // 2, :], KT[pr, hh // 2, :])], [Vn[:, kt, 64 * hh:64 * hh + 64] for kt in range(2)],
                              64, [(6, 256 * t + 64 * (hh % 4)) for t in range(2)], [qT_t, kT_t, ve]))
            ydeps = run_attention("A0", heads, [kT_pe, c6], lambda h0: h0 // 2, 4, mask=(cbias, k_m), fill=lambda h: s5_more(2 if h == 0 else 1),
                                  bufs=(Kn[:, :, :].rearrange("p t (a k) -> p t a k", a=2), Qn[:, :, :].rearrange("p t (a k) -> p t a k", a=2),
                                        CC[:, :, :, :].rearrange("p r j c -> p r (j c)"), None))
            s5_more(99)
            scope.pop()
            s5scope.close()

            c = PLAN["glu"][0]
            s = chunk(c)
            for k in range(4):
                for m in range(4):
                    b = 4 + m // 2
                    o = 256 * (m % 2)
                    w = slice(512 * k + 128 * m, 512 * k + 128 * m + 128)
                    tk = mm3(PS[:, b, o:o + 256], WH[:, s, w], WL[:, s, w], YAh[:, 8 + k, :], YAl[:, 8 + k, :],
                             k == 0 and m % 2 == 0, k == 3 and m % 2 == 1, split_tok[c], gl[k],
                             bank[b] if k == 0 and m % 2 == 0 else None)
            used_tok[c] = tk
            pump()
            ty = S(lambda e: e.activation(T0[:, :, :], PS[:, 4:6, :].rearrange("p a (b c) -> p (a b) c", b=2), ACT.Tanh, scale=0.5), tk)
            bank[4] = bank[5] = [ty]
            t2 = V(lambda e: e.tensor_scalar(T0[:, :, :], T0[:, :, :], 0.5, 0.5, MUL, ADD), ty)
            t3 = V(lambda e: e.tensor_tensor(T0[:, :, :], T0[:, :, :], yq[:, :, :], MUL), t2)
            t4 = S(lambda e: e.activation(YAh[:, 4:8, :], T0[:, :, :], ACT.Copy), t3)
            t5 = V(lambda e: e.tensor_tensor(YAl[:, 4:8, :], T0[:, :, :], YAh[:, 4:8, :].bitcast(f32), SUB), t4)
            for i in range(4, 8):
                ydeps[i] = t5
            ends = wide_mm(PLAN["ev_out"], lambda k: (YAh, YAl, k), lambda k: ydeps[k])
            scope.pop()
        xt = residual(ends, 1.0, k_bc)
        k_bc = gain_row(2, xt)
        ends = ffn("ffn0", xt, "norm_ffn_pre", 0, ends)
        xt = residual(ends, 1.0, k_bc)
        k_bc = gain_row(1, xt)

        KM, VM = sb("KM", [128, 2, 4, 256]), sb("VM", [128, 2, 2, 512])
        kmt, vmt = {}, {}
        k_mem = {}

        def mem_project(i, MN, fence):
            k_mem = [load("pool", MN[:, t, :], A["mem"][128 * t:128 * t + 128, :], f"c_mem{i}{t}", fence) for t in range(2)]
            return k_mem

        def mem_k(i, mr, rs, tk, bks, kz, *deps):
            z, zz = [], []
            for t in range(2):
                a = S(lambda e, t=t: e.activation(kz[:, t, :], PS[:, bks[t], :], ACT.Copy, scale=mr[:, t:t + 1]), tk, rs, *deps)
                bank[bks[t]] = [a]
                z.append(a)
            for t in range(2):
                r = head_rstd(kz[:, t, :], 4, 128, st[:, 8 + 4 * t:12 + 4 * t], z[t])
                zz.append(scaled(kz[:, t, :], 4, 128, st[:, 8 + 4 * t:12 + 4 * t], r))
            return zz

        def mem_v(i, mr, rs, tk, bks):
            for t in range(2):
                a = S(lambda e, t=t: e.activation(VM[:, i, t, :], PS[:, bks[t], :], ACT.Copy, scale=mr[:, t:t + 1]), tk, rs)
                bank[bks[t]] = [a]
                vmt.setdefault(i, []).append(a)

        def mem_turn(i, kz, zz, bks):
            kmt[i] = gain_turn(kz, zz, lambda j: KM[:, i, j:j + 2, :], col("memk_norm_2", i), bks)

        def gain_turn(src, toks, dst, gain, bks, ntile=4):
            out = []
            for jp in range(ntile // 2):
                b = bks[jp % 2]
                for j in range(2):
                    for t in range(2):
                        tk = transp(PS[:, b, j * 256 + t * 128:j * 256 + t * 128 + 128],
                                    src[:, t, 128 * (2 * jp + j):128 * (2 * jp + j) + 128], toks[t],
                                    bank[b] if j == 0 and t == 0 else None)
                a = S(lambda e, b=b, jp=jp: e.activation(dst(2 * jp), PS[:, b, :].rearrange("p (a c) -> p a c", a=2),
                                                         ACT.Copy, scale=gain), tk)
                bank[b] = [a]
                out.append(a)
            return out

        with ExitStack() as sc:
            scope.append(sc)
            fence = last()
            XB = sb("XB", [128, 8, 259])
            GT = sb("GT", [128, 8, 256])
            XC = sb("XC", [128, 8, 256])
            TR, TI = sb("TR", [128, 8, 256]), sb("TI", [128, 8, 256])
            ZN = sb("ZN", [128, 2, 2, 512])
            MN = YG
            KZ = sb("KZ", [128, 2, 512])
            k_mem = mem_project(0, MN, fence)
            h = to_features(X, xt, "norm_mix_pre", 8, (4, 5, 6, 7), ends)
            rs = row_norm(X, xt, st[:, 2:4])
            pump()
            z0 = V(lambda e: e.memset(XB[:, :, 0:3], 0.0), fence)
            lm = sb("lm", [128, 8, 8])
            L = lambda i: lm[:, i, :]
            l1 = S(lambda e: e.activation(L(0), col("rg_lam", 0, 8), ACT.Abs), fence)
            l2 = S(lambda e: e.activation(L(0), L(0), ACT.Exp, scale=-1.0), l1)
            l3 = V(lambda e: e.tensor_scalar(L(1), L(0), 2.0, None, ADD), l2)
            l4 = V(lambda e: e.reciprocal(L(1), L(1)), l3)
            l5 = V(lambda e: e.tensor_tensor(L(1), L(1), L(0), MUL), l4)
            l6 = V(lambda e: e.tensor_tensor(L(2), L(1), L(1), MUL), l5)
            a = V(lambda e: e.tensor_scalar(L(3), L(2), 1.0 / 19, 1.0 / 17, MUL, ADD), l6)
            for m in (15, 13, 11, 9, 7, 5, 3, 1):
                a = V(lambda e: e.tensor_tensor(L(3), L(3), L(2), MUL), a)
                a = V(lambda e, m=m: e.tensor_scalar(L(3), L(3), 1.0 / m, None, ADD), a)
            l7 = V(lambda e: e.tensor_tensor(L(3), L(3), L(1), MUL), a)
            l8 = V(lambda e: e.tensor_scalar(L(4), col("rg_lam", 0, 8), -1.0, 0.0, MUL, ALU.max), l7)
            l9 = V(lambda e: e.scalar_tensor_tensor(L(3), L(3), 2.0, L(4), MUL, ADD), l8)
            l10 = V(lambda e: e.tensor_scalar(L(5), L(3), 4.0, None, MUL), l9)
            l11 = V(lambda e: e.tensor_scalar(L(6), L(3), -4.0, None, MUL), l9)
            l12 = V(lambda e: e.tensor_scalar(L(0), col("rg_b_r", 0, 8), 0.5, None, MUL), l5)
            l13 = V(lambda e: e.tensor_scalar(L(1), col("rg_b_i", 0, 8), 0.5, None, MUL), l7)
            k_l = [l10, l11, l12, l13]

            zt, xb, xc, gt, ztok = {}, {}, {}, {}, {}

            def od_evac(g, n, pr, tk):
                ztok[g] = []
                for t in range(2):
                    a = S(lambda e: e.activation(ZN[:, n % 2, t, :], PS[:, pr[t], :], ACT.Copy, scale=st[:, 2 + t:3 + t]),
                          tk, rs, zt.get(n - 2), fence)
                    bank[pr[t]] = [a]
                    ztok[g].append(a)

            def od_turn(g, n, bks):
                for jp in range(2):
                    b = bks[jp]
                    for j in range(2):
                        for t in range(2):
                            tk = transp(PS[:, b, j * 256 + t * 128:j * 256 + t * 128 + 128],
                                        ZN[:, n % 2, t, 128 * (2 * jp + j):128 * (2 * jp + j) + 128], ztok[g][t],
                                        bank[b] if j == 0 and t == 0 else None)
                    zt[n] = tk
                    src = PS[:, b, :].rearrange("p (a c) -> p a c", a=2)
                    i0 = (4 * g + 2 * jp) % 8
                    if g < 2:
                        a = S(lambda e: e.activation(XB[:, i0:i0 + 2, 3:259], src, ACT.Copy), tk, fence)
                        xb[i0] = xb[i0 + 1] = a
                    else:
                        a = S(lambda e: e.activation(GT[:, i0:i0 + 2, :], src, ACT.Gelu_apprx_tanh), tk, fence)
                        gt[i0] = gt[i0 + 1] = a
                    bank[b] = [a]

            def conv(g):
                for jp in (4 * g, 4 * g + 2):
                    for j in (jp, jp + 1):
                        xc[j] = V(lambda e: e.tensor_scalar(XC[:, j, :], XB[:, j, 3:259], col("rg_conv_w", 24 + j), col("rg_conv_b", j),
                                                            MUL, ADD), xb[j], z0, fence)
                    for w in range(3):
                        for j in (jp, jp + 1):
                            xc[j] = V(lambda e: e.scalar_tensor_tensor(XC[:, j, :], XB[:, j, w:w + 256], col("rg_conv_w", 8 * w + j),
                                                                       XC[:, j, :], MUL, ADD), xc[j])

            def conv_parts(g):
                js = slice(4 * g, 4 * g + 4)
                hi = S(lambda e: e.activation(YAh[:, js, :], XC[:, js, :], ACT.Copy), [xc[j] for j in range(4 * g, 4 * g + 4)], fence)
                lo = V(lambda e: e.tensor_tensor(YAl[:, js, :], XC[:, js, :], YAh[:, js, :].bitcast(f32), SUB), hi, fence)
                for j in range(4 * g, 4 * g + 4):
                    xc[j] = lo

            HS = XC

            def gates(i, bks):
                c = PLAN[f"rg{i}"][0]
                s = chunk(c)
                tt_ = {}
                for hb in (2 * i, 2 * i + 1):
                    for gi in range(2):
                        b = bks[2 * (hb % 2) + gi]
                        for j in range(2):
                            for k in range(2):
                                o = 1024 * (hb % 2) + 512 * gi + 256 * k + 128 * j
                                tk = mm3(PS[:, b, 256 * j:256 * j + 256], WH[:, s, o:o + 128], WL[:, s, o:o + 128],
                                         YAh[:, 2 * hb + k, :], YAl[:, 2 * hb + k, :], k == 0, k == 1,
                                         split_tok[c], xc[2 * hb + k], bank[b] if j == 0 and k == 0 else None)
                        es = []
                        for j in range(2):
                            es.append(S(lambda e: e.activation((TR, TI)[gi][:, 2 * hb + j, :], PS[:, b, 256 * j:256 * j + 256], ACT.Tanh,
                                                               bias=L(gi)[:, 2 * hb + j:2 * hb + j + 1], scale=0.5), tk, k_l, fence))
                        bank[b] = es
                        tt_[(gi, hb)] = es
                used_tok[c] = tk
                yield
                pump()
                js = range(4 * i, 4 * i + 4)
                al = slice(4 * i, 4 * i + 4)
                th = [S(lambda e: e.activation(XB[:, j, 0:256], TR[:, j, :], ACT.Tanh, bias=L(5)[:, j:j + 1], scale=L(5)[:, j:j + 1]),
                        tt_[(0, j // 2)], xc[j]) for j in js]
                aa = [S(lambda e: e.activation(TR[:, j, :], TR[:, j, :], ACT.Exp, bias=L(6)[:, j:j + 1], scale=L(6)[:, j:j + 1]), th[j - 4 * i])
                      for j in js]
                yield
                b4 = V(lambda e: e.scalar_tensor_tensor(TI[:, al, :], TI[:, al, :], 1.0, XC[:, al, :], ADD, MUL),
                       [tt_[(1, hb)] for hb in (2 * i, 2 * i + 1)], xc[4 * i])
                b1 = S(lambda e: e.activation(HS[:, al, :], TR[:, al, :], ACT.Square), aa, b4)
                b2 = V(lambda e: e.scalar_tensor_tensor(HS[:, al, :], HS[:, al, :], 1.0, XB[:, al, 0:256], ADD, MUL), b1, th)
                b3 = S(lambda e: e.activation(HS[:, al, :], HS[:, al, :], ACT.Sqrt, scale=0.25), b2)
                b6 = V(lambda e: e.memset(TR[:, al, 0:1], 0.0), b1)
                yield
                fl = lambda a, hs: a[:, hs, :].rearrange("p a b -> p (a b)")
                for hs in (slice(4 * i, 4 * i + 2), slice(4 * i + 2, 4 * i + 4)):
                    b5 = V(lambda e: e.tensor_tensor(TI[:, hs, :], TI[:, hs, :], HS[:, hs, :], MUL), b3, b4)
                    b7 = V(lambda e: e.tensor_tensor_scan(fl(HS, hs), fl(TR, hs), fl(TI, hs), 0.0, MUL, ADD), b5, b6)
                    b8 = V(lambda e: e.tensor_tensor(HS[:, hs, :], HS[:, hs, :], GT[:, hs, :], MUL), b7, [gt[j] for j in js])
                    b9 = S(lambda e: e.activation(YAh[:, hs, :], HS[:, hs, :], ACT.Copy), b8, tk)
                    b10 = V(lambda e: e.tensor_tensor(YAl[:, hs, :], HS[:, hs, :], YAh[:, hs, :].bitcast(f32), SUB), b9, tk)
                    for m in range(hs.start, hs.stop):
                        ydeps[m] = b10

            def once(*fns):
                left = list(fns)

                def hook():
                    while left:
                        left.pop(0)()
                return hook

            tk = nat_mm(PLAN["od0"], 4, 8, 512, (HTh, HTl), h, (0, 1))
            od_evac(0, 0, (0, 1), tk)
            tk = nat_mm(PLAN["od1"], 4, 8, 512, (HTh, HTl), h, (2, 3), hook=once(lambda: od_turn(0, 0, (4, 5))))
            od_evac(1, 1, (2, 3), tk)
            conv(0)
            tk = nat_mm(PLAN["od2"], 4, 8, 512, (HTh, HTl), h, (0, 1),
                        hook=once(lambda: od_turn(1, 1, (4, 5)), lambda: conv_parts(0)))
            od_evac(2, 0, (0, 1), tk)
            conv(1)
            g0, g1 = gates(0, (6, 7, 2, 3)), gates(1, (2, 3, 0, 1))
            next(g0)
            next(g0)
            od3 = nat_mm(PLAN["od3"], 4, 8, 512, (HTh, HTl), h, (0, 1),
                         hook=once(lambda: conv_parts(1), lambda: od_turn(2, 0, (4, 5)), lambda: next(g0)))
            od_evac(3, 1, (0, 1), od3)
            tm = turn_rows(MN, k_mem, (4, 5, 6, 7))
            hm = split_rows(tm, "mem_norm_2", 0, (4, 5, 6, 7), od3)
            next(g1)
            next(g0, None)
            od_turn(3, 1, (4, 5))
            next(g1)
            rm = row_norm(MN, k_mem, st[:, 16:18])
            tk = nat_mm(PLAN["mem00"], 4, 8, 512, (HTh, HTl), hm, (6, 7), hook=once(lambda: next(g1)))
            tk1 = nat_mm(PLAN["mem01"], 4, 8, 512, (HTh, HTl), hm, (4, 5), hook=once(lambda: next(g1, None)))
            zz = mem_k(0, st[:, 16:18], rm, tk, (6, 7), KZ)
            mem_v(0, st[:, 16:18], rm, tk1, (4, 5))
            ends = wide_mm(PLAN["od_out"], lambda k: (YAh, YAl, k), lambda k: ydeps[k])
            mem_turn(0, KZ, zz, (4, 5))
            scope.pop()
        xt = residual(ends, 1.0, k_bc)
        k_bc = gain_row(3, xt)
        ends = ffn("ffn1", xt, "norm_ffn_pre", 8, ends)
        xt = residual(ends, 1.0, k_bc)

        with ExitStack() as sc:
            scope.append(sc)
            fence = last()
            QMT = sb("QMT", [128, 4, 256])
            QTn, KTn = sb("QTn", [128, 8, 256]), sb("KTn", [128, 8, 256])
            QTp = sb("QTp", [64, 8, 256])
            KPT = sb("KPT", [64, 256])
            tb, tg = sb("tb", [128, 2, 2, 64]), sb("tg", [128, 2, 2, 2, 64])
            GR = sb("GR", [128, 2, 64])
            ZA, ZB, ZC, ZD = (sb(f"Z{i}", [128, 2, 512]) for i in range(4))
            RP, RQ = BC[:, 0:512].rearrange("p (h d) -> p h d", d=64), BC[:, 512:1024].rearrange("p (h d) -> p h d", d=64)
            gq = sb("gq", [128, 2])
            VV = MN = YG
            CTh, CTl = YAh, YAl
            k_tb = load("pool", tb[:, :, :, :], A["tab2"][:, 0:256].rearrange("p (c t d) -> p c t d", c=2, t=2), "c_tb", fence)
            k_gr = load("pool", GR[:, :, :], A["rows"][:, 4096:4224].rearrange("p (a d) -> p a d", a=2), "c_gr", fence)
            k_mem = mem_project(1, MN, fence)
            sc_mla = 192.0 ** -0.5
            sc_mem = 128.0 ** -0.5

            h = to_features(X, xt, "norm_mix_2", 0, (4, 5, 6, 7), ends)
            rs = row_norm(X, xt, st[:, 2:4])
            pump()

            def z_evac(pr, dst, n, tk, *deps):
                out = []
                for t in range(2):
                    a = S(lambda e, t=t: e.activation(dst[:, t, 0:n], PS[:, pr[t], 0:n], ACT.Copy, scale=st[:, 2 + t:3 + t]), tk, rs, *deps)
                    bank[pr[t]] = [a]
                    out.append(a)
                return out

            def c_norm(Z, n, d, so, toks):
                out = []
                for t in range(2):
                    r = head_rstd(Z[:, t, 0:d], 1, d, st[:, so + t:so + t + 1], toks[t])
                    out.append(V(lambda e, t=t: e.tensor_scalar(Z[:, t, 0:d], Z[:, t, 0:d], st[:, so + t:so + t + 1], None, MUL), r))
                return out

            def group(cs, per, nkt, k0, off, pr, Z, deps, free, keep=False, copy=None):
                tk = nat_mm(cs, per, nkt, 512, (CTh[:, k0:k0 + nkt, :], CTl[:, k0:k0 + nkt, :]), deps, pr, off=off, keep=keep)
                out = []
                for t in range(2):
                    a = S(lambda e, t=t: e.activation(Z[:, t, :], PS[:, pr[t], :], ACT.Copy), tk, free)
                    bank[pr[t]] = [a]
                    out.append(a)
                return out

            def norm_group(Z, nh, d, toks, so):
                out = []
                for t in range(2):
                    r = head_rstd(Z[:, t, :], nh, d, st[:, so:so + nh], toks[t])
                    out.append(scaled(Z[:, t, :], nh, d, st[:, so:so + nh], r))
                    so += nh
                return out

            ta = nat_mm(PLAN["mla_a"], 4, 8, 448, (HTh, HTl), h, (0, 1))
            za = z_evac((0, 1), ZA, 448, ta, fence)
            zq = c_norm(ZA, 0, 384, 20, za)
            tb_ = nat_mm(PLAN["mla_b"], 8, 8, 256, (HTh, HTl), h, (2, 3))
            zb = z_evac((2, 3), ZB, 256, tb_, fence)
            zk = c_norm(ZB, 0, 256, 22, zb)
            tm = turn_rows(MN, k_mem, (4, 5, 6, 7))
            rm = row_norm(MN, k_mem, st[:, 16:18])
            k_tg = [rope_table(tg[:, i, :, :, :], tb, GR[:, i, :], 64, k_tb, k_gr, fence) for i in range(2)]
            k_q = V(lambda e: e.tensor_scalar(tg[:, 0, :, :, :], tg[:, 0, :, :, :], sc_mla, None, MUL), k_tg[0])
            g1 = V(lambda e: e.tensor_scalar(gq[:, 0:1], col("mla_qn"), sc_mla, None, MUL), fence)
            g2 = V(lambda e: e.tensor_scalar(gq[:, 1:2], col("memq_norm_2", 0), sc_mem, None, MUL))
            tc_ = nat_mm(PLAN["mla_c"], 4, 8, 512, (HTh, HTl), h, (0, 1))
            zc = z_evac((0, 1), ZC, 512, tc_, fence)
            hm = split_rows(tm, "mem_norm_2", 0, (4, 5, 6, 7), tc_)

            gn = lambda k: col("mla_q_a_norm_2", k) if k < 3 else col("mla_kv_a_norm_2", k - 3)

            def c_turn(ks, b):
                for i, k in enumerate(ks):
                    for t in range(2):
                        src = ZA[:, t, 128 * k:128 * k + 128] if k < 3 else ZB[:, t, 128 * (k - 3):128 * (k - 3) + 128]
                        tk = transp(PS[:, b, 256 * i + 128 * t:256 * i + 128 * t + 128], src, (zq if k < 3 else zk)[t],
                                    bank[b] if t == 0 and i == 0 else None)
                return parts(ks, CTh, CTl, b, tk, gn, fence)

            ctt = c_turn((0, 1), 2) + c_turn((2, 3), 3)
            tk = nat_mm(PLAN["mem10"], 4, 8, 512, (HTh, HTl), hm, (0, 1))
            ctt += c_turn((4,), 4)
            ckt = ctt[3:5]
            zmk = mem_k(1, st[:, 16:18], rm, tk, (0, 1), ZD, fence)
            z2 = group(PLAN["qb2"], 3, 3, 0, 0, (2, 3), ZB, ctt[0:3], last("pe"))
            zm = norm_group(ZC, 4, 128, zc, 26)
            kp = []
            for t in range(2):
                r = head_rstd(ZA[:, t, 384:448], 1, 64, st[:, 24 + t:25 + t], za[t])
                kp.append(rope(ZA[:, t, 384:448], 1, 64, t, tg[:, 1, :, :, :], RP, RQ, (st[:, 24 + t:25 + t], r), za[t], k_tg, fence))
            qp = []
            for t in range(2):
                so = st[:, 42 + 8 * t:50 + 8 * t]
                r = head_rstd(ZB[:, t, :], 8, 64, so, z2[t])
                qp.append(rope(ZB[:, t, :], 8, 64, t, tg[:, 0, :, :, :], RP, RQ, (so, r), z2[t], k_q, kp))
            qmt = gain_turn(ZC, zm, lambda j: QMT[:, j:j + 2, :], gq[:, 1:2], (5, 6))
            qm_pe = last("pe")
            tk = nat_mm(PLAN["mem11"], 4, 8, 512, (HTh, HTl), hm, (0, 1))
            mem_v(1, st[:, 16:18], rm, tk, (0, 1))
            for t in range(2):
                tk = transp(PS[0:64, 7, 128 * t:128 * t + 128], ZA[:, t, 384:448], kp[t], bank[7] if t == 0 else None)
            kpt = S(lambda e: e.activation(KPT[:, :], PS[0:64, 7, 0:256], ACT.Copy), tk, fence)
            bank[7] = [kpt]
            za_pe = tk
            mem_turn(1, ZD, zmk, (4, 5))
            zd_pe = last("pe")
            z0 = group(PLAN["qb0"], 3, 3, 0, 0, (2, 3), ZA, ctt[0:3], za_pe)
            c = PLAN["kvb0"][0]
            zk0 = group([c], 2, 2, 3, 0, (0, 1), ZC, ckt, qm_pe, keep=True)
            n0 = norm_group(ZA, 4, 128, z0, 34)
            nk0 = norm_group(ZC, 4, 128, zk0, 26)
            qpt = []
            for h2 in range(4):
                b = 4 + h2
                for j in range(2):
                    for t in range(2):
                        hh = 2 * h2 + j
                        tk = transp(PS[0:64, b, 256 * j + 128 * t:256 * j + 128 * t + 128], ZB[:, t, 64 * hh:64 * hh + 64], qp[t],
                                    bank[b] if j == 0 and t == 0 else None)
                a = S(lambda e, b=b, h2=h2: e.activation(QTp[:, 2 * h2:2 * h2 + 2, :], PS[0:64, b, :].rearrange("p (a c) -> p a c", a=2), ACT.Copy),
                      tk, fence)
                bank[b] = [a]
                qpt.append(a)
            qp_pe = tk
            vt = {}
            vt[0] = group([c], 2, 2, 3, 1024, (2, 3), VV[:, :, 0:512], ckt, [fence, tm, rm])
            qt = {0: gain_turn(ZA, n0, lambda j: QTn[:, j:j + 2, :], gq[:, 0:1], (4, 5))}
            za_pe = last("pe")
            kt = {0: gain_turn(ZC, nk0, lambda j: KTn[:, j:j + 2, :], col("mla_kn"), (6, 7))}
            qt[1], kt[1], vt[1] = [], [], []
            ct_pe = []
            z1, zk1 = [], []
            n1, nk1 = [], []

            def fill(h):
                c = PLAN["kvb1"][0]
                if h == 0:
                    z1.extend(group(PLAN["qb1"], 3, 3, 0, 0, (6, 7), ZB, ctt[0:3], qp_pe))
                    n1.extend(norm_group(ZB, 4, 128, z1, 34))
                elif h == 1:
                    zk1.extend(group([c], 2, 2, 3, 0, (6, 7), ZD, ckt, zd_pe, keep=True))
                    nk1.extend(norm_group(ZD, 4, 128, zk1, 26))
                elif h == 2:
                    vt[1].extend(group([c], 2, 2, 3, 1024, (6, 7), VV[:, :, 512:1024], ckt, [fence, tm, rm]))
                    ct_pe.extend(last("pe"))
                elif h == 4:
                    qt[1].extend(gain_turn(ZB, n1, lambda j: QTn[:, 4 + j:6 + j, :], gq[:, 0:1], (2, 3)))
                elif h == 5:
                    kt[1].extend(gain_turn(ZD, nk1, lambda j: KTn[:, 4 + j:6 + j, :], col("mla_kn"), (2, 3)))

            heads = []
            for hh in range(4):
                heads.append(([(QMT[:, hh, :], KM[:, 0, hh, :])], [VM[:, 0, kt_, 128 * hh:128 * hh + 128] for kt_ in range(2)],
                              128, [(4 + t, 128 * hh) for t in range(2)], [qmt, kmt[0], vmt[0]]))
            for hh in range(8):
                g = hh // 4
                heads.append(([(QTn[:, hh, :], KTn[:, hh, :]), (QTp[:, hh, :], KPT[:, :])],
                              [VV[:, kt_, 128 * hh:128 * hh + 128] for kt_ in range(2)], 128,
                              [(6 - 2 * g + t, 128 * (hh % 4)) for t in range(2)], [qt[g], qpt, kt[g], kpt, vt[g]]))
            quad = lambda a: a[:, :, :].rearrange("p a (b k) -> p a b k", b=2)
            ydeps = run_attention("A2", heads, [za_pe, last("pe"), qp], lambda h0: 8 if h0 == 0 else h0 - 4, 4, fill=fill, yfree=ct_pe,
                                  bufs=(quad(ZA), None, BC[:, :].rearrange("p (a k) -> p a k", a=2), quad(ZC)))
            scope.pop()
        ends = wide_mm(PLAN["out0"], lambda k: (YAh, YAl, k), lambda k: ydeps[k])
        xt = add_residual(ends)
        ends = ffn("ffn2", xt, "norm_ffn_2", 0, ends)
        xt = add_residual(ends)

        with ExitStack() as sc:
            scope.append(sc)
            fence = last()
            tb, tg = sb("tbg", [128, 2, 2, 128]), sb("tgg", [128, 2, 2, 2, 128])
            GR = sb("GRg", [128, 2, 128])
            k_tb = load("pool", tb[:, :, :, :], A["tab2"][:, 256:768].rearrange("p (c t d) -> p c t d", c=2, t=2), "c_tb", fence)
            k_gr = load("pool", GR[:, :, :], A["rows"][:, 4224:4480].rearrange("p (a d) -> p a d", a=2), "c_gr", fence)
            Z = [sb(f"Zg{i}", [128, 2, 512]) for i in range(4)]
            QT, KT2, QMT = sb("QTg", [128, 8, 256]), sb("KTg", [128, 2, 256]), sb("QMg", [128, 4, 256])
            RP, RQ = (BC[:, 512 * i:512 * i + 512].rearrange("p (h d) -> p h d", d=128) for i in range(2))
            gq2 = sb("gqg", [128, 2])
            k1 = V(lambda e: e.tensor_scalar(gq2[:, 0:1], col("memq_norm_2", 1), sc_mem, None, MUL), fence)
            k2 = V(lambda e: e.memset(gq2[:, 1:2], sc_mem), fence)
            h = to_features(X, xt, "norm_mix_2", 8, (4, 5, 6, 7), ends)
            rs = row_norm(X, xt, st[:, 2:4])
            pump()
            k_tg = [rope_table(tg[:, i, :, :, :], tb, GR[:, i, :], 128, k_tb, k_gr, fence) for i in range(2)]
            zt, n, post = {}, {}, {g: [] for g in range(4)}

            def evac(g, pr, tk):
                zt[g] = []
                for t in range(2):
                    a = S(lambda e: e.activation(Z[g][:, t, :], PS[:, pr[t], :], ACT.Copy, scale=st[:, 2 + t:3 + t]), tk, rs, fence)
                    bank[pr[t]] = [a]
                    zt[g].append(a)

            def norm(g):
                nh = 2 if g == 2 else 4
                so = (8, 34, 20, 26)[g]
                n[g] = []
                for t in range(2):
                    z, sl = Z[g][:, t, 0:128 * nh], st[:, so + nh * t:so + nh * t + nh]
                    r = head_rstd(z, nh, 128, sl, zt[g][t])
                    n[g].append(scaled(z, nh, 128, sl, r) if g == 3 else
                                rope(z, nh, 128, t, tg[:, int(g == 2), :, :, :], RP, RQ, (sl, r), zt[g][t], k_tg, fence))

            def turned(g, bks):
                dst = lambda j: (QMT[:, j:j + 2, :] if g == 3 else KT2[:, :, :] if g == 2 else QT[:, 4 * g + j:4 * g + j + 2, :])
                post[g].extend(gain_turn(Z[g], n[g], dst, gq2[:, 0:1] if g == 3 else 1.0 if g == 2 else gq2[:, 1:2], bks,
                                         2 if g == 2 else 4))

            for g, pr, prev, bks in ((3, (0, 1), None, None), (2, (2, 3), 3, (4, 5)), (0, (6, 7), 2, (2, 3))):
                tk = nat_mm(PLAN[f"gqa{g}"], 4, 8, 512, (HTh, HTl), h, pr)
                evac(g, pr, tk)
                if prev is not None:
                    turned(prev, bks)
                norm(g)

            def fill(h_):
                c = PLAN["gqa1"]
                if h_ == 0:
                    tk = nat_mm(c, 4, 8, 512, (HTh, HTl), h, (6, 7))
                    evac(1, (6, 7), tk)
                elif h_ == 2:
                    turned(0, (2, 3))
                    norm(1)
                elif h_ == 6:
                    turned(1, (2, 3))

            heads = []
            for hh in range(4):
                heads.append(([(QMT[:, hh, :], KM[:, 1, hh, :])], [VM[:, 1, kt, 128 * hh:128 * hh + 128] for kt in range(2)],
                              128, [(4 + t, 128 * hh) for t in range(2)], [post[3], kmt[1], vmt[1]]))
            for hh in range(8):
                kv = hh // 4
                heads.append(([(QT[:, hh, :], KT2[:, kv, :])], [Z[2][:, kt, 256 + 128 * kv:384 + 128 * kv] for kt in range(2)],
                              128, [(6 - 2 * kv + t, 128 * (hh % 4)) for t in range(2)], [post[kv], post[2], zt[2]]))
            ydeps = run_attention("A3", heads, fence, lambda h0: 8 if h0 == 0 else h0 - 4, 4, fill=fill)
            ends = wide_mm(PLAN["out1"], lambda k: (YAh, YAl, k), lambda k: ydeps[k])
            scope.pop()
        xt = add_residual(ends)
        ends = ffn("ffn3", xt, "norm_ffn_2", 8, ends)
        xt = add_residual(ends)
        outs = [load("sp", A["out"][128 * t:128 * t + 128, :], X[:, t, :], f"c_o{t}", xt[t]) for t in range(2)]
        end = lambda e: None

        Q.count()
        block = top.enter_context(nc.Block())

        @block.sync
        def _(e):
            Q.emit("sp", e, sems)
            for t in range(2):
                e.wait_ge(sems[f"c_o{t}"], outs[t].value)

        @block.gpsimd
        def _(e):
            Q.emit("pool", e, sems)

        @block.scalar
        def _(e):
            Q.emit("act", e, sems)

        @block.vector
        def _(e):
            Q.emit("dve", e, sems)

        @block.tensor
        def _(e):
            Q.emit("pe", e, sems)


def kernel(**inputs):
    import concourse.bacc as bacc
    from concourse.bass_utils import run_bass_kernel_spmd

    a = {k: np.asarray(v) for k, v in inputs.items()}
    PLAN, order = plan()
    tab, tab2 = tables()
    rows = np.concatenate([a["norm_mix_post"][0], a["norm_mix_post"][1], a["norm_ffn_post"][0], a["norm_ffn_post"][1],
                           a["mla_q_norm_2"][0, 128:], a["mla_k_norm_2"][0, 128:], a["gqa_q_norm_2"][0], a["gqa_k_norm_2"][0]])
    arrays = {
        "w": pack(a, order),
        "cols": columns(a),
        "rows": np.ascontiguousarray(np.broadcast_to(rows[None, :], (128, rows.shape[0]))),
        "s5": s5_layout(a),
        "tab": tab,
        "tab2": tab2,
        "x": np.ascontiguousarray(a["x"][0]),
        "mem": np.ascontiguousarray(a["mem_2"][0]),
        "pos": np.ascontiguousarray(a["positions"].reshape(2, 128).T),
    }
    nc = bacc.Bacc("TRN2", target_bir_lowering=False, num_devices=1)
    A = {n: nc.dram_tensor("in_" + n, v.shape, mybir.dt.from_np(v.dtype), kind="ExternalInput").ap() for n, v in arrays.items()}
    A["out"] = nc.dram_tensor("out_x", (256, 1024), mybir.dt.float32, kind="ExternalOutput").ap()
    program(nc, A, PLAN, len(order))
    r = run_bass_kernel_spmd(nc, [{"in_" + n: v for n, v in arrays.items()}], core_ids=[0])
    return np.asarray(r.results[0]["out_x"]).reshape(1, 256, 1024)
```

```python
import numpy as np
import concourse.bass as bass
from concourse import mybir
from contextlib import ExitStack

F = 2816
CH = 2048
NR = 3
NW = 3



def cut(name, lead, k0, nk, cols):
    return ("mat", name, lead, k0, nk, tuple(cols))


def wide(name, lead, nkt):
    return [[cut(name, lead, k, 2, [(0, 1024)])] for k in range(0, nkt, 2)]


def nat(name, lead, cols, nkt=8, per=4):
    return [[cut(name, lead, k, per, cols)] for k in range(0, nkt, per)]


def ffn_chunks(gate, up, uo, down, lead):
    out = []
    for g in range(11):
        for k in (0, 4):
            out.append([("pair", gate, up, lead, k, 4, 256 * g, uo + 256 * g)])
    return out + wide(down, lead, 22)


def plan():
    p = {}
    order = []

    def add(key, chunks):
        p[key] = list(range(len(order), len(order) + len(chunks)))
        order.extend(chunks)

    for key, c in (("u", 1536), ("q", 0), ("k", 512), ("v", 1024)):
        add("ev_" + key, nat("ev_w_in", 0, [(c, 512)]))
    add("glu", nat("s5_w_glu", 0, [(0, 512)], 4))
    add("ev_out", wide("ev_w_out", 0, 8))
    add("ffn0", ffn_chunks("ffn_w_gate", "ffn_w_up", 0, "ffn_w_down", 0))
    for g in range(4):
        add(f"od{g}", nat("od_w_in", 0, [(512 * g, 512)]))
        if g > 1:
            add(f"rg{g - 2}", [[("rg", 2 * g - 4), ("rg", 2 * g - 3)]])
    for i in range(2):
        add(f"mem0{i}", nat("w_mem_kv_2", 0, [(512 * i, 512)]))
    add("od_out", wide("od_w_out", 0, 8))
    add("ffn1", ffn_chunks("ffn_w_gate", "ffn_w_up", 0, "ffn_w_down", 1))
    add("mla_a", nat("mla_w_in_2", 0, [(0, 384), (640, 64)]))
    add("mla_b", nat("mla_w_in_2", 0, [(384, 256)], 8, 8))
    add("mla_c", nat("mla_w_in_2", 0, [(704, 512)]))
    add("mem10", nat("w_mem_kv_2", 1, [(0, 512)]))
    add("qb2", nat("mla_w_q_b_2", 0, [(192 * h + 128, 64) for h in range(8)], 3, 3))
    add("mem11", nat("w_mem_kv_2", 1, [(512, 512)]))
    for g in range(2):
        hs = range(4 * g, 4 * g + 4)
        add(f"qb{g}", nat("mla_w_q_b_2", 0, [(192 * h, 128) for h in hs], 3, 3))
        add(f"kvb{g}", [[cut("mla_w_kv_b_2", 0, 0, 2, [(256 * h + 128 * j, 128) for h in hs]) for j in range(2)]])
    add("out0", wide("w_out_2", 0, 12))
    add("ffn2", ffn_chunks("w_gate_up_2", "w_gate_up_2", F, "w_down_2", 0))
    for g in (3, 2, 0, 1):
        add(f"gqa{g}", nat("gqa_w_in_2", 0, [(512 * g, 512)]))
    add("out1", wide("w_out_2", 1, 12))
    add("ffn3", ffn_chunks("w_gate_up_2", "w_gate_up_2", F, "w_down_2", 1))
    return p, order


def kmat(a, k0, nk, c0, nc_):
    return a[128 * k0:128 * (k0 + nk), c0:c0 + nc_].reshape(nk, 128, nc_).transpose(1, 0, 2)


def pack(inputs, order):
    out = np.zeros((len(order), 128, CH), np.float32)
    for n, pieces in enumerate(order):
        at = 0
        for pc in pieces:
            if pc[0] == "mat":
                _, name, lead, k0, nk, cols = pc
                a = inputs[name][lead]
                w = np.concatenate([kmat(a, k0, nk, c, m) for c, m in cols], axis=2)
            elif pc[0] == "pair":
                _, gate, up, lead, k0, nk, cg, cu = pc
                w = np.concatenate([kmat(inputs[gate][lead], k0, nk, cg, 256),
                                    kmat(inputs[up][lead], k0, nk, cu, 256)], axis=2)
            else:
                w = np.concatenate([kmat(inputs[nm][0][pc[1]], 0, 2, 0, 256) for nm in ("rg_w_r", "rg_w_i")], axis=1)
            w = w.reshape(128, -1)
            out[n, :, at:at + w.shape[1]] = w
            at += w.shape[1]
    return out


COLS = [("norm_mix_pre", 16), ("norm_ffn_pre", 16), ("norm_mix_2", 16), ("norm_ffn_2", 16), ("mem_norm_2", 8),
        ("memq_norm_2", 2), ("memk_norm_2", 2), ("mla_q_a_norm_2", 3), ("mla_kv_a_norm_2", 2),
        ("mla_qn", 1), ("mla_kn", 1), ("rg_conv_w", 32), ("rg_conv_b", 8), ("rg_b_r", 8), ("rg_b_i", 8),
        ("rg_lam", 8), ("s5_d", 4), ("s5_a_re", 16), ("s5_a_im", 16), ("s5_log_dt", 16)]
COL = {}
_n = 0
for _name, _w in COLS:
    COL[_name] = _n
    _n += _w
NCOL = _n


def columns(inputs):
    parts = []
    for name, w in COLS:
        if name in ("mla_qn", "mla_kn"):
            a = inputs["mla_q_norm_2" if name == "mla_qn" else "mla_k_norm_2"][0, :128]
            parts.append(a.reshape(1, 128).T)
        elif name in ("s5_a_re", "s5_a_im"):
            parts.append(inputs[name][0].reshape(16, 128).T)
        elif name == "s5_log_dt":
            parts.append(np.repeat(inputs[name][0].reshape(16, 2), 64, axis=1).T)
        else:
            parts.append(np.ascontiguousarray(inputs[name]).reshape(w, 128).T)
    return np.ascontiguousarray(np.concatenate(parts, axis=1))


def s5_layout(inputs):
    out = []
    for name in ("s5_b_re", "s5_b_im"):
        b = inputs[name][0].reshape(4, 4, 2, 64, 16)
        w = np.zeros((4, 4, 2, 16, 2, 64), np.float32)
        for g in range(2):
            w[:, :, g, :, g, :] = b[:, :, g].transpose(0, 1, 3, 2)
        out.append(w.transpose(1, 2, 3, 0, 4, 5).reshape(128, 512))
    for name in ("s5_c_re", "s5_c_im"):
        c = inputs[name][0].reshape(16, 2, 16, 64)
        out.append(c.transpose(1, 3, 0, 2).reshape(128, 256))
    return np.ascontiguousarray(np.concatenate(out, axis=1))


def rope_tables(dim):
    row = np.repeat(np.arange(4, dtype=np.float32), 64)
    col = np.tile(np.arange(64, dtype=np.float32), 4)
    ax = dim // 2
    inv = (np.float32(10000.0) ** (-np.arange(0, ax, 2, dtype=np.float32) / np.float32(ax))).astype(np.float32)
    cs, sn = [], []
    for pos in (row, col):
        ang = (pos[:, None] * inv).astype(np.float32)
        cs += [np.cos(ang), np.cos(ang)]
        sn += [-np.sin(ang), np.sin(ang)]
    return [np.concatenate(t, axis=1).astype(np.float32).reshape(2, 128, dim).transpose(1, 0, 2).reshape(128, 2 * dim)
            for t in (cs, sn)]


def tables():
    q = np.arange(256)[:, None]
    k = np.arange(256)[None, :]
    d = q - k
    c = ((d >= 0) & (d <= 128)).astype(np.float32) + ((d >= 0) & (d % 4 == 0)) + ((d >= 0) & (d % 16 == 0))
    bias = np.where(c > 0, np.log(np.maximum(c, 1)), -1e30)
    two = lambda a: a.reshape(2, 128, 256).transpose(1, 0, 2).reshape(128, 512)
    inv = (np.float32(500000.0) ** (-(np.arange(8, dtype=np.float32) * np.float32(2.0) / np.float32(16)))).astype(np.float32)
    ident = np.eye(128, dtype=np.float32)
    t0 = [ident, two(bias), np.tile(np.arange(256, dtype=np.float32), (128, 1)), np.tile(inv, (128, 1))]
    a = np.ascontiguousarray(np.concatenate([x.astype(np.float32) for x in t0], axis=1))
    b = np.ascontiguousarray(np.concatenate(rope_tables(64) + rope_tables(128), axis=1))
    return a, b


class Tok:

    def __init__(self, sem, inc):
        self.sem, self.inc, self.value, self.used = sem, inc, None, False


class Later:

    def matmul(self, *a, **k):
        return lambda e: e.matmul(*a, **k)

    def transpose(self, *a, **k):
        return lambda e: e.transpose(*a, **k)

    def activation(self, *a, **k):
        return lambda e: e.activation(*a, **k)

    def tensor_tensor(self, *a, **k):
        return lambda e: e.tensor_tensor(*a, **k)

    def tensor_scalar(self, *a, **k):
        return lambda e: e.tensor_scalar(*a, **k)

    def scalar_tensor_tensor(self, *a, **k):
        return lambda e: e.scalar_tensor_tensor(*a, **k)

    def tensor_copy(self, *a, **k):
        return lambda e: e.tensor_copy(*a, **k)

    def tensor_reduce(self, *a, **k):
        return lambda e: e.tensor_reduce(*a, **k)

    def tensor_tensor_scan(self, *a, **k):
        return lambda e: e.tensor_tensor_scan(*a, **k)

    def tensor_tensor_reduce(self, *a, **k):
        return lambda e: e.tensor_tensor_reduce(*a, **k)

    def reciprocal(self, *a, **k):
        return lambda e: e.reciprocal(*a, **k)

    def memset(self, *a, **k):
        return lambda e: e.memset(*a, **k)

    def dma_start(self, *a, **k):
        return lambda e: e.dma_start(*a, **k)


LATER = Later()


def flat(deps):
    out = []
    for d in deps:
        out += flat(d) if isinstance(d, (list, tuple)) else [] if d is None else [d]
    return out


class Queues:

    def __init__(self):
        self.q = {}

    def op(self, eng, fn, *deps):
        t = Tok(eng, 1)
        self.put(eng, fn, t, deps)
        return t

    def dma(self, eng, out, in_, sem, *deps):
        t = Tok(sem, 16)
        t.used = True
        self.put(eng, lambda e: e.dma_start(out, in_), t, deps)
        return t

    def put(self, eng, fn, t, deps):
        deps = flat(deps)
        for d in deps:
            d.used = True
        self.q.setdefault(eng, []).append((fn(LATER), t, deps))

    def count(self):
        total = {}
        for eng in self.q:
            for _, t, _ in self.q[eng]:
                if t.used:
                    total[t.sem] = total.get(t.sem, 0) + t.inc
                    t.value = total[t.sem]

    def emit(self, eng, e, sems):
        seen = {}
        for fn, t, deps in self.q.get(eng, []):
            need = {}
            for d in deps:
                need[d.sem] = max(need.get(d.sem, 0), d.value)
            for s in sorted(need, key=str):
                if seen.get(s, 0) < need[s]:
                    e.wait_ge(sems[s], need[s])
                    seen[s] = need[s]
            ins = fn(e)
            if t.used:
                ins.then_inc(sems[t.sem], t.inc)


def program(nc, A, PLAN, NCH):
    f32, f32r, i32 = mybir.dt.float32, mybir.dt.float32r, mybir.dt.int32
    ALU, ACT, AX = mybir.AluOpType, mybir.ActivationFunctionType, mybir.AxisListType
    MUL, ADD, SUB = ALU.mult, ALU.add, ALU.subtract
    Q = Queues()
    PE = lambda fn, *d: Q.op("pe", fn, *d)
    V = lambda fn, *d: Q.op("dve", fn, *d)
    S = lambda fn, *d: Q.op("act", fn, *d)
    G = lambda fn, *d: Q.op("pool", fn, *d)
    TWO_PI = 6.283185307179586

    top = ExitStack()
    with top:
        scope = [top]

        def sb(name, shape, dt=f32):
            return scope[-1].enter_context(nc.sbuf_tensor(name, shape, dt))

        def sem(name):
            return top.enter_context(nc.semaphore(name))

        sems = {k: sem("s_" + k) for k in ("pe", "dve", "act", "pool")}
        for r in range(NR):
            sems[f"w{r}"] = sem(f"s_w{r}")

        def load(eng, out, in_, name, *deps):
            if name not in sems:
                sems[name] = sem("s_" + name)
            return Q.dma(eng, out, in_, name, *deps)

        X = sb("X", [128, 2, 1024])
        HTh, HTl = sb("HTh", [128, 8, 256], f32r), sb("HTl", [128, 8, 256], f32r)
        YAh, YAl = sb("YAh", [128, 12, 256], f32r), sb("YAl", [128, 12, 256], f32r)
        RAW = sb("RAW", [128, NR, CH])
        WH, WL = sb("WH", [128, NW, CH], f32r), sb("WL", [128, NW, CH], f32r)
        BC = sb("BC", [128, 1024])
        ident = sb("ident", [128, 128])
        cst = sb("cst", [128, NCOL])
        st = sb("st", [128, 64])
        mh = sb("mh", [128, 16])
        YG = sb("YG", [128, 2, 1024])
        PS = top.enter_context(nc.psum_tensor("PS", [128, 8, 512], f32))
        bank = [[] for _ in range(8)]

        def col(name, i=0, n=1):
            return cst[:, COL[name] + i:COL[name] + i + n]

        split_tok, used_tok, raw_free, dma_tok = {}, {}, {}, {}
        nxt = {"dma": 0, "split": 0}

        def stream_load():
            c = nxt["dma"]
            if c >= NCH:
                return
            nxt["dma"] = c + 1
            dma_tok[c] = Q.dma("sp", RAW[:, c % NR, :], A["w"][c], f"w{c % NR}", raw_free.get(c - NR))

        def stream_split(cuts=1):
            c = nxt["split"]
            nxt["split"] = c + 1
            s, r = c % NW, c % NR
            split_tok[c] = []
            for i in range(cuts):
                w = slice(CH // cuts * i, CH // cuts * (i + 1))
                hi = S(lambda e: e.activation(WH[:, s, w], RAW[:, r, w], ACT.Copy), dma_tok[c], used_tok.get(c - NW))
                lo = V(lambda e: e.tensor_tensor(WL[:, s, w], RAW[:, r, w], WH[:, s, w].bitcast(f32), SUB),
                       hi, dma_tok[c], used_tok.get(c - NW))
                split_tok[c].append(lo)
            raw_free[c] = [hi, lo]
            stream_load()

        def pump():
            while nxt["split"] < NCH and (nxt["split"] < NW or (nxt["split"] - NW) in used_tok):
                stream_split()

        def chunk(c):
            while nxt["split"] <= c:
                stream_split()
            return c % NW

        def mm(out, a, b, start, stop, *deps):
            return PE(lambda e: e.matmul(out, a, b, start=start, stop=stop), *deps)

        def mm3(out, ah, al, bh, bl, start, stop, *deps):
            mm(out, ah, bh, start, False, *deps)
            mm(out, ah, bl, False, False)
            return mm(out, al, bh, False, stop)

        def nat_mm(cs, per, nkt, N, src, srcdeps, banks, off=0, keep=False, hook=None, edge=None):
            hi, lo = src

            def product(c, s, k, t):
                w = slice(off + (k % per) * N, off + (k % per + 1) * N)
                return mm3(PS[:, banks[t], 0:N], hi[:, k, 128 * t:128 * t + 128], lo[:, k, 128 * t:128 * t + 128],
                           WH[:, s, w], WL[:, s, w], k == 0, k == nkt - 1, split_tok[c][:k + 1],
                           srcdeps[t][k] if edge else srcdeps[k], bank[banks[t]] if k == 0 else None)

            if edge:
                at = [(c, chunk(c)) for c in cs]
                for k in range(nkt):
                    product(*at[k // per], k, 0)
                    if k == edge.when:
                        edge.turn(1)
                        pump()
                        edge.rs = row_norm(X, edge.x, st[:, 2:4])
                for k in range(nkt):
                    tk = product(*at[k // per], k, 1)
                    used_tok[cs[k // per]] = tk
                    if k == per - 1:
                        pump()
                return tk
            k = 0
            for c in cs:
                s = chunk(c)
                for _ in range(min(per, nkt - k)):
                    for t in range(2):
                        tk = product(c, s, k, t)
                    k += 1
                if not keep:
                    used_tok[c] = tk
                    if c != cs[-1] or hook:
                        pump()
                if hook:
                    hook()
            return tk

        def wide_mm(cs, src_of, dep_of, edge, behind=None, after=()):
            n = len(cs)

            def product(c, s, k, t):
                hi, lo, j = src_of(k)
                for half in range(2):
                    w = slice((k % 2) * 1024 + half * 512, (k % 2) * 1024 + half * 512 + 512)
                    tk = mm3(PS[:, 2 * t + half, :], hi[:, j, 128 * t:128 * t + 128], lo[:, j, 128 * t:128 * t + 128],
                             WH[:, s, w], WL[:, s, w], k == 0, k == 2 * n - 1, split_tok[c], dep_of(k),
                             bank[2 * t + half] if k == 0 else None)
                return tk

            for ci, c in enumerate(cs[:-2]):
                s = chunk(c)
                for t in range(2):
                    for k in (2 * ci, 2 * ci + 1):
                        tk = product(c, s, k, t)
                used_tok[c] = tk
                if ci == 0 and behind:
                    behind()
                pump()
                if ci < len(after):
                    after[ci]()
            at = [(c, chunk(c)) for c in cs[-2:] for _ in range(2)]
            for t in range(2):
                for i in range(4):
                    tk = product(*at[i], 2 * n - 4 + i, t)
                    if t == 1 and i == 1:
                        used_tok[cs[-2]] = tk
                        pump()
                    if t == 1 and i == 3:
                        edge.turn(0)
                        pump()
                if t == 0:
                    edge.add(0, tk)
            used_tok[cs[-1]] = tk
            edge.add(1, tk)

        def transp(out, in_, *deps):
            p = in_.shape[0]
            return PE(lambda e: e.transpose(out, in_, ident[0:p, 0:p]), *deps)

        def turn_rows(src, srctok, banks, free=None):
            T = [None] * 8
            for t in range(2):
                for k in range(8):
                    b, o = banks[k // 2], (k % 2) * 256 + t * 128
                    T[k] = transp(PS[:, b, o:o + 128], src[:, t, 128 * k:128 * k + 128], srctok[t], bank[b] if t == 0 else None)
            return T

        def split_rows(T, gain, gi, banks, free):
            return [d for j in range(4) for d in parts((2 * j, 2 * j + 1), HTh, HTl, banks[j], T[2 * j + 1],
                                                       lambda k: col(gain, gi + k), free)]

        def parts(ks, dh, dl, b, tk, gain, free):
            for i, k in enumerate(ks):
                hi = S(lambda e: e.activation(dh[:, k, :], PS[:, b, 256 * i:256 * i + 256], ACT.Copy, scale=gain(k)), tk, free)
            out = []
            for i, k in enumerate(ks):
                out.append(V(lambda e: e.scalar_tensor_tensor(dl[:, k, :], PS[:, b, 256 * i:256 * i + 256], gain(k),
                                                              dh[:, k, :].bitcast(f32), MUL, SUB), hi, free))
            bank[b] = out[-1:]
            return out

        def rstd(out, ss, n, eps_toks, free=None):
            w = out.shape[1]
            a = V(lambda e: e.tensor_scalar(out, ss, 1.0 / n, 1e-6, MUL, ADD), eps_toks, free)
            return G(lambda e: e.tensor_tensor(out, out, mh[:, 0:w], ALU.pow), a, k_mh)

        def row_norm(src, srctok, out):
            a = [square(lambda e: e.activation(JK[:, :], src[:, t, :], ACT.Square, accum_out=out[:, t:t + 1]), srctok[t])
                 for t in range(2)]
            return rstd(out, out, 1024, a)

        JK = sb("JK", [128, 1024])
        jk = [None]

        def square(fn, *deps):
            jk[0] = S(fn, jk[0], *deps)
            return jk[0]

        def post_norm(gain_tok):
            def step(t, end):
                sq, yg = [], []
                for hf in range(2):
                    y = PS[:, 2 * t + hf, :]
                    cs = slice(512 * hf, 512 * hf + 512)
                    sq.append(square(lambda e: e.activation(JK[:, cs], y, ACT.Square,
                                                            accum_out=st[:, 60 + 2 * t + hf:61 + 2 * t + hf]), end))
                    yg.append(V(lambda e: e.tensor_tensor(YG[:, t, cs], y, BC[:, cs], MUL), sq[-1], gain_tok))
                    bank[2 * t + hf] = yg[-1:]
                s0 = V(lambda e: e.tensor_tensor(st[:, t:t + 1], st[:, 60 + 2 * t:61 + 2 * t], st[:, 61 + 2 * t:62 + 2 * t], ADD), sq)
                r = rstd(st[:, t:t + 1], st[:, t:t + 1], 1024, s0)
                return [V(lambda e: e.scalar_tensor_tensor(X[:, t, 512 * hf:512 * hf + 512], YG[:, t, 512 * hf:512 * hf + 512],
                                                           st[:, t:t + 1], X[:, t, 512 * hf:512 * hf + 512], MUL, ADD), r, yg)
                        for hf in range(2)]
            return step

        def plain(t, end):
            out = []
            for hf in range(2):
                x = X[:, t, 512 * hf:512 * hf + 512]
                out.append(V(lambda e: e.tensor_tensor(x, PS[:, 2 * t + hf, :], x, ADD), end))
                bank[2 * t + hf] = out[-1:]
            return out

        class Edge:

            def __init__(self, step, gain=None, gi=0):
                self.step, self.gain, self.gi = step, gain, gi
                self.when = 3 if step is plain else 5
                self.x, self.h = [None, None], [None, None]
                self.free = None

            def add(self, t, end):
                if self.free is None:
                    self.free = end
                self.x[t] = self.step(t, end)

            def turn(self, t):
                if not self.gain:
                    return
                self.h[t] = []
                gain = lambda k: col(self.gain, self.gi + k)
                tok = [None] * 2
                for j in range(2):
                    for i in range(4):
                        k = 4 * j + i
                        tok[j] = transp(PS[:, 4 + 2 * t + j, 128 * i:128 * i + 128], X[:, t, 128 * k:128 * k + 128],
                                        self.x[t][j], bank[4 + 2 * t + j] if i == 0 else None)
                ts = slice(128 * t, 128 * t + 128)
                for j in range(2):
                    src = lambda i: PS[:, 4 + 2 * t + j, 128 * i:128 * i + 128]
                    hi = [S(lambda e: e.activation(HTh[:, 4 * j + i, ts], src(i), ACT.Copy, scale=gain(4 * j + i)), tok[j], self.free)
                          for i in range(4)]
                    lo = [V(lambda e: e.scalar_tensor_tensor(HTl[:, 4 * j + i, ts], src(i), gain(4 * j + i),
                                                             HTh[:, 4 * j + i, ts].bitcast(f32), MUL, SUB), hi[-1], self.free)
                          for i in range(4)]
                    bank[4 + 2 * t + j] = lo[-1:]
                    self.h[t] += lo

        def last(*names):
            return [Q.q[n][-1][1] for n in (names or ("pe", "dve", "act", "pool")) if Q.q.get(n)]

        def ffn(key, edge, after):
            cs = PLAN[key]
            with ExitStack() as sc:
                scope.append(sc)
                fence = last()
                YBh, YBl = sb(key + "YBh", [128, 10, 256], f32r), sb(key + "YBl", [128, 10, 256], f32r)
                TH, SG, AN = (sb(key + n, [128, 2, 2, 256]) for n in ("TH", "SG", "AN"))
                scope.pop()
                ydst = lambda j: (YAh, YAl, j) if j < 12 else (YBh, YBl, j - 12)
                pairs = [(0, 1), (6, 7), (2, 3)]
                tk = nat_mm(cs[0:2], 4, 8, 512, (HTh, HTl), edge.h, pairs[0], edge=edge)
                rs = edge.rs
                rs2 = V(lambda e: e.tensor_tensor(st[:, 6:8], st[:, 2:4], st[:, 2:4], MUL), rs)
                rsh = V(lambda e: e.tensor_scalar(st[:, 4:6], st[:, 2:4], 0.5, None, MUL), rs)
                done = {}
                free = {"TH": {}, "AN": {}}

                def act(g, tk):
                    p = pairs[g % 3]
                    for t in range(2):
                        gg, uu = PS[:, p[t], 0:256], PS[:, p[t], 256:512]
                        b = g % 2
                        th = S(lambda e, t=t, b=b, gg=gg: e.activation(TH[:, b, t, :], gg, ACT.Tanh, scale=st[:, 4 + t:5 + t]),
                               tk, rsh, free["TH"].get((g - 2, t)), fence)
                        sg = V(lambda e, t=t, b=b, gg=gg: e.scalar_tensor_tensor(SG[:, b, t, :], TH[:, b, t, :], 1.0, gg, ADD, MUL),
                               th, fence)
                        free["TH"][(g, t)] = sg
                        an = V(lambda e, t=t, b=b, uu=uu: e.scalar_tensor_tensor(AN[:, b, t, :], uu, st[:, 6 + t:7 + t],
                                                                                 SG[:, b, t, :], MUL, MUL),
                               sg, rs2, free["AN"].get(g - 2))
                        bank[p[t]] = [an]
                        done[(g, t)] = an

                ydep = {}

                def fold(g):
                    b = 4 + g % 2
                    for t in range(2):
                        for j in range(2):
                            tk = transp(PS[:, b, j * 256 + t * 128:j * 256 + t * 128 + 128],
                                        AN[:, g % 2, t, 128 * j:128 * j + 128], done[(g, t)], bank[b] if t == 0 and j == 0 else None)
                    free["AN"][g] = tk
                    hi, lo, j = ydst(2 * g)
                    src = PS[:, b, :].rearrange("p (a c) -> p a c", a=2)
                    a = S(lambda e: e.activation(hi[:, j:j + 2, :], src, ACT.Copy, scale=0.5), tk, fence)
                    l = V(lambda e: e.scalar_tensor_tensor(lo[:, j:j + 2, :], src, 0.5, hi[:, j:j + 2, :].bitcast(f32), MUL, SUB), a, fence)
                    bank[b] = [a, l]
                    ydep[2 * g] = ydep[2 * g + 1] = l

                h = [edge.h[0][k:k + 1] + edge.h[1][k:k + 1] for k in range(8)]
                for g in range(11):
                    if g:
                        tk = nat_mm(cs[2 * g:2 * g + 2], 4, 8, 512, (HTh, HTl), h, pairs[g % 3])
                        pump()
                        fold(g - 1)
                    act(g, tk)
                wide_mm(cs[22:], ydst, lambda k: ydep[k], after, lambda: fold(10))

        def run_attention(nm, heads, free, yout, per_out, mask=None, fill=None, sbanks=(0, 1), tbanks=(2, 3), bufs=None, yfree=None):
            nH = len(heads)
            P, SM, Y, PT = bufs or (None,) * 4
            P = sb(nm + "P", [128, 2, 2, 256]) if P is None else P
            PT = sb(nm + "PT", [128, 2, 2, 256]) if PT is None else PT
            M, den = sb(nm + "M", [128, nH, 2]), sb(nm + "den", [128, 2, nH])
            dv = heads[0][2]
            wd = per_out * dv
            Y = sb(nm + "Y", [128, 2, wd]) if Y is None else Y
            ex, pvt, pt_ready, turned, ydeps, ytr = {}, {}, {}, {}, {}, [None]
            nk = lambda t: t + 1 if mask else 2
            sdone = {}

            def products(h):
                parts_, _, _, _, deps = heads[h]
                b = sbanks[h % 2]
                for t in range(2):
                    for i, (q, k) in enumerate(parts_):
                        tk = mm(PS[:, b, 256 * t:256 * t + 128 * nk(t)], q[:, 128 * t:128 * t + 128], k[:, 0:128 * nk(t)],
                                i == 0, i == len(parts_) - 1, deps, bank[b] if t == 0 and i == 0 else None)
                sdone[h] = tk

            def scores(h):
                b = sbanks[h % 2]
                tk = sdone[h]
                src = PS[:, b, :].rearrange("p (t k) -> p t k", t=2)
                ex[h] = []
                if mask:
                    for t in range(2):
                        n = 128 * nk(t)
                        m = V(lambda e: e.tensor_tensor_reduce(out=SM[:, h % 2, t, 0:n], in0=src[:, t, 0:n], in1=mask[0][:, t, 0:n],
                                                               scale=-1.0, scalar=3e38, op0=ADD, op1=ALU.min,
                                                               accum_out=M[:, h, t:t + 1]),
                              tk, ex.get(h - 2), mask[1], free)
                        ex[h].append(S(lambda e: e.activation(P[:, h % 2, t, 0:n], SM[:, h % 2, t, 0:n], ACT.Exp,
                                                              bias=M[:, h, t:t + 1], scale=-1.0, accum_out=den[:, t, h:h + 1]),
                                       m, turned.get(h - 2), free))
                    bank[b] = [m]
                else:
                    m = V(lambda e: e.tensor_reduce(M[:, h, :], src, AX.X, ALU.max, negate=True), tk)
                    for t in range(2):
                        ex[h].append(S(lambda e: e.activation(P[:, h % 2, t, :], src[:, t, :], ACT.Exp, bias=M[:, h, t:t + 1],
                                                              accum_out=den[:, t, h:h + 1]), m, turned.get(h - 2), free))
                    bank[b] = ex[h][-1:]

            def turn(h):
                b = tbanks[h % 2]
                for t in range(2):
                    for kt in range(nk(t)):
                        tk = transp(PS[:, b, kt * 256 + t * 128:kt * 256 + t * 128 + 128],
                                    P[:, h % 2, t, 128 * kt:128 * kt + 128], ex[h][t],
                                    bank[b] if t == 0 and kt == 0 else None)
                turned[h] = tk
                if mask:
                    dst, src = PT[:, h % 2, :, :].rearrange("p t k -> p (t k)"), PS[:, b, :]
                    cs = [(dst[:, 0:256], src[:, 0:256]), (dst[:, 384:512], src[:, 384:512])]
                else:
                    cs = [(PT[:, h % 2, :, :], PS[:, b, :].rearrange("p (t k) -> p t k", t=2))]
                for dst, src in cs:
                    if mask:
                        c = S(lambda e: e.activation(dst, src, ACT.Copy), tk, pvt.get(h - 2), free)
                    else:
                        c = V(lambda e: e.tensor_copy(dst, src), tk, pvt.get(h - 2), free)
                bank[b] = [c]
                pt_ready[h] = c

            def pv(h):
                _, v, dv, out, deps = heads[h]
                for t in range(2):
                    b, o = out[t]
                    for kt in range(nk(t)):
                        tk = mm(PS[:, b, o:o + dv], PT[:, h % 2, kt, 128 * t:128 * t + 128], v[kt],
                                kt == 0, kt == nk(t) - 1, pt_ready[h], deps, bank[b] if kt == 0 and h % per_out == 0 else None)
                pvt[h] = tk

            def finish(h0):
                hs = slice(h0, h0 + per_out)
                r = V(lambda e: e.reciprocal(den[:, :, hs], den[:, :, hs]), [ex[h] for h in range(h0, h0 + per_out)])
                ys = []
                for t in range(2):
                    b, o = heads[h0][3][t]
                    ys.append(V(lambda e: e.tensor_tensor(Y[:, t, :].rearrange("p (h d) -> p h d", d=dv),
                                                          PS[:, b, o:o + wd].rearrange("p (h d) -> p h d", d=dv),
                                                          den[:, t, hs].unsqueeze(2).to_broadcast([128, per_out, dv]), MUL),
                                r, pvt[h0 + per_out - 1], ytr[0], free))
                    bank[b] = [ys[-1]]
                for jp in range(wd // 256):
                    b = tbanks[jp] if mask else heads[h0][3][jp][0]
                    for j in range(2):
                        for t in range(2):
                            tk = transp(PS[:, b, j * 256 + t * 128:j * 256 + t * 128 + 128],
                                        Y[:, t, 128 * (2 * jp + j):128 * (2 * jp + j) + 128], ys[t],
                                        bank[b] if j == 0 and t == 0 else None)
                    ytr[0] = tk
                    i0 = yout(h0) + 2 * jp
                    src = PS[:, b, :].rearrange("p (a c) -> p a c", a=2)
                    hi = S(lambda e: e.activation(YAh[:, i0:i0 + 2, :], src, ACT.Copy), tk, yfree)
                    lo = V(lambda e: e.tensor_tensor(YAl[:, i0:i0 + 2, :], src, YAh[:, i0:i0 + 2, :].bitcast(f32), SUB), hi)
                    bank[b] = [hi, lo]
                    ydeps[i0] = ydeps[i0 + 1] = lo

            for h in range(nH + 2):
                if h < nH:
                    products(h)
                    if not mask:
                        scores(h)
                if fill and mask:
                    fill(h)
                    if h < nH:
                        scores(h)
                if 0 <= h - 1 < nH:
                    turn(h - 1)
                if fill and not mask:
                    fill(h)
                if 0 <= h - 2 < nH:
                    pv(h - 2)
                    if (h - 2) % per_out == per_out - 1:
                        finish(h - 2 - per_out + 1)
            return ydeps

        def head_rstd(zs, nh, d, out, ztoks):
            b = []
            for n, (z, ztok) in enumerate(zip(zs, ztoks)):
                if nh <= 4:
                    b += [square(lambda e: e.activation(JK[:, d * i:d * i + d], z[:, d * i:d * i + d], ACT.Square,
                                                        accum_out=out[:, nh * n + i:nh * n + i + 1]), ztok) for i in range(nh)]
                else:
                    j = JK[:, 512 * n:512 * n + nh * d]
                    a = square(lambda e: e.activation(j, z, ACT.Square), ztok)
                    b.append(V(lambda e: e.tensor_reduce(out[:, nh * n:nh * n + nh], j.rearrange("p (h d) -> p h d", d=d), AX.X, ADD), a))
            jk[0] = b[-2:]
            return rstd(out, out, d, b)

        def head_norm(zs, nh, d, so, ztoks):
            r = head_rstd(zs, nh, d, st[:, so:so + nh * len(zs)], ztoks)
            return lambda: [scaled(z, nh, d, st[:, so + nh * n:so + nh * n + nh], r, ztoks[n]) for n, z in enumerate(zs)]

        def scaled(z, nh, d, r, *toks):
            zv = z.rearrange("p (h d) -> p h d", d=d)
            return V(lambda e: e.tensor_tensor(zv, zv, r.unsqueeze(2).to_broadcast([128, nh, d]), MUL), *toks)

        def each(*fns):
            left = list(fns)
            return lambda: left.pop(0)()

        def once(*fns):
            left = list(fns)

            def hook():
                while left:
                    left.pop(0)()
            return hook

        k_c = load("sp", cst[:, :], A["cols"][:, :], "c_c")
        k_id = load("sp", ident[:, :], A["tab"][:, 0:128], "c_id")
        k_x = [load("sp", X[:, 0, :], A["x"][0:128, :], "c_x0")]
        k_mh = G(lambda e: e.memset(mh[:, :], -0.5))

        def rope_table(dst, tb, gr, d, *deps):
            q = d // 4
            out = []
            for t in range(2):
                out.append(V(lambda e: e.tensor_tensor(dst[:, 0, t, :], tb[:, 0, t, :], gr, MUL), *deps))
                v = lambda a: a.rearrange("p (a f c) -> p a f c", a=2, f=2)
                for f in range(2):
                    out.append(V(lambda e: e.tensor_tensor(v(dst[:, 1, t, :])[:, :, f, :], v(tb[:, 1, t, :])[:, :, f, :],
                                                           v(gr)[:, :, 1 - f, :], MUL), *deps))
            return out

        def rope(z, nh, d, t, tg, RP, RQ, r, tok, *deps):
            zv = z.rearrange("p (h d) -> p h d", d=d)
            cb = tg[:, 0, t, :].unsqueeze(1).to_broadcast([128, nh, d])
            x = [V(lambda e: e.tensor_tensor(RP[:, 0:nh, :], zv, cb, MUL), tok, *deps)]
            q = d // 4
            for ax in range(2):
                for f in range(2):
                    a, b = 2 * q * ax + q * f, 2 * q * ax + q * (1 - f)
                    s_ = tg[:, 1, t, a:a + q].unsqueeze(1).to_broadcast([128, nh, q])
                    x.append(V(lambda e: e.tensor_tensor(RQ[:, 0:nh, a:a + q], zv[:, :, b:b + q], s_, MUL), *deps))
            y = V(lambda e: e.tensor_tensor(zv, RP[:, 0:nh, :], RQ[:, 0:nh, :], ADD), x)
            return V(lambda e: e.tensor_tensor(zv, zv, r[0].unsqueeze(2).to_broadcast([128, nh, d]), MUL), y, r[1])

        def gain_row(i, *deps):
            return load("sp" if i == 0 else "pool", BC[:, :], A["rows"][:, 1024 * i:1024 * i + 1024], "c_bc" if i else "c_b0", *deps)

        with ExitStack() as sc:
            scope.append(sc)
            cbias = sb("cbias", [128, 2, 256])
            tt = sb("tt", [128, 256])
            inv = sb("inv", [128, 8])
            uT = sb("uT", [128, 4, 256])
            Qn, Kn, Vn = sb("Qn", [128, 2, 512]), sb("Kn", [128, 2, 512]), sb("Vn", [128, 2, 512])
            QT, KT = sb("QT", [128, 4, 256]), sb("KT", [128, 4, 256])
            yq = sb("yq", [128, 4, 256])
            s5scope = sc.enter_context(ExitStack())
            scope.append(s5scope)
            BB = sb("BB", [128, 2, 4, 128])
            CC = sb("CC", [128, 2, 16, 16])
            pos = sb("pos", [128, 2], i32)
            k_p = load("sp", pos[:, :], A["pos"][:, :], "c_p")
            k_i = load("sp", inv[:, :], A["tab"][:, 896:904], "c_i")
            stream_load()
            k_x.append(load("sp", X[:, 1, :], A["x"][128:256, :], "c_x1"))
            for _ in range(NR - 1):
                stream_load()
            k_t = load("sp", tt[:, :], A["tab"][:, 640:896], "c_t")
            k_B = load("sp", BB[:, :, :, :], A["s5"][:, 0:1024].rearrange("p (r q s) -> p r q s", r=2, q=4), "c_B")
            k_C = load("sp", CC[:, :, :, :], A["s5"][:, 1024:1536].rearrange("p (r j c) -> p r j c", r=2, j=16), "c_C")
            k_m = load("sp", cbias[:, :, :], A["tab"][:, 128:640].rearrange("p (t k) -> p t k", t=2), "c_m")
            k_bc = gain_row(0)

            S(lambda e: e.activation(st[:, 62:64], mh[:, 0:2], ACT.Copy), k_mh)
            s5 = sb("s5", [128, 16, 16])
            p = lambda i: s5[:, i, :]
            DT, R, TH_, PH, SN, CS, N1, N2, DEN, FR, FI = (p(i) for i in range(11))
            d1 = S(lambda e: e.activation(DT, col("s5_log_dt", 0, 16), ACT.Exp), k_c)
            d2 = V(lambda e: e.tensor_tensor(R, col("s5_a_re", 0, 16), DT, MUL), d1)
            d3 = S(lambda e: e.activation(R, R, ACT.Exp), d2)
            d4 = V(lambda e: e.tensor_tensor(TH_, col("s5_a_im", 0, 16), DT, MUL), d1)
            MAGIC = 12582912.0
            C1, C2 = 6.28125, float(np.float32(0.0019350051879882812))
            C3 = TWO_PI - C1 - C2

            def reduce_2pi(x, n, *deps):
                a = V(lambda e: e.tensor_scalar(n, x, 1.0 / TWO_PI, MAGIC, MUL, ADD), *deps)
                a = V(lambda e: e.tensor_scalar(n, n, MAGIC, None, SUB), a)
                for cc in (C1, C2, C3):
                    a = V(lambda e, cc=cc: e.scalar_tensor_tensor(x, n, -cc, x, MUL, ADD), a)
                return V(lambda e: e.tensor_scalar(x, x, 3.1415925, -3.1415925, ALU.min, ALU.max), a)

            d5 = reduce_2pi(TH_, N1, d4)
            d6 = V(lambda e: e.tensor_scalar(PH, TH_, 1.0 / TWO_PI, None, MUL), d5)
            ang = sb("ang", [128, 2, 8])
            angn = sb("angn", [128, 2, 8])
            rc, rsn = sb("rc", [128, 2, 2, 8]), sb("rsn", [128, 2, 2, 8])
            posf = sb("posf", [128, 2])
            a1 = V(lambda e: e.tensor_copy(posf[:, :], pos[:, :]), k_p)
            for t in range(2):
                a2 = V(lambda e, t=t: e.tensor_scalar(ang[:, t, :], inv[:, :], posf[:, t:t + 1], None, MUL), a1, k_i)
            a3 = reduce_2pi(ang[:, :, :], angn[:, :, :], a2)
            edge = Edge(plain, "norm_mix_pre", 0)
            edge.x, edge.free = [[[k, k_id]] * 2 for k in k_x], k_c
            edge.turn(0)
            stream_split(4)
            a4 = S(lambda e: e.activation(angn[:, :, :], ang[:, :, :], ACT.Abs), a3)
            d7 = S(lambda e: e.activation(N1, TH_, ACT.Abs), d5)
            a7 = V(lambda e: e.tensor_scalar(angn[:, :, :], angn[:, :, :], -1.0, TWO_PI / 4, MUL, ADD), a4)
            d8 = V(lambda e: e.tensor_scalar(N1, N1, -1.0, TWO_PI / 4, MUL, ADD), d7)
            for hh in range(2):
                a5 = S(lambda e, hh=hh: e.activation(rsn[:, :, hh, :], ang[:, :, :], ACT.Sin), a3)
                a6 = S(lambda e, hh=hh: e.activation(rc[:, :, hh, :], angn[:, :, :], ACT.Sin), a7)
            k_rope = [a5, a6]
            d9 = S(lambda e: e.activation(SN, TH_, ACT.Sin), d5)
            d10 = S(lambda e: e.activation(CS, N1, ACT.Sin), d8)
            AR, AI = col("s5_a_re", 0, 16), col("s5_a_im", 0, 16)
            e1 = V(lambda e: e.tensor_tensor(SN, SN, R, MUL), d9, d3)
            e2 = V(lambda e: e.tensor_tensor(CS, CS, R, MUL), d10, d3)
            e3 = V(lambda e: e.tensor_scalar(CS, CS, -1.0, None, ADD), e2)
            e4 = V(lambda e: e.tensor_tensor(N1, AR, AR, MUL), e3)
            e5 = V(lambda e: e.tensor_tensor(N2, AI, AI, MUL))
            e6 = V(lambda e: e.tensor_tensor(DEN, N1, N2, ADD), e4, e5)
            e7 = V(lambda e: e.reciprocal(DEN, DEN), e6)
            e8 = V(lambda e: e.tensor_tensor(N1, CS, AR, MUL), e6, e3)
            e9 = V(lambda e: e.tensor_tensor(N2, SN, AI, MUL), e6, e1)
            e10 = V(lambda e: e.tensor_tensor(FR, N1, N2, ADD), e8, e9)
            e11 = V(lambda e: e.tensor_tensor(FR, FR, DEN, MUL), e10, e7)
            e12 = V(lambda e: e.tensor_tensor(N1, SN, AR, MUL), e10)
            e13 = V(lambda e: e.tensor_tensor(N2, CS, AI, MUL), e10)
            e14 = V(lambda e: e.tensor_tensor(FI, N1, N2, SUB), e12, e13)
            k_f = V(lambda e: e.tensor_tensor(FI, FI, DEN, MUL), e14, e11)
            pump()
            mm_u = nat_mm(PLAN["ev_u"], 4, 8, 512, (HTh, HTl), edge.h, (0, 1), edge=edge)
            rs = edge.rs
            h = [[edge.h[t][k] for t in range(2)] for k in range(8)]
            CP = sb("CP", [128, 3, 4, 128])

            def evac(banks, dst, tk):
                out = []
                for t in range(2):
                    a = S(lambda e, t=t: e.activation(dst[:, t, :], PS[:, banks[t], :], ACT.Copy, scale=st[:, 2 + t:3 + t]), tk, rs)
                    bank[banks[t]] = [a]
                    out.append(a)
                pump()
                return out

            def turn_pairs(src, toks, dst, bks, scale=1.0):
                out = []
                for jp in range(2):
                    b = bks[jp]
                    for j in range(2):
                        for t in range(2):
                            tk = transp(PS[:, b, j * 256 + t * 128:j * 256 + t * 128 + 128],
                                        src[:, t, 128 * (2 * jp + j):128 * (2 * jp + j) + 128], toks[t],
                                        bank[b] if j == 0 and t == 0 else None)
                    a = S(lambda e, b=b, jp=jp: e.activation(dst[:, 2 * jp:2 * jp + 2, :],
                                                             PS[:, b, :].rearrange("p (a c) -> p a c", a=2), ACT.Copy, scale=scale), tk)
                    bank[b] = [a]
                    out.append(a)
                return out

            ue = evac((0, 1), Qn, mm_u)
            CF = sb("CF", [128, 3, 16, 16])
            CT = sb("CT", [128, 16, 16])
            fr = FR.unsqueeze(2).to_broadcast([128, 16, 16])
            fi = FI.unsqueeze(2).to_broadcast([128, 16, 16])
            c1 = V(lambda e: e.tensor_tensor(CF[:, 0, :, :], CC[:, 0, :, :], fr, MUL), k_f, k_C)
            c2 = V(lambda e: e.tensor_tensor(CT[:, :, :], CC[:, 1, :, :], fi, MUL), k_f)
            c3 = V(lambda e: e.tensor_tensor(CF[:, 0, :, :], CF[:, 0, :, :], CT[:, :, :], SUB), c1, c2)
            V(lambda e: e.tensor_scalar(CF[:, 1, :, :], CF[:, 0, :, :], -1.0, None, MUL), c3)
            c4 = V(lambda e: e.tensor_tensor(CF[:, 2, :, :], CC[:, 0, :, :], fi, MUL), c3)
            c5 = V(lambda e: e.tensor_tensor(CT[:, :, :], CC[:, 1, :, :], fr, MUL), c3)
            c6 = V(lambda e: e.tensor_tensor(CF[:, 2, :, :], CF[:, 2, :, :], CT[:, :, :], ADD), c4, c5)
            k_cf = V(lambda e: e.tensor_scalar(CF[:, 2, :, :], CF[:, 2, :, :], -1.0, None, MUL), c6)
            k_cp0 = G(lambda e: e.memset(CP[:, :, :, :], 0.0))
            cosT, sinT = sb("cosT", [128, 4, 256]), sb("sinT", [128, 4, 256])
            T2, TN = (JK[:, 512 * i:512 * i + 512].rearrange("p (a b) -> p a b", a=2) for i in range(2))
            W = [sb(f"W{i}", [128, 2, 256]) for i in range(4)]
            hp = sb("hp", [128, 1])
            k_hp = G(lambda e: e.memset(hp[:, 0:1], TWO_PI / 4))
            T0, T1 = (YG[:, i, :].rearrange("p (a b) -> p a b", a=4) for i in range(2))
            ssm, gl = {}, {}

            def gelu(q0, q1):
                qs, hs = slice(q0, q1), slice(8 + q0, 8 + q1)
                gy = S(lambda e: e.activation(yq[:, qs, :], yq[:, qs, :], ACT.Gelu_apprx_tanh), [ssm[i] for i in range(q0, q1)])
                gh = S(lambda e: e.activation(YAh[:, hs, :], yq[:, qs, :], ACT.Copy), gy)
                lo = V(lambda e: e.tensor_tensor(YAl[:, hs, :], yq[:, qs, :], YAh[:, hs, :].bitcast(f32), SUB), gh)
                for q in range(q0, q1):
                    gl[q] = lo

            def s5_steps():
                tab, used, w_read, v_free, cp, cp_read, turns = {}, {}, None, {}, None, None, {}
                y = None

                def turn_angles(k):
                    C = cosT[:, 2 * (k % 2):2 * (k % 2) + 2, :]
                    turns[k] = [S(lambda e: e.activation(C[:, i, :], tt[:, :], ACT.Copy, scale=PH[:, 2 * k + i:2 * k + i + 1]),
                                  used.get(k - 2), d6, k_t) for i in range(2)]

                def table(k):
                    C, Sn = cosT[:, 2 * (k % 2):2 * (k % 2) + 2, :], sinT[:, 2 * (k % 2):2 * (k % 2) + 2, :]
                    ns = [V(lambda e: e.tensor_scalar(Sn[:, i, :], C[:, i, :], MAGIC, None, ADD), turns[k][i], used.get(k - 2))
                          for i in range(2)]
                    nr = V(lambda e: e.scalar_tensor_tensor(TN[:, :, :], Sn, MAGIC, C, SUB, SUB), ns, jk if k == 0 else tab[k - 1])
                    ab = S(lambda e: e.activation(C, TN[:, :, :], ACT.Abs), nr)
                    sn = S(lambda e: e.activation(Sn, TN[:, :, :], ACT.Sin, scale=-6.283185), nr)
                    cs = S(lambda e: e.activation(C, C, ACT.Sin, bias=hp[:, 0:1], scale=-6.283185), ab, k_hp)
                    tab[k] = [sn, cs]
                    return C, Sn

                def b_u(k):
                    for jj in (2 * (k % 2), 2 * (k % 2) + 1):
                        b = 4 + jj % 2
                        for ri in range(2):
                            bu = mm(PS[:, b, 256 * ri:256 * ri + 256], BB[32 * jj:32 * jj + 32, ri, k // 2, :],
                                    uT[32 * jj:32 * jj + 32, k // 2, :], True, True, k_B, uT_t, bank[b] if ri == 0 else None)
                    return bu

                def c_h(k, w, cp):
                    for jj in (2 * (k % 2), 2 * (k % 2) + 1):
                        for i in range(4):
                            y = mm(PS[:, 7, 0:256], CP[:, (0, 1, 2, 2)[i], jj, :], W[i][:, jj % 2, :], jj == 0 and i == 0, jj == 3 and i == 3,
                                   w[i], cp, bank[7] if jj == 0 and i == 0 else None)
                    if k % 2:
                        q = k // 2
                        ssm[q] = V(lambda e: e.scalar_tensor_tensor(yq[:, q, :], uT[:, q, :], col("s5_d", q), PS[:, 7, 0:256], MUL, ADD), y)
                        bank[7] = [ssm[q]]
                        if q > 1:
                            gelu(0 if q == 2 else 3, q + 1)
                    return y

                turn_angles(0)
                CS_ = {0: table(0)}
                yield
                bu = b_u(0)
                before = None
                for k in range(8):
                    C, Sn = CS_[k]
                    a = slice(2 * (k % 2), 2 * (k % 2) + 2)
                    br, bi = PS[:, 4:6, 0:256], PS[:, 4:6, 256:512]
                    A0, A1 = T0[:, a, :], T1[:, a, :]
                    fr = v_free.get(k - 2)
                    v1 = V(lambda e: e.tensor_tensor(A0, br, C, MUL), bu, tab[k], fr)
                    v3 = V(lambda e: e.tensor_tensor(A1, bi, C, MUL), fr)
                    v2 = V(lambda e: e.tensor_tensor(T2[:, :, :], bi, Sn, MUL), jk if k == 0 else v_free[k - 1])
                    v5 = V(lambda e: e.tensor_tensor(A0, A0, T2[:, :, :], ADD), v1, v2)
                    v4 = V(lambda e: e.tensor_tensor(T2[:, :, :], br, Sn, MUL), v5)
                    bank[4] = bank[5] = [v4]
                    v6 = V(lambda e: e.tensor_tensor(A1, A1, T2[:, :, :], SUB), v3, v4)
                    if k < 7:
                        turn_angles(k + 1)
                    if before:
                        w_read = c_h(*before)
                        if k % 2 == 0:
                            cp_read = w_read
                    yield
                    if k < 7:
                        bu = b_u(k + 1)
                        CS_[k + 1] = table(k + 1)
                    if k % 2 == 0:
                        cp = []
                        for jj in range(4):
                            for half in range(2):
                                ps = slice(64 * half, 64 * half + 64)
                                cp.append(S(lambda e: e.activation(CP[ps, :, jj, 32 * jj + 16 * half:32 * jj + 16 * half + 16],
                                                                   CF[ps, :, 2 * k + jj, :], ACT.Copy), k_cf, k_cp0, cp_read))
                    g1, g2 = [], []
                    for i in range(2):
                        rj = R[:, 2 * k + i:2 * k + i + 1].to_broadcast([128, 256])
                        g1.append(V(lambda e: e.tensor_tensor_scan(A0[:, i, :], rj, A0[:, i, :], 0.0, MUL, ADD), v5, d3))
                        g2.append(V(lambda e: e.tensor_tensor_scan(A1[:, i, :], rj, A1[:, i, :], 0.0, MUL, ADD), v6))
                    w = [V(lambda e: e.tensor_tensor(W[i][:, :, :], (A0, A1)[i % 2], (C, Sn)[i in (1, 2)], MUL),
                           (g1, g2)[i % 2], w_read) for i in range(4)]
                    used[k] = v_free[k] = w
                    before = (k, w, cp)
                    yield
                c_h(*before)
                jk[0] = w[-1]

            steps = s5_steps()

            def s5_more(n=1):
                for _ in range(n):
                    next(steps, None)

            uT_t = []
            tk = nat_mm(PLAN["ev_q"], 4, 8, 512, (HTh, HTl), h, (2, 3),
                        hook=each(lambda: (uT_t.extend(turn_pairs(Qn, ue, uT, (4, 5))), s5_more()), s5_more))
            qe = evac((2, 3), Qn, tk)
            tk = nat_mm(PLAN["ev_k"], 4, 8, 512, (HTh, HTl), h, (0, 1), hook=s5_more)
            ke = evac((0, 1), Kn, tk)

            RA, RBb = sb("RA", [128, 8, 16]), sb("RBb", [128, 8, 16])

            def rope16(z, toks, prev):
                for t in range(2):
                    zv = z[:, t, :].rearrange("p (h d) -> p h d", d=64)[:, :, 0:16]
                    cb = rc[:, t, :, :].rearrange("p a b -> p (a b)").unsqueeze(1).to_broadcast([128, 8, 16])
                    sbb = rsn[:, t, :, :].rearrange("p a b -> p (a b)").unsqueeze(1).to_broadcast([128, 8, 16])
                    x1 = G(lambda e: e.tensor_tensor(RA[:, :, :], zv, cb, MUL), toks[t], k_rope, prev)
                    x2 = G(lambda e: e.tensor_tensor(RBb[:, :, :], zv, sbb, MUL), prev)
                    x3 = G(lambda e: e.tensor_tensor(zv[:, :, 0:8], RA[:, :, 0:8], RBb[:, :, 8:16], SUB), x1, x2)
                    prev = G(lambda e: e.tensor_tensor(zv[:, :, 8:16], RA[:, :, 8:16], RBb[:, :, 0:8], ADD), x3)
                return prev

            rq = rope16(Qn, qe, None)
            rk = rope16(Kn, ke, rq)
            qT_t, kT_t = [], []
            tk = nat_mm(PLAN["ev_v"], 4, 8, 512, (HTh, HTl), h, (2, 3),
                        hook=each(lambda: (qT_t.extend(turn_pairs(Qn, [rq, rq], QT, (0, 1), 0.125)), s5_more()),
                                  lambda: (kT_t.extend(turn_pairs(Kn, [rk, rk], KT, (0, 1))), s5_more())))
            kT_pe = last("pe")
            ve = evac((2, 3), Vn, tk)
            heads = []
            for hh in range(8):
                pr = slice(64 * (hh % 2), 64 * (hh % 2) + 64)
                heads.append(([(QT[pr, hh // 2, :], KT[pr, hh // 2, :])], [Vn[:, kt, 64 * hh:64 * hh + 64] for kt in range(2)],
                              64, [(6, 256 * t + 64 * (hh % 4)) for t in range(2)], [qT_t, kT_t, ve]))
            ydeps = run_attention("A0", heads, [kT_pe, c6], lambda h0: h0 // 2, 4, mask=(cbias, k_m), fill=lambda h: s5_more(2 if h == 0 else 1),
                                  bufs=(Kn[:, :, :].rearrange("p t (a k) -> p t a k", a=2), Qn[:, :, :].rearrange("p t (a k) -> p t a k", a=2),
                                        CC[:, :, :, :].rearrange("p r j c -> p r (j c)"), None))
            s5_more(99)
            scope.pop()
            s5scope.close()

            c = PLAN["glu"][0]
            s = chunk(c)
            for k in range(4):
                for m in range(4):
                    b = 4 + m // 2
                    o = 256 * (m % 2)
                    w = slice(512 * k + 128 * m, 512 * k + 128 * m + 128)
                    tk = mm3(PS[:, b, o:o + 256], WH[:, s, w], WL[:, s, w], YAh[:, 8 + k, :], YAl[:, 8 + k, :],
                             k == 0 and m % 2 == 0, k == 3 and m % 2 == 1, split_tok[c], gl[k],
                             bank[b] if k == 0 and m % 2 == 0 else None)
            used_tok[c] = tk
            pump()
            ty = S(lambda e: e.activation(T0[:, :, :], PS[:, 4:6, :].rearrange("p a (b c) -> p (a b) c", b=2), ACT.Tanh, scale=0.5), tk)
            bank[4] = bank[5] = [ty]
            t2 = V(lambda e: e.tensor_scalar(T0[:, :, :], T0[:, :, :], 0.5, 0.5, MUL, ADD), ty)
            t3 = V(lambda e: e.tensor_tensor(T0[:, :, :], T0[:, :, :], yq[:, :, :], MUL), t2)
            t4 = S(lambda e: e.activation(YAh[:, 4:8, :], T0[:, :, :], ACT.Copy), t3)
            t5 = V(lambda e: e.tensor_tensor(YAl[:, 4:8, :], T0[:, :, :], YAh[:, 4:8, :].bitcast(f32), SUB), t4)
            for i in range(4, 8):
                ydeps[i] = t5
            edge = Edge(post_norm(k_bc), "norm_ffn_pre", 0)
            wide_mm(PLAN["ev_out"], lambda k: (YAh, YAl, k), lambda k: ydeps[k], edge)
            scope.pop()
        k_bc = gain_row(2, edge.x)
        after = Edge(post_norm(k_bc), "norm_mix_pre", 8)
        ffn("ffn0", edge, after)
        edge = after
        k_bc = gain_row(1, edge.x)

        KM, VM = sb("KM", [128, 2, 4, 256]), sb("VM", [128, 2, 2, 512])
        kmt, vmt = {}, {}
        k_mem = {}

        def mem_project(i, MN, fence):
            k_mem = [load("pool", MN[:, t, :], A["mem"][128 * t:128 * t + 128, :], f"c_mem{i}{t}", fence) for t in range(2)]
            return k_mem

        def mem_k(i, mr, rs, tk, bks, kz, *deps):
            z = []
            for t in range(2):
                a = S(lambda e, t=t: e.activation(kz[:, t, :], PS[:, bks[t], :], ACT.Copy, scale=mr[:, t:t + 1]), tk, rs, *deps)
                bank[bks[t]] = [a]
                z.append(a)
            return z

        def mem_k_norm(kz, z):
            return head_norm([kz[:, t, :] for t in range(2)], 4, 128, 8, z)

        def mem_v(i, mr, rs, tk, bks):
            for t in range(2):
                a = S(lambda e, t=t: e.activation(VM[:, i, t, :], PS[:, bks[t], :], ACT.Copy, scale=mr[:, t:t + 1]), tk, rs)
                bank[bks[t]] = [a]
                vmt.setdefault(i, []).append(a)

        def mem_turn(i, kz, zz, bks):
            kmt[i] = gain_turn(kz, zz, lambda j: KM[:, i, j:j + 2, :], col("memk_norm_2", i), bks)

        def gain_turn(src, toks, dst, gain, bks, ntile=4):
            out = []
            for jp in range(ntile // 2):
                b = bks[jp % 2]
                for j in range(2):
                    for t in range(2):
                        tk = transp(PS[:, b, j * 256 + t * 128:j * 256 + t * 128 + 128],
                                    src[:, t, 128 * (2 * jp + j):128 * (2 * jp + j) + 128], toks[t],
                                    bank[b] if j == 0 and t == 0 else None)
                a = S(lambda e, b=b, jp=jp: e.activation(dst(2 * jp), PS[:, b, :].rearrange("p (a c) -> p a c", a=2),
                                                         ACT.Copy, scale=gain), tk)
                bank[b] = [a]
                out.append(a)
            return out

        with ExitStack() as sc:
            scope.append(sc)
            fence = last()
            XB = sb("XB", [128, 8, 259])
            GT = sb("GT", [128, 8, 256])
            XC = sb("XC", [128, 8, 256])
            TR, TI = sb("TR", [128, 8, 256]), sb("TI", [128, 8, 256])
            ZN = sb("ZN", [128, 2, 2, 512])
            MN = YG
            KZ = sb("KZ", [128, 2, 512])
            k_mem = mem_project(0, MN, fence)
            z0 = V(lambda e: e.memset(XB[:, :, 0:3], 0.0), fence)
            od0 = nat_mm(PLAN["od0"], 4, 8, 512, (HTh, HTl), edge.h, (0, 1), edge=edge)
            lm = sb("lm", [128, 8, 8])
            L = lambda i: lm[:, i, :]
            l1 = S(lambda e: e.activation(L(0), col("rg_lam", 0, 8), ACT.Abs), fence)
            l2 = S(lambda e: e.activation(L(0), L(0), ACT.Exp, scale=-1.0), l1)
            l3 = V(lambda e: e.tensor_scalar(L(1), L(0), 2.0, None, ADD), l2)
            l4 = V(lambda e: e.reciprocal(L(1), L(1)), l3)
            l5 = V(lambda e: e.tensor_tensor(L(1), L(1), L(0), MUL), l4)
            l6 = V(lambda e: e.tensor_tensor(L(2), L(1), L(1), MUL), l5)
            a = V(lambda e: e.tensor_scalar(L(3), L(2), 1.0 / 19, 1.0 / 17, MUL, ADD), l6)
            for m in (15, 13, 11, 9, 7, 5, 3, 1):
                a = V(lambda e: e.tensor_tensor(L(3), L(3), L(2), MUL), a)
                a = V(lambda e, m=m: e.tensor_scalar(L(3), L(3), 1.0 / m, None, ADD), a)
            l7 = V(lambda e: e.tensor_tensor(L(3), L(3), L(1), MUL), a)
            l8 = V(lambda e: e.tensor_scalar(L(4), col("rg_lam", 0, 8), -1.0, 0.0, MUL, ALU.max), l7)
            l9 = V(lambda e: e.scalar_tensor_tensor(L(3), L(3), 2.0, L(4), MUL, ADD), l8)
            l10 = V(lambda e: e.tensor_scalar(L(5), L(3), 4.0, None, MUL), l9)
            l11 = V(lambda e: e.tensor_scalar(L(6), L(3), -4.0, None, MUL), l9)
            l12 = V(lambda e: e.tensor_scalar(L(0), col("rg_b_r", 0, 8), 0.5, None, MUL), l5)
            l13 = V(lambda e: e.tensor_scalar(L(1), col("rg_b_i", 0, 8), 0.5, None, MUL), l7)
            k_l = [l10, l11, l12, l13]

            tk = od0
            rs = edge.rs
            zt, xb, xc, gt, ztok = {}, {}, {}, {}, {}

            def od_evac(g, n, pr, tk):
                ztok[g] = []
                for t in range(2):
                    a = S(lambda e: e.activation(ZN[:, n % 2, t, :], PS[:, pr[t], :], ACT.Copy, scale=st[:, 2 + t:3 + t]),
                          tk, rs, zt.get(n - 2), fence)
                    bank[pr[t]] = [a]
                    ztok[g].append(a)
                pump()

            def od_turn(g, n, bks):
                for jp in range(2):
                    b = bks[jp]
                    for j in range(2):
                        for t in range(2):
                            tk = transp(PS[:, b, j * 256 + t * 128:j * 256 + t * 128 + 128],
                                        ZN[:, n % 2, t, 128 * (2 * jp + j):128 * (2 * jp + j) + 128], ztok[g][t],
                                        bank[b] if j == 0 and t == 0 else None)
                    zt[n] = tk
                    src = PS[:, b, :].rearrange("p (a c) -> p a c", a=2)
                    i0 = (4 * g + 2 * jp) % 8
                    if g < 2:
                        a = S(lambda e: e.activation(XB[:, i0:i0 + 2, 3:259], src, ACT.Copy), tk, fence)
                        xb[i0] = xb[i0 + 1] = a
                    else:
                        a = S(lambda e: e.activation(GT[:, i0:i0 + 2, :], src, ACT.Gelu_apprx_tanh), tk, fence)
                        gt[i0] = gt[i0 + 1] = a
                    bank[b] = [a]

            def conv(g):
                for jp in (4 * g, 4 * g + 2):
                    for j in (jp, jp + 1):
                        xc[j] = V(lambda e: e.tensor_scalar(XC[:, j, :], XB[:, j, 3:259], col("rg_conv_w", 24 + j), col("rg_conv_b", j),
                                                            MUL, ADD), xb[j], z0, fence)
                    for w in range(3):
                        for j in (jp, jp + 1):
                            xc[j] = V(lambda e: e.scalar_tensor_tensor(XC[:, j, :], XB[:, j, w:w + 256], col("rg_conv_w", 8 * w + j),
                                                                       XC[:, j, :], MUL, ADD), xc[j])

            def conv_parts(g):
                js = slice(4 * g, 4 * g + 4)
                hi = S(lambda e: e.activation(YAh[:, js, :], XC[:, js, :], ACT.Copy), [xc[j] for j in range(4 * g, 4 * g + 4)], fence)
                lo = V(lambda e: e.tensor_tensor(YAl[:, js, :], XC[:, js, :], YAh[:, js, :].bitcast(f32), SUB), hi, fence)
                for j in range(4 * g, 4 * g + 4):
                    xc[j] = lo

            HS = XC

            def gates(i, bks):
                c = PLAN[f"rg{i}"][0]
                s = chunk(c)
                tt_ = {}
                for hb in (2 * i, 2 * i + 1):
                    for gi in range(2):
                        b = bks[2 * (hb % 2) + gi]
                        for j in range(2):
                            for k in range(2):
                                o = 1024 * (hb % 2) + 512 * gi + 256 * k + 128 * j
                                tk = mm3(PS[:, b, 256 * j:256 * j + 256], WH[:, s, o:o + 128], WL[:, s, o:o + 128],
                                         YAh[:, 2 * hb + k, :], YAl[:, 2 * hb + k, :], k == 0, k == 1,
                                         split_tok[c], xc[2 * hb + k], bank[b] if j == 0 and k == 0 else None)
                        es = []
                        for j in range(2):
                            es.append(S(lambda e: e.activation((TR, TI)[gi][:, 2 * hb + j, :], PS[:, b, 256 * j:256 * j + 256], ACT.Tanh,
                                                               bias=L(gi)[:, 2 * hb + j:2 * hb + j + 1], scale=0.5), tk, k_l, fence))
                        bank[b] = es
                        tt_[(gi, hb)] = es
                used_tok[c] = tk
                yield
                pump()
                js = range(4 * i, 4 * i + 4)
                al = slice(4 * i, 4 * i + 4)
                th = [S(lambda e: e.activation(XB[:, j, 0:256], TR[:, j, :], ACT.Tanh, bias=L(5)[:, j:j + 1], scale=L(5)[:, j:j + 1]),
                        tt_[(0, j // 2)], xc[j]) for j in js]
                aa = [S(lambda e: e.activation(TR[:, j, :], TR[:, j, :], ACT.Exp, bias=L(6)[:, j:j + 1], scale=L(6)[:, j:j + 1]), th[j - 4 * i])
                      for j in js]
                yield
                b4 = V(lambda e: e.scalar_tensor_tensor(TI[:, al, :], TI[:, al, :], 1.0, XC[:, al, :], ADD, MUL),
                       [tt_[(1, hb)] for hb in (2 * i, 2 * i + 1)], xc[4 * i])
                b1 = S(lambda e: e.activation(HS[:, al, :], TR[:, al, :], ACT.Square), aa, b4)
                b2 = V(lambda e: e.scalar_tensor_tensor(HS[:, al, :], HS[:, al, :], 1.0, XB[:, al, 0:256], ADD, MUL), b1, th)
                b3 = S(lambda e: e.activation(HS[:, al, :], HS[:, al, :], ACT.Sqrt, scale=0.25), b2)
                b6 = V(lambda e: e.memset(TR[:, al, 0:1], 0.0), b1)
                yield
                fl = lambda a, hs: a[:, hs, :].rearrange("p a b -> p (a b)")
                for hs in (slice(4 * i, 4 * i + 2), slice(4 * i + 2, 4 * i + 4)):
                    b5 = V(lambda e: e.tensor_tensor(TI[:, hs, :], TI[:, hs, :], HS[:, hs, :], MUL), b3, b4)
                    b7 = V(lambda e: e.tensor_tensor_scan(fl(HS, hs), fl(TR, hs), fl(TI, hs), 0.0, MUL, ADD), b5, b6)
                    b8 = V(lambda e: e.tensor_tensor(HS[:, hs, :], HS[:, hs, :], GT[:, hs, :], MUL), b7, [gt[j] for j in js])
                    b9 = S(lambda e: e.activation(YAh[:, hs, :], HS[:, hs, :], ACT.Copy), b8, tk)
                    b10 = V(lambda e: e.tensor_tensor(YAl[:, hs, :], HS[:, hs, :], YAh[:, hs, :].bitcast(f32), SUB), b9, tk)
                    for m in range(hs.start, hs.stop):
                        ydeps[m] = b10

            h = [[edge.h[t][k] for t in range(2)] for k in range(8)]
            od_evac(0, 0, (0, 1), tk)
            tk = nat_mm(PLAN["od1"], 4, 8, 512, (HTh, HTl), h, (2, 3), hook=once(lambda: od_turn(0, 0, (4, 5))))
            od_evac(1, 1, (2, 3), tk)
            conv(0)
            tk = nat_mm(PLAN["od2"], 4, 8, 512, (HTh, HTl), h, (0, 1),
                        hook=once(lambda: od_turn(1, 1, (4, 5)), lambda: conv_parts(0)))
            od_evac(2, 0, (0, 1), tk)
            conv(1)
            g0, g1 = gates(0, (6, 7, 2, 3)), gates(1, (2, 3, 0, 1))
            next(g0)
            next(g0)
            od3 = nat_mm(PLAN["od3"], 4, 8, 512, (HTh, HTl), h, (0, 1),
                         hook=each(lambda: (conv_parts(1), od_turn(2, 0, (4, 5)), next(g0)), lambda: None))
            od_evac(3, 1, (0, 1), od3)
            tm = turn_rows(MN, k_mem, (4, 5, 6, 7))
            hm = split_rows(tm, "mem_norm_2", 0, (4, 5, 6, 7), od3)
            next(g1)
            next(g0, None)
            od_turn(3, 1, (4, 5))
            next(g1)
            next(g1)
            tk = nat_mm(PLAN["mem00"], 4, 8, 512, (HTh, HTl), hm, (6, 7), hook=lambda: None)
            tk1 = nat_mm(PLAN["mem01"], 4, 8, 512, (HTh, HTl), hm, (4, 5), hook=each(lambda: next(g1, None), lambda: None))
            z, zz = [], []

            def mem_out():
                rm = row_norm(MN, k_mem, st[:, 16:18])
                z.extend(mem_k(0, st[:, 16:18], rm, tk, (6, 7), KZ))
                mem_v(0, st[:, 16:18], rm, tk1, (4, 5))

            edge = Edge(post_norm(k_bc), "norm_ffn_pre", 8)
            wide_mm(PLAN["od_out"], lambda k: (YAh, YAl, k), lambda k: ydeps[k], edge,
                    after=(mem_out, lambda: zz.extend(mem_k_norm(KZ, z)())))
            mem_turn(0, KZ, zz, (6, 7))
            scope.pop()
        k_bc = gain_row(3, edge.x)
        after = Edge(post_norm(k_bc), "norm_mix_2", 0)
        ffn("ffn1", edge, after)
        edge = after

        with ExitStack() as sc:
            scope.append(sc)
            fence = last()
            QMT = sb("QMT", [128, 4, 256])
            QTn, KTn = sb("QTn", [128, 8, 256]), sb("KTn", [128, 8, 256])
            QTp = sb("QTp", [64, 8, 256])
            KPT = sb("KPT", [64, 256])
            tb, tg = sb("tb", [128, 2, 2, 64]), sb("tg", [128, 2, 2, 2, 64])
            GR = sb("GR", [128, 2, 64])
            ZA, ZB, ZC, ZD = (sb(f"Z{i}", [128, 2, 512]) for i in range(4))
            RP, RQ = BC[:, 0:512].rearrange("p (h d) -> p h d", d=64), BC[:, 512:1024].rearrange("p (h d) -> p h d", d=64)
            gq = sb("gq", [128, 2])
            VV = MN = YG
            CTh, CTl = YAh, YAl
            k_tb = load("pool", tb[:, :, :, :], A["tab2"][:, 0:256].rearrange("p (c t d) -> p c t d", c=2, t=2), "c_tb", fence)
            k_gr = load("pool", GR[:, :, :], A["rows"][:, 4096:4224].rearrange("p (a d) -> p a d", a=2), "c_gr", fence)
            k_mem = mem_project(1, MN, fence)
            sc_mla = 192.0 ** -0.5
            sc_mem = 128.0 ** -0.5

            ta = nat_mm(PLAN["mla_a"], 4, 8, 448, (HTh, HTl), edge.h, (0, 1), edge=edge)
            h = [[edge.h[t][k] for t in range(2)] for k in range(8)]
            rs = edge.rs

            def z_evac(pr, dst, n, tk, *deps, held=False):
                out = []
                for t in range(2):
                    a = S(lambda e, t=t: e.activation(dst[:, t, 0:n], PS[:, pr[t], 0:n], ACT.Copy, scale=st[:, 2 + t:3 + t]), tk, rs, *deps)
                    bank[pr[t]] = [a]
                    out.append(a)
                if not held:
                    pump()
                return out

            def c_norm(Z, n, d, so, toks):
                r = head_rstd([Z[:, t, 0:d] for t in range(2)], 1, d, st[:, so:so + 2], toks)
                return [V(lambda e: e.tensor_scalar(Z[:, t, 0:d], Z[:, t, 0:d], st[:, so + t:so + t + 1], None, MUL), r) for t in range(2)]

            def group(cs, per, nkt, k0, off, pr, Z, deps, free, keep=False, held=False):
                tk = nat_mm(cs, per, nkt, 512, (CTh[:, k0:k0 + nkt, :], CTl[:, k0:k0 + nkt, :]), deps, pr, off=off, keep=keep)
                out = []
                for t in range(2):
                    a = S(lambda e, t=t: e.activation(Z[:, t, :], PS[:, pr[t], :], ACT.Copy), tk, free)
                    bank[pr[t]] = [a]
                    out.append(a)
                if not held:
                    pump()
                return out

            def norm_group(Z, nh, d, toks, so):
                return head_norm([Z[:, t, :] for t in range(2)], nh, d, so, toks)

            za = z_evac((0, 1), ZA, 448, ta, fence)
            zq = c_norm(ZA, 0, 384, 20, za)
            tb_ = nat_mm(PLAN["mla_b"], 8, 8, 256, (HTh, HTl), h, (2, 3))
            zb = z_evac((2, 3), ZB, 256, tb_, fence)
            zk = c_norm(ZB, 0, 256, 22, zb)
            tm = turn_rows(MN, k_mem, (4, 5, 6, 7))
            rm = row_norm(MN, k_mem, st[:, 16:18])
            k_tg = [rope_table(tg[:, i, :, :, :], tb, GR[:, i, :], 64, k_tb, k_gr, fence) for i in range(2)]
            k_q = V(lambda e: e.tensor_scalar(tg[:, 0, :, :, :], tg[:, 0, :, :, :], sc_mla, None, MUL), k_tg[0])
            g1 = V(lambda e: e.tensor_scalar(gq[:, 0:1], col("mla_qn"), sc_mla, None, MUL), fence)
            g2 = V(lambda e: e.tensor_scalar(gq[:, 1:2], col("memq_norm_2", 0), sc_mem, None, MUL))
            tc_ = nat_mm(PLAN["mla_c"], 4, 8, 512, (HTh, HTl), h, (0, 1))
            zc = z_evac((0, 1), ZC, 512, tc_, fence, held=True)
            hm = split_rows(tm, "mem_norm_2", 0, (4, 5, 6, 7), tc_)
            pump()

            gn = lambda k: col("mla_q_a_norm_2", k) if k < 3 else col("mla_kv_a_norm_2", k - 3)

            def c_turn(ks, b):
                for i, k in enumerate(ks):
                    for t in range(2):
                        src = ZA[:, t, 128 * k:128 * k + 128] if k < 3 else ZB[:, t, 128 * (k - 3):128 * (k - 3) + 128]
                        tk = transp(PS[:, b, 256 * i + 128 * t:256 * i + 128 * t + 128], src, (zq if k < 3 else zk)[t],
                                    bank[b] if t == 0 and i == 0 else None)
                return parts(ks, CTh, CTl, b, tk, gn, fence)

            ctt = c_turn((0, 1), 2) + c_turn((2, 3), 3)
            zm = norm_group(ZC, 4, 128, zc, 26)
            r_pe = head_rstd([ZA[:, t, 384:448] for t in range(2)], 1, 64, st[:, 24:26], za)
            zm = zm()
            kp = []
            for t in range(2):
                kp.append(rope(ZA[:, t, 384:448], 1, 64, t, tg[:, 1, :, :, :], RP, RQ, (st[:, 24 + t:25 + t], r_pe), za[t], k_tg, fence))
            tk = nat_mm(PLAN["mem10"], 4, 8, 512, (HTh, HTl), hm, (0, 1))
            ctt += c_turn((4,), 4)
            ckt = ctt[3:5]
            zmk = mem_k(1, st[:, 16:18], rm, tk, (0, 1), ZD, fence)
            pump()
            zmk = mem_k_norm(ZD, zmk)
            z2 = group(PLAN["qb2"], 3, 3, 0, 0, (2, 3), ZB, ctt[0:3], last("pe"))
            qp = []
            r = head_rstd([ZB[:, t, :] for t in range(2)], 8, 64, st[:, 42:58], z2)
            zmk = zmk()
            for t in range(2):
                so = st[:, 42 + 8 * t:50 + 8 * t]
                qp.append(rope(ZB[:, t, :], 8, 64, t, tg[:, 0, :, :, :], RP, RQ, (so, r), z2[t], k_q, kp))
            qmt = gain_turn(ZC, zm, lambda j: QMT[:, j:j + 2, :], gq[:, 1:2], (5, 6))
            qm_pe = last("pe")
            tk = nat_mm(PLAN["mem11"], 4, 8, 512, (HTh, HTl), hm, (0, 1))
            mem_v(1, st[:, 16:18], rm, tk, (0, 1))
            pump()
            for t in range(2):
                tk = transp(PS[0:64, 7, 128 * t:128 * t + 128], ZA[:, t, 384:448], kp[t], bank[7] if t == 0 else None)
            kpt = S(lambda e: e.activation(KPT[:, :], PS[0:64, 7, 0:256], ACT.Copy), tk, fence)
            bank[7] = [kpt]
            za_pe = tk
            mem_turn(1, ZD, zmk, (4, 5))
            zd_pe = last("pe")
            z0 = group(PLAN["qb0"], 3, 3, 0, 0, (2, 3), ZA, ctt[0:3], za_pe)
            c = PLAN["kvb0"][0]
            zk0 = group([c], 2, 2, 3, 0, (0, 1), ZC, ckt, qm_pe, keep=True)
            n0 = norm_group(ZA, 4, 128, z0, 34)
            nk0 = norm_group(ZC, 4, 128, zk0, 8)
            n0 = n0()
            nk0 = nk0()
            qpt = []
            for h2 in range(4):
                b = 4 + h2
                for j in range(2):
                    for t in range(2):
                        hh = 2 * h2 + j
                        tk = transp(PS[0:64, b, 256 * j + 128 * t:256 * j + 128 * t + 128], ZB[:, t, 64 * hh:64 * hh + 64], qp[t],
                                    bank[b] if j == 0 and t == 0 else None)
                a = S(lambda e, b=b, h2=h2: e.activation(QTp[:, 2 * h2:2 * h2 + 2, :], PS[0:64, b, :].rearrange("p (a c) -> p a c", a=2), ACT.Copy),
                      tk, fence)
                bank[b] = [a]
                qpt.append(a)
            qp_pe = tk
            vt = {}
            vt[0] = group([c], 2, 2, 3, 1024, (2, 3), VV[:, :, 0:512], ckt, [fence, tm, rm])
            qt = {0: gain_turn(ZA, n0, lambda j: QTn[:, j:j + 2, :], gq[:, 0:1], (4, 5))}
            za_pe = last("pe")
            kt = {0: gain_turn(ZC, nk0, lambda j: KTn[:, j:j + 2, :], col("mla_kn"), (6, 7))}
            qt[1], kt[1], vt[1], later = [], [], [], []
            ct_pe = []
            z1, zk1 = [], []
            n1, nk1 = [], []

            def fill(h):
                c = PLAN["kvb1"][0]
                if h == 0:
                    z1.extend(group(PLAN["qb1"], 3, 3, 0, 0, (6, 7), ZB, ctt[0:3], qp_pe, held=True))
                elif h == 1:
                    later.append(norm_group(ZB, 4, 128, z1, 34))
                    zk1.extend(group([c], 2, 2, 3, 0, (6, 7), ZD, ckt, zd_pe, keep=True, held=True))
                elif h == 2:
                    n1.extend(later.pop()())
                    later.append(norm_group(ZD, 4, 128, zk1, 8))
                    vt[1].extend(group([c], 2, 2, 3, 1024, (6, 7), VV[:, :, 512:1024], ckt, [fence, tm, rm], held=True))
                    ct_pe.extend(last("pe"))
                elif h == 3:
                    pump()
                    nk1.extend(later.pop()())
                    qt[1].extend(gain_turn(ZB, n1, lambda j: QTn[:, 4 + j:6 + j, :], gq[:, 0:1], (2, 3)))
                elif h == 5:
                    kt[1].extend(gain_turn(ZD, nk1, lambda j: KTn[:, 4 + j:6 + j, :], col("mla_kn"), (2, 3)))

            heads = []
            for hh in range(4):
                heads.append(([(QMT[:, hh, :], KM[:, 0, hh, :])], [VM[:, 0, kt_, 128 * hh:128 * hh + 128] for kt_ in range(2)],
                              128, [(4 + t, 128 * hh) for t in range(2)], [qmt, kmt[0], vmt[0]]))
            for hh in range(8):
                g = hh // 4
                heads.append(([(QTn[:, hh, :], KTn[:, hh, :]), (QTp[:, hh, :], KPT[:, :])],
                              [VV[:, kt_, 128 * hh:128 * hh + 128] for kt_ in range(2)], 128,
                              [(6 - 2 * g + t, 128 * (hh % 4)) for t in range(2)], [qt[g], qpt, kt[g], kpt, vt[g]]))
            quad = lambda a: a[:, :, :].rearrange("p a (b k) -> p a b k", b=2)
            ydeps = run_attention("A2", heads, [za_pe, last("pe"), qp], lambda h0: 8 if h0 == 0 else h0 - 4, 4, fill=fill, yfree=ct_pe,
                                  bufs=(quad(ZA), None, BC[:, :].rearrange("p (a k) -> p a k", a=2), quad(ZC)))
            scope.pop()
        edge = Edge(plain, "norm_ffn_2", 0)
        wide_mm(PLAN["out0"], lambda k: (YAh, YAl, k), lambda k: ydeps[k], edge)
        after = Edge(plain, "norm_mix_2", 8)
        ffn("ffn2", edge, after)
        edge = after

        with ExitStack() as sc:
            scope.append(sc)
            fence = last()
            tb, tg = sb("tbg", [128, 2, 2, 128]), sb("tgg", [128, 2, 2, 2, 128])
            GR = sb("GRg", [128, 2, 128])
            k_tb = load("pool", tb[:, :, :, :], A["tab2"][:, 256:768].rearrange("p (c t d) -> p c t d", c=2, t=2), "c_tb", fence)
            k_gr = load("pool", GR[:, :, :], A["rows"][:, 4224:4480].rearrange("p (a d) -> p a d", a=2), "c_gr", fence)
            Z = [sb(f"Zg{i}", [128, 2, 512]) for i in range(4)]
            QT, KT2, QMT = sb("QTg", [128, 8, 256]), sb("KTg", [128, 2, 256]), sb("QMg", [128, 4, 256])
            RP, RQ = (BC[:, 512 * i:512 * i + 512].rearrange("p (h d) -> p h d", d=128) for i in range(2))
            gq2 = sb("gqg", [128, 2])
            V(lambda e: e.tensor_scalar(gq2[:, 0:1], col("memq_norm_2", 1), sc_mem, None, MUL), fence)
            V(lambda e: e.memset(gq2[:, 1:2], sc_mem), fence)
            tk = nat_mm(PLAN["gqa3"], 4, 8, 512, (HTh, HTl), edge.h, (0, 1), edge=edge)
            h = [[edge.h[t][k] for t in range(2)] for k in range(8)]
            rs = edge.rs
            k_tg = [rope_table(tg[:, i, :, :, :], tb, GR[:, i, :], 128, k_tb, k_gr, fence) for i in range(2)]
            zt, n, post = {}, {}, {g: [] for g in range(4)}

            def evac(g, pr, tk):
                zt[g] = []
                for t in range(2):
                    a = S(lambda e: e.activation(Z[g][:, t, :], PS[:, pr[t], :], ACT.Copy, scale=st[:, 2 + t:3 + t]), tk, rs, fence)
                    bank[pr[t]] = [a]
                    zt[g].append(a)

            def norm(g):
                nh = 2 if g == 2 else 4
                so = (8, 34, 20, 26)[g]
                z = [Z[g][:, t, 0:128 * nh] for t in range(2)]
                if g == 3:
                    n[g] = head_norm(z, nh, 128, so, zt[g])()
                    return
                r = head_rstd(z, nh, 128, st[:, so:so + 2 * nh], zt[g])
                n[g] = []
                for t in range(2):
                    yield
                    n[g].append(rope(z[t], nh, 128, t, tg[:, int(g == 2), :, :, :], RP, RQ, (st[:, so + nh * t:so + nh * t + nh], r),
                                     zt[g][t], k_tg, fence))

            def turned(g, bks):
                dst = lambda j: (QMT[:, j:j + 2, :] if g == 3 else KT2[:, :, :] if g == 2 else QT[:, 4 * g + j:4 * g + j + 2, :])
                post[g].extend(gain_turn(Z[g], n[g], dst, gq2[:, 0:1] if g == 3 else 1.0 if g == 2 else gq2[:, 1:2], bks,
                                         2 if g == 2 else 4))

            for g, pr, prev, bks in ((3, (0, 1), None, None), (2, (2, 3), 3, (4, 5)), (0, (6, 7), 2, (2, 3))):
                if prev is not None:
                    tk = nat_mm(PLAN[f"gqa{g}"], 4, 8, 512, (HTh, HTl), h, pr)
                evac(g, pr, tk)
                pump()
                if prev is not None:
                    turned(prev, bks)
                for _ in norm(g):
                    pass

            norm1 = norm(1)

            def fill(h_):
                c = PLAN["gqa1"]
                if h_ == 0:
                    tk = nat_mm(c, 4, 8, 512, (HTh, HTl), h, (6, 7))
                    evac(1, (6, 7), tk)
                elif h_ == 1:
                    pump()
                if h_ == 3:
                    turned(0, (2, 3))
                if 1 <= h_ < 4:
                    next(norm1, None)
                if h_ == 4:
                    turned(1, (2, 3))

            heads = []
            for hh in range(4):
                heads.append(([(QMT[:, hh, :], KM[:, 1, hh, :])], [VM[:, 1, kt, 128 * hh:128 * hh + 128] for kt in range(2)],
                              128, [(4 + t, 128 * hh) for t in range(2)], [post[3], kmt[1], vmt[1]]))
            for hh in range(8):
                kv = hh // 4
                heads.append(([(QT[:, hh, :], KT2[:, kv, :])], [Z[2][:, kt, 256 + 128 * kv:384 + 128 * kv] for kt in range(2)],
                              128, [(6 - 2 * kv + t, 128 * (hh % 4)) for t in range(2)], [post[kv], post[2], zt[2]]))
            ydeps = run_attention("A3", heads, fence, lambda h0: 8 if h0 == 0 else h0 - 4, 4, fill=fill)
            edge = Edge(plain, "norm_ffn_2", 8)
            wide_mm(PLAN["out1"], lambda k: (YAh, YAl, k), lambda k: ydeps[k], edge)
            scope.pop()
        after = Edge(plain)
        ffn("ffn3", edge, after)
        xt = after.x
        outs = {f"c_o{t}{hf}": load(("sp", "act")[hf], A["out"][128 * t:128 * t + 128, 512 * hf:512 * hf + 512],
                                    X[:, t, 512 * hf:512 * hf + 512], f"c_o{t}{hf}", xt[t][hf])
                for t in range(2) for hf in range(2)}

        Q.count()
        block = top.enter_context(nc.Block())

        @block.sync
        def _(e):
            Q.emit("sp", e, sems)
            for name in outs:
                e.wait_ge(sems[name], outs[name].value)

        @block.gpsimd
        def _(e):
            Q.emit("pool", e, sems)

        @block.scalar
        def _(e):
            Q.emit("act", e, sems)

        @block.vector
        def _(e):
            Q.emit("dve", e, sems)

        @block.tensor
        def _(e):
            Q.emit("pe", e, sems)


def kernel(**inputs):
    import concourse.bacc as bacc
    from concourse.bass_utils import run_bass_kernel_spmd

    a = {k: np.asarray(v) for k, v in inputs.items()}
    PLAN, order = plan()
    tab, tab2 = tables()
    rows = np.concatenate([a["norm_mix_post"][0], a["norm_mix_post"][1], a["norm_ffn_post"][0], a["norm_ffn_post"][1],
                           a["mla_q_norm_2"][0, 128:], a["mla_k_norm_2"][0, 128:], a["gqa_q_norm_2"][0], a["gqa_k_norm_2"][0]])
    arrays = {
        "w": pack(a, order),
        "cols": columns(a),
        "rows": np.ascontiguousarray(np.broadcast_to(rows[None, :], (128, rows.shape[0]))),
        "s5": s5_layout(a),
        "tab": tab,
        "tab2": tab2,
        "x": np.ascontiguousarray(a["x"][0]),
        "mem": np.ascontiguousarray(a["mem_2"][0]),
        "pos": np.ascontiguousarray(a["positions"].reshape(2, 128).T),
    }
    nc = bacc.Bacc("TRN2", target_bir_lowering=False, num_devices=1)
    A = {n: nc.dram_tensor("in_" + n, v.shape, mybir.dt.from_np(v.dtype), kind="ExternalInput").ap() for n, v in arrays.items()}
    A["out"] = nc.dram_tensor("out_x", (256, 1024), mybir.dt.float32, kind="ExternalOutput").ap()
    program(nc, A, PLAN, len(order))
    r = run_bass_kernel_spmd(nc, [{"in_" + n: v for n, v in arrays.items()}], core_ids=[0])
    return np.asarray(r.results[0]["out_x"]).reshape(1, 256, 1024)
```
